# Optimizing a Trainium2 kernel written in Bass

```python
import jax, jax.numpy as jnp
from jax import lax
import numpy as np

D_MODEL = 1024
BATCH = 1
SEQ = 512
DEPTH = 1
DEC_BATCH = 1
DEC_SEQ = 512
PAST_LEN = 128

GRID_W = 64
HEAD_DIM = 64
N_Q_HEADS = 8
N_KV_HEADS = 2
Q_GROUP = N_Q_HEADS // N_KV_HEADS
ATTN_W = N_Q_HEADS * HEAD_DIM
KV_W = N_KV_HEADS * HEAD_DIM
LRU_W = D_MODEL - ATTN_W
LRU_BLOCKS = 8
LRU_BLOCK_DIM = LRU_W // LRU_BLOCKS
CONV_W = 4
LRU_C = 8.0
N_EXPERTS = 16
EXPERT_CAPACITY_FACTOR = 2
D_EXPERT = D_MODEL
Q_BLOCK = 128
ROPE_THETA = 10000.0
EPS = 1e-6
IN_W = ATTN_W + 2 * KV_W + 2 * LRU_W

kernel_name = "hybrid_gqa_rglru_ec_moe_encoder"

def _rmsnorm(x, g):
    x32 = x.astype(jnp.float32)
    y = x32 * lax.rsqrt(jnp.mean(x32 * x32, axis=-1, keepdims=True) + EPS)
    return (y * g.astype(jnp.float32)).astype(x.dtype)

def _axial_angles(seq_len):
    rows = seq_len // GRID_W
    row = jnp.repeat(jnp.arange(rows, dtype=jnp.float32), GRID_W)
    col = jnp.tile(jnp.arange(GRID_W, dtype=jnp.float32), rows)
    axis_dim = HEAD_DIM // 2
    inv_freq = ROPE_THETA ** (-jnp.arange(0, axis_dim, 2, dtype=jnp.float32) / axis_dim)
    return row[:, None] * inv_freq[None, :], col[:, None] * inv_freq[None, :]

def _rope_half(x, ang):
    f = ang.shape[-1]
    cos = jnp.cos(ang)[None, :, None, :]
    sin = jnp.sin(ang)[None, :, None, :]
    x1, x2 = x[..., :f], x[..., f:]
    return jnp.concatenate([x1 * cos - x2 * sin, x2 * cos + x1 * sin], axis=-1)

def _apply_axial_rope(x, row_ang, col_ang):
    half = HEAD_DIM // 2
    x32 = x.astype(jnp.float32)
    out = jnp.concatenate([_rope_half(x32[..., :half], row_ang),
                           _rope_half(x32[..., half:], col_ang)], axis=-1)
    return out.astype(x.dtype)

def _attention(q, k, v):
    B, S = q.shape[0], q.shape[1]
    nblk = S // Q_BLOCK
    qb = q.reshape(B, nblk, Q_BLOCK, N_KV_HEADS, Q_GROUP, HEAD_DIM)
    qb = jnp.moveaxis(qb, 1, 0)
    scale = HEAD_DIM ** -0.5

    def one_block(qblk):
        s = jnp.einsum('bqkgd,bskd->bkgqs', qblk, k).astype(jnp.float32) * scale
        p = jax.nn.softmax(s, axis=-1).astype(v.dtype)
        return jnp.einsum('bkgqs,bskd->bqkgd', p, v)

    o = lax.map(one_block, qb)
    return jnp.moveaxis(o, 0, 1).reshape(B, S, ATTN_W)

def _centred_dwconv(x, w, b):
    S = x.shape[1]
    left = CONV_W // 2
    right = CONV_W - 1 - left
    xp = jnp.pad(x, ((0, 0), (left, right), (0, 0)))
    out = b + xp[:, 0:S] * w[0]
    for tap in range(1, CONV_W):
        out = out + xp[:, tap:tap + S] * w[tap]
    return out

def _blockdiag(x, w, b):
    B, S = x.shape[0], x.shape[1]
    xb = x.reshape(B, S, LRU_BLOCKS, LRU_BLOCK_DIM)
    return jnp.einsum('bsnd,nde->bsne', xb, w).reshape(B, S, LRU_W) + b

def _lin_combine(c1, c2):
    a1, b1 = c1
    a2, b2 = c2
    return a1 * a2, a2 * b1 + b2

def _rglru_direction(xc, w_r, b_r, w_i, b_i, lam, reverse):
    r = jax.nn.sigmoid(_blockdiag(xc, w_r, b_r).astype(jnp.float32))
    i = jax.nn.sigmoid(_blockdiag(xc, w_i, b_i).astype(jnp.float32))
    log_a = -LRU_C * r * jax.nn.softplus(-lam.astype(jnp.float32))
    a = jnp.exp(log_a)
    mult = jnp.sqrt(-jnp.expm1(2.0 * log_a))
    bterm = mult * i * xc.astype(jnp.float32)
    _, h = lax.associative_scan(_lin_combine, (a, bterm), reverse=reverse, axis=1)
    return h

def _expert_choice_moe(h, router_w, w_gate, w_up, w_down):
    B, S, D = h.shape
    T = B * S
    cap = max(1, EXPERT_CAPACITY_FACTOR * T // N_EXPERTS)
    xt = h.reshape(T, D)
    affinity = jax.nn.softmax(jnp.einsum('td,de->te', xt, router_w).astype(jnp.float32), axis=-1)
    gate_vals, tok_idx = lax.top_k(affinity.T, cap)
    xs = jnp.take(xt, tok_idx, axis=0)
    hid = jax.nn.silu(jnp.einsum('ecd,edf->ecf', xs, w_gate)) * jnp.einsum('ecd,edf->ecf', xs, w_up)
    ys = jnp.einsum('ecf,efd->ecd', hid, w_down) * gate_vals[..., None].astype(h.dtype)
    out = jnp.zeros((T, D), h.dtype).at[tok_idx.reshape(-1)].add(ys.reshape(-1, D))
    return out.reshape(B, S, D)

def _encoder_layer(x, norm1_g, w_in, q_norm_g, k_norm_g, conv_w, conv_b,
                   lru_w_r, lru_b_r, lru_w_i, lru_b_i, lru_lambda, w_out,
                   norm2_g, router_w, exp_w_gate, exp_w_up, exp_w_down):
    B, S, _ = x.shape
    h = _rmsnorm(x, norm1_g)
    proj = jnp.einsum('bsd,de->bse', h, w_in)
    q, k, v, xr, gate = jnp.split(
        proj, [ATTN_W, ATTN_W + KV_W, ATTN_W + 2 * KV_W, ATTN_W + 2 * KV_W + LRU_W], axis=-1)
    q = _rmsnorm(q.reshape(B, S, N_Q_HEADS, HEAD_DIM), q_norm_g)
    k = _rmsnorm(k.reshape(B, S, N_KV_HEADS, HEAD_DIM), k_norm_g)
    v = v.reshape(B, S, N_KV_HEADS, HEAD_DIM)
    row_ang, col_ang = _axial_angles(S)
    q = _apply_axial_rope(q, row_ang, col_ang)
    k = _apply_axial_rope(k, row_ang, col_ang)
    attn_out = _attention(q, k, v)
    xc = _centred_dwconv(xr, conv_w, conv_b)
    h_lru = (_rglru_direction(xc, lru_w_r[0], lru_b_r[0], lru_w_i[0], lru_b_i[0], lru_lambda[0], False)
             + _rglru_direction(xc, lru_w_r[1], lru_b_r[1], lru_w_i[1], lru_b_i[1], lru_lambda[1], True))
    lru_out = (h_lru * jax.nn.gelu(gate.astype(jnp.float32), approximate=True)).astype(x.dtype)
    mixed = jnp.concatenate([attn_out, lru_out], axis=-1)
    x = x + jnp.einsum('bse,ed->bsd', mixed, w_out)
    h2 = _rmsnorm(x, norm2_g)
    return x + _expert_choice_moe(h2, router_w, exp_w_gate, exp_w_up, exp_w_down)

def _trunk(x, norm1_g, w_in, q_norm_g, k_norm_g, conv_w, conv_b,
           lru_w_r, lru_b_r, lru_w_i, lru_b_i, lru_lambda, w_out,
           norm2_g, router_w, exp_w_gate, exp_w_up, exp_w_down):
    for l in range(DEPTH):
        x = _encoder_layer(x, norm1_g[l], w_in[l], q_norm_g[l], k_norm_g[l], conv_w[l], conv_b[l],
                           lru_w_r[l], lru_b_r[l], lru_w_i[l], lru_b_i[l], lru_lambda[l], w_out[l],
                           norm2_g[l], router_w[l], exp_w_gate[l], exp_w_up[l], exp_w_down[l])
    return x

def setup_inputs(seed: int = 0) -> dict:
    key = jax.random.key(seed)
    ks = jax.random.split(key, 20)
    f32 = jnp.float32
    nrm = lambda k, shape, s: jax.random.normal(k, shape, f32) * s
    u = jax.random.uniform(ks[12], (DEPTH, 2, LRU_W), f32, minval=0.9, maxval=0.999)
    a_base = u ** (1.0 / LRU_C)
    lam = jnp.log(a_base) - jnp.log1p(-a_base)
    return {
        "x_prompt": nrm(ks[0], (BATCH, SEQ, D_MODEL), 1.0),
        "x_sample": nrm(ks[1], (DEC_BATCH, DEC_SEQ, D_MODEL), 1.0),
        "norm1_g": 1.0 + nrm(ks[2], (DEPTH, D_MODEL), 0.02),
        "w_in": nrm(ks[3], (DEPTH, D_MODEL, IN_W), D_MODEL ** -0.5),
        "q_norm_g": 1.0 + nrm(ks[4], (DEPTH, HEAD_DIM), 0.02),
        "k_norm_g": 1.0 + nrm(ks[5], (DEPTH, HEAD_DIM), 0.02),
        "conv_w": nrm(ks[6], (DEPTH, CONV_W, LRU_W), CONV_W ** -0.5),
        "conv_b": nrm(ks[7], (DEPTH, LRU_W), 0.02),
        "lru_w_r": nrm(ks[8], (DEPTH, 2, LRU_BLOCKS, LRU_BLOCK_DIM, LRU_BLOCK_DIM), LRU_BLOCK_DIM ** -0.5),
        "lru_b_r": nrm(ks[9], (DEPTH, 2, LRU_W), 0.02),
        "lru_w_i": nrm(ks[10], (DEPTH, 2, LRU_BLOCKS, LRU_BLOCK_DIM, LRU_BLOCK_DIM), LRU_BLOCK_DIM ** -0.5),
        "lru_b_i": nrm(ks[11], (DEPTH, 2, LRU_W), 0.02),
        "lru_lambda": lam,
        "w_out": nrm(ks[13], (DEPTH, D_MODEL, D_MODEL), D_MODEL ** -0.5),
        "norm2_g": 1.0 + nrm(ks[14], (DEPTH, D_MODEL), 0.02),
        "router_w": nrm(ks[15], (DEPTH, D_MODEL, N_EXPERTS), D_MODEL ** -0.5),
        "exp_w_gate": nrm(ks[16], (DEPTH, N_EXPERTS, D_MODEL, D_EXPERT), D_MODEL ** -0.5),
        "exp_w_up": nrm(ks[17], (DEPTH, N_EXPERTS, D_MODEL, D_EXPERT), D_MODEL ** -0.5),
        "exp_w_down": nrm(ks[18], (DEPTH, N_EXPERTS, D_EXPERT, D_MODEL), D_EXPERT ** -0.5),
    }

def reference(x_prompt, x_sample, norm1_g, w_in, q_norm_g, k_norm_g, conv_w, conv_b,
              lru_w_r, lru_b_r, lru_w_i, lru_b_i, lru_lambda, w_out,
              norm2_g, router_w, exp_w_gate, exp_w_up, exp_w_down):
    y_prompt = _trunk(x_prompt, norm1_g, w_in, q_norm_g, k_norm_g, conv_w, conv_b,
                      lru_w_r, lru_b_r, lru_w_i, lru_b_i, lru_lambda, w_out,
                      norm2_g, router_w, exp_w_gate, exp_w_up, exp_w_down)
    y_sample = _trunk(x_sample, norm1_g, w_in, q_norm_g, k_norm_g, conv_w, conv_b,
                      lru_w_r, lru_b_r, lru_w_i, lru_b_i, lru_lambda, w_out,
                      norm2_g, router_w, exp_w_gate, exp_w_up, exp_w_down)
    return (y_prompt, y_sample)


_drawn_inputs = setup_inputs


def setup_inputs(seed=0):
    import zlib

    import numpy as np

    out = dict(_drawn_inputs(seed))
    spreads = {}
    factors = {'norm1_g': 3.412,
     'q_norm_g': 8.0,
     'k_norm_g': 8.0,
     'lru_b_r': 8.0,
     'lru_b_i': 7.82,
     'norm2_g': 3.828}
    for name, (base, spread) in spreads.items():
        noise = np.random.default_rng([zlib.crc32(name.encode()), seed]).standard_normal(out[name].shape)
        drawn = base * np.exp(spread * noise) if base else spread * noise
        out[name] = __import__('jax').numpy.asarray(drawn.astype(out[name].dtype))
    for name, factor in factors.items():
        out[name] = (out[name] * factor).astype(out[name].dtype)
    return out
```

```python
from contextlib import ExitStack

import concourse.bass as bass
from concourse import mybir

F32 = mybir.dt.float32
F32R = mybir.dt.float32r
U32 = mybir.dt.uint32
ALU = mybir.AluOpType
ACT = mybir.ActivationFunctionType
AX_X = mybir.AxisListType.X

P = 128
SEQS = 2
GRID_W = 64
ROPE_THETA = 10000.0
EPS = 1e-6
LRU_C = 8.0
CONV_LEFT = 2


def layer_program(nc, x0, x1, norm1_g, w_in, q_norm_g, k_norm_g, conv_w, conv_b, lru_w_r, lru_b_r,
                  lru_w_i, lru_b_i, lru_lambda, w_out, norm2_g, router_w, w_gate, w_up, w_down,
                  rope_cos, rope_sin, y):
    S, D = x0.shape[1], x0.shape[2]
    T = SEQS * S
    NB = T // P
    BPS = S // P
    KC = D // P
    HD = q_norm_g.shape[1]
    LRU_W = lru_lambda.shape[2]
    CT = LRU_W // P
    ATTN_W = D - LRU_W
    HQ = ATTN_W // HD
    KV_W = (w_in.shape[2] - ATTN_W - 2 * LRU_W) // 2
    QKV = ATTN_W + 2 * KV_W
    TAPS = conv_w.shape[1]
    BD = lru_w_r.shape[3]
    KVH = KV_W // HD
    E = router_w.shape[2]
    CAP = 2 * S // E
    assert SEQS * CAP == P and HD * 2 == P
    h2_rows = nc.dram_tensor("h2_rows", (T, D), F32, kind="Internal").ap()

    GW = 256
    XR0, GATE0 = QKV, QKV + LRU_W
    GROUPS = [("xr", 0, XR0), ("gate", 0, GATE0), ("xr", 2, XR0 + GW), ("gate", 2, GATE0 + GW),
              ("qkv", 0, 0), ("qkv", GW, GW), ("qkv", 2 * GW, 2 * GW)]
    NG = len(GROUPS)
    JOBS = 4

    ctx = ExitStack()
    sem = lambda name: ctx.enter_context(nc.semaphore(name))

    base = -(-nc.sbuf_base // 64) * 64
    K = 1024

    def at(name, offset, shape, dt):
        return nc.alloc_sbuf_tensor_at(name, shape, dt, offset=base + offset)

    ident = at("ident", 0, [P, P], F32)
    small = at("small", 512, [P, 256], F32)
    vec_rows = at("vec_rows", 1536, [44, P], F32)
    vecs = at("vecs", 2048, [P, 44], F32)
    SM = 2560
    eps = small[:, 0:1]
    sumsq1 = small[:, 8:16]
    root1 = small[:, 16:24]
    rstd1 = small[:, 24:32]
    sp_neg, sp_abs, sp_exp, sp_den, sp_z, sp_z2, sp_p, sp_pos = (small[:, 32 + 8 * i:40 + 8 * i] for i in range(8))
    lru_c, neg_c, neg_2c = (small[:, 96 + 8 * i:104 + 8 * i] for i in range(3))
    V_CONVW, V_CONVB, V_BR, V_BI, V_LAM = 0, 16, 20, 28, 36

    lru_out = at("lru_out", SM, [P, CT, T], F32)
    qkv = at("qkv", SM + 16 * K, [P, NB, QKV], F32)
    R1 = SM + 40 * K
    hT_hi = at("hT_hi", R1, [P, KC, T], F32R)
    hT_lo = at("hT_lo", R1 + 32 * K, [P, KC, T], F32R)
    w_raw = at("w_raw", R1 + 64 * K, [P, KC, GW], F32)
    w_hi = at("w_hi", R1 + 72 * K, [P, 2, KC, GW], F32R)
    w_lo = at("w_lo", R1 + 88 * K, [P, 2, KC, GW], F32R)
    XP = S + TAPS - 1
    xr_pad = at("xr_pad", R1 + 104 * K, [P, CT, SEQS, XP], F32)
    R2 = R1 + 104 * K + 16480
    bd_raw = at("bd_raw", R2, [P, 4, P], F32)
    bd_hi = at("bd_hi", R2 + 2 * K, [P, 4, P], F32R)
    bd_lo = at("bd_lo", R2 + 4 * K, [P, 4, P], F32R)
    R3 = R2 + 6 * K
    xc = at("xc", R3, [P, T], F32)
    rt = [at(f"rt{d}", R3 + (4 + 16 * d) * K, [P, T], F32) for d in range(2)]
    ib = [at(f"ib{d}", R3 + (8 + 16 * d) * K, [P, T], F32) for d in range(2)]
    decay = [at(f"decay{d}", R3 + (12 + 16 * d) * K, [P, T], F32) for d in range(2)]
    mult = [at(f"mult{d}", R3 + (16 + 16 * d) * K, [P, T], F32) for d in range(2)]
    xc_hi = at("xc_hi", R3 + 12 * K, [P, T], F32R)
    xc_lo = at("xc_lo", R3 + 28 * K, [P, T], F32R)
    x_nat = at("x_nat", R3, [P, NB, D], F32)
    g1b = at("g1b", SM + 16 * K, [P, D], F32)
    x_norm = at("x_norm", SM + 20 * K, [P, 2, D], F32)
    junk = at("junk", SM + 28 * K, [P, D], F32)

    mixA_hi = at("mixA_hi", R1, [P, ATTN_W // P, T], F32R)
    mixA_lo = at("mixA_lo", R1 + 16 * K, [P, ATTN_W // P, T], F32R)
    qT = at("qT", R1 + 32 * K, [P, SEQS, HQ, S], F32R)
    kT = at("kT", R1 + 64 * K, [P, SEQS, KVH, 2, S], F32R)
    VW = (2 * KVH + 1) * HD
    v_hi = at("v_hi", R1 + 80 * K, [P, NB, VW], F32R)
    v_lo = at("v_lo", R1 + 90 * K, [P, NB, VW], F32R)
    prob = at("prob", R1 + 100 * K, [P, 2, BPS, S], F32)
    probT_hi = at("probT_hi", R1 + 116 * K, [P, BPS, S], F32R)
    probT_lo = at("probT_lo", R1 + 124 * K, [P, BPS, S], F32R)
    R4 = R1 + 132 * K
    QK = ATTN_W + KV_W
    NH = HQ + KVH
    turned = at("turned", R4, [P, QK], F32)
    swapped = at("swapped", R4 + 2560, [P, QK], F32)
    qk_norm = at("qk_norm", R4 + 5120, [P, QK], F32)
    q_pair = at("q_pair", R4 + 7680, [P, HQ, 2, HD], F32)
    k_pair = at("k_pair", R4 + 7680 + 4 * K, [P, KVH, 2, 2, HD], F32)
    cos_sin = at("cos_sin", R4 + 7680 + 6 * K, [P, 2, BPS, HD], F32)
    tab = at("tab", R4 + 7680 + 8 * K, [P, 4, BPS, HD], F32)
    gains = at("gains", R4 + 7680 + 12 * K, [P, 4, HD], F32)
    qk_sq = at("qk_sq", R4 + 7680 + 13 * K, [P, QK], F32)
    qk_stat = at("qk_stat", R4 + 7680 + 13 * K + 2560, [P, 4, NB * NH], F32)
    row_stat = at("row_stat", R4 + 7680 + 17 * K + 512, [P, 3, SEQS * HQ * BPS], F32)
    assert R4 + 7680 + 17 * K + 512 + 3 * 256 <= nc.sbuf_usable_end - base
    assert QK * 4 == 2560 and VW * NB * 4 == 10 * K

    g2b = at("g2b", SM + 8 * K, [P, D], F32)
    router = at("router", SM + 12 * K, [P, KC, E], F32)
    h2T = at("h2T", SM, [P, 2, KC, P], F32)
    x_again = at("x_again", SM + 16 * K, [P, 2, D], F32)
    x2 = at("x2", SM + 24 * K, [P, 2, D], F32)
    h2 = at("h2", SM + 32 * K, [P, 2, D], F32)
    mixL_hi = at("mixL_hi", R1 + 32 * K, [P, CT, T], F32R)
    mixL_lo = at("mixL_lo", R1 + 48 * K, [P, CT, T], F32R)
    wo_hi = at("wo_hi", R1 + 64 * K, [P, KC, D], F32R)
    wo_lo = at("wo_lo", R1 + 96 * K, [P, KC, D], F32R)
    wo_raw = at("wo_raw", R1 + 128 * K, [P, 2, D], F32)
    R5 = SM + 12 * K + 512
    aff_e = at("aff_e", R5, [P, NB, E], F32)
    aff_pad = at("aff_pad", R5 + 512, [P, BPS, 48], F32)
    aff_stat = at("aff_stat", R5 + 512 + 768, [P, 3, NB], F32)
    aff_work = at("aff_work", R1, [48, 2, S], F32)
    top_val = at("top_val", R1 + 4 * K, [48, CAP], F32)
    top_idx = at("top_idx", R1 + 4 * K + 256, [48, CAP], U32)
    stacked = at("stacked", R1 + 4 * K + 512, [E, 2, P], F32)
    idx_all = at("idx_all", SM - 256, [P, E], U32)
    gate_all = at("gate_all", SM - 128, [P, E], F32)

    RAW0 = nc.sbuf_usable_end - base - 32 * K
    RAW0 -= RAW0 % 64
    raw_gate = at("raw_gate", RAW0, [P, 4, 2, D], F32)
    raw_down = at("raw_down", R1 + 64 * K, [P, 4, 2, D], F32)
    raw_up = at("raw_up", R1 + 96 * K, [P, 4, 2, D], F32)
    e_hi = at("e_hi", R1 + 8 * K, [P, 4, D], F32R)
    e_lo = at("e_lo", R1 + 24 * K, [P, 4, D], F32R)
    xs = at("xs", R1 + 40 * K, [P, 2, D], F32)
    xsT_hi = at("xsT_hi", SM, [P, 2, KC, P], F32R)
    xsT_lo = at("xsT_lo", SM + 8 * K, [P, 2, KC, P], F32R)
    silu = at("silu", SM + 16 * K, [P, D], F32)
    hid = at("hid", SM + 20 * K, [P, D], F32)
    hidT_hi = at("hidT_hi", SM + 24 * K, [P, KC, P], F32R)
    hidT_lo = at("hidT_lo", SM + 28 * K, [P, KC, P], F32R)
    ys = at("ys", SM + 32 * K, [P, D], F32)
    idx_now = at("idx_now", SM + 36 * K, [P, 4], U32)
    assert RAW0 >= R1 + 128 * K

    assert R3 + 36 * K <= nc.sbuf_usable_end - base, (R3 + 36 * K, nc.sbuf_usable_end - base)

    bank = nc.alloc_psum_tensor("bank", [P, 8, 512], F32)

    x_loaded = [sem(f"x_loaded{b}") for b in range(NB)]
    g1_loaded, vec_loaded = sem("g1_loaded"), sem("vec_loaded")
    pool_ready, ident_zeroed = sem("pool_ready"), sem("ident_zeroed")
    sumsq_ready, root_ready, rstd_ready = sem("sumsq_ready"), sem("root_ready"), sem("rstd_ready")
    xn_ready, xt_done, ht_hi_done, ht_lo_done = sem("xn_ready"), sem("xt_done"), sem("ht_hi_done"), sem("ht_lo_done")
    wraw_loaded, whi_done, wlo_done = sem("wraw_loaded"), sem("whi_done"), sem("wlo_done")
    proj_done = sem("proj_done")
    xr_out, gate_out, qkv_out = sem("xr_out"), sem("gate_out"), sem("qkv_out")
    vec_t, vec_copied = sem("vec_t"), sem("vec_copied")
    dve_step, sp_exp_done, lru_c_done = sem("dve_step"), sem("sp_exp_done"), sem("lru_c_done")
    bd_loaded, bd_hi_done, bd_lo_done = sem("bd_loaded"), sem("bd_hi_done"), sem("bd_lo_done")
    xc_done, xc_hi_done, xc_lo_done = sem("xc_done"), sem("xc_hi_done"), sem("xc_lo_done")
    gates_done, sigm_done = sem("gates_done"), sem("sigm_done")
    exps_done, tanh_done, mult2_done, root_done, scan_done = (
        sem("exps_done"), sem("tanh_done"), sem("mult2_done"), sem("root_done"), sem("scan_done"))
    act_step = sem("act_step")
    tabs_loaded, tabs_done, v_zeroed = sem("tabs_loaded"), sem("tabs_done"), sem("v_zeroed")
    qk_sq_done, qk_sum_done, qk_root_done, qk_rstd_done = (
        sem("qk_sq_done"), sem("qk_sum_done"), sem("qk_root_done"), sem("qk_rstd_done"))
    turned_done, swapped_done, qk_norm_done = sem("turned_done"), sem("swapped_done"), sem("qk_norm_done")
    qk_hi_done, qk_lo_done, v_hi_done, v_lo_done = sem("qk_hi_done"), sem("qk_lo_done"), sem("v_hi_done"), sem("v_lo_done")
    qkT_done, qkT_out = sem("qkT_done"), sem("qkT_out")
    scores_done, max_done, exp_done, recip_done, prob_done = (
        sem("scores_done"), sem("max_done"), sem("exp_done"), sem("recip_done"), sem("prob_done"))
    probT_done, probT_hi_done, probT_lo_done = sem("probT_done"), sem("probT_hi_done"), sem("probT_lo_done")
    pv_done, mixA_hi_done, mixA_lo_done = sem("pv_done"), sem("mixA_hi_done"), sem("mixA_lo_done")
    consts3_loaded, mixL_hi_done, mixL_lo_done = sem("consts3_loaded"), sem("mixL_hi_done"), sem("mixL_lo_done")
    wo_loaded = [sem(f"wo_loaded{i}") for i in range(2)]
    wo_hi_done, wo_lo_done = sem("wo_hi_done"), sem("wo_lo_done")
    xa_loaded = [sem(f"xa_loaded{i}") for i in range(2)]
    outproj_done, x2_done, sumsq2_done, root2_done, h2_done = (
        sem("outproj_done"), sem("x2_done"), sem("sumsq2_done"), sem("root2_done"), sem("h2_done"))
    x2_stored = [sem(f"x2_stored{i}") for i in range(2)]
    h2_stored = [sem(f"h2_stored{i}") for i in range(2)]
    h2T_done, h2T_out, logits_done = sem("h2T_done"), sem("h2T_out"), sem("logits_done")
    aff_shifted, aff_exp_done, aff_done, affT_done = sem("aff_shifted"), sem("aff_exp_done"), sem("aff_done"), sem("affT_done")
    stacked_done, stackedT_done, routed = sem("stacked_done"), sem("stackedT_done"), sem("routed")
    pad_zeroed = sem("pad_zeroed")
    gate_loaded = [sem(f"gate_loaded{i}") for i in range(4)]
    down_loaded = [sem(f"down_loaded{i}") for i in range(4)]
    up_loaded = [sem(f"up_loaded{i}") for i in range(4)]
    row_hi, row_lo, row_used = sem("row_hi"), sem("row_lo"), sem("row_used")
    idx_copied, xs_loaded, xsT_done, xsT_hi_done, xsT_lo_done = (
        sem("idx_copied"), [sem(f"xs_loaded{i}") for i in range(2)], sem("xsT_done"), sem("xsT_hi_done"), sem("xsT_lo_done"))
    silu_done, hid_done, hidT_done, hidT_hi_done, hidT_lo_done = (
        sem("silu_done"), sem("hid_done"), sem("hidT_done"), sem("hidT_hi_done"), sem("hidT_lo_done"))
    ys_done, scattered, ys_free = sem("ys_done"), sem("scattered"), sem("ys_free")
    gather_ready, scatter_ready = sem("gather_ready"), sem("scatter_ready")

    SEMS_OF = {"xr": xr_out, "gate": gate_out, "qkv": qkv_out}

    def evacuated(g, j):
        kind = GROUPS[g][0]
        before = sum(GROUPS[i][0] == kind for i in range(g))
        return SEMS_OF[kind], JOBS * before + j + 1

    steps = []
    for b in range(NB):
        steps.append(("normalise", b))
        if b == 3:
            steps.append(("split_w", 0))
    steps.append(("vectors",))
    LRU_AT = {2: ("conv", 0), 4: ("gates", 0, 0), 5: ("gates", 0, 1), 6: ("decay", 0), 7: ("scan", 0),
              9: ("conv", 1), 10: ("gates", 1, 0), 11: ("gates", 1, 1), 12: ("decay", 1), 13: ("scan", 1),
              14: ("conv", 2), 15: ("gates", 2, 0), 16: ("gates", 2, 1), 17: ("decay", 2), 18: ("scan", 2),
              19: ("conv", 3), 20: ("gates", 3, 0), 21: ("gates", 3, 1), 22: ("decay", 3), 23: ("scan", 3)}
    for n in range(NG * JOBS):
        g, j = divmod(n, JOBS)
        steps.append(("project", g, j))
        if n:
            steps.append(("empty", (n - 1) // JOBS, (n - 1) % JOBS))
        if j == 0 and g + 1 < NG:
            steps.append(("split_w", g + 1))
        if n in LRU_AT:
            steps.append(LRU_AT[n])
    steps.append(("empty", NG - 1, JOBS - 1))

    HEADS = SEQS * HQ
    USES = 3
    attn = [("stats", 0)]
    for b in range(BPS):
        attn += [("prepare", b), ("turn", b)]
    for n in range(HEADS + 3):
        attn.append(("head", n))
        if n == 0:
            attn.append(("stats", 1))
        if 2 <= n <= BPS + 1:
            attn.append(("turn", BPS + n - 2))
        if 1 <= n <= BPS:
            attn.append(("prepare", BPS + n - 1))

    def prep_bank(n):
        return 4 + n % 4 if n < USES * BPS else 7

    def prep_free(n):
        return n - 3 if n < USES * BPS else n

    def pair_cols(head):
        kv = head % HQ // (HQ // KVH)
        first = 2 * HD * kv + (HD if head % 2 == 0 else 0)
        return slice(first, first + 2 * HD)

    block = ctx.enter_context(nc.Block())

    @block.sync
    def _(sp):
        for b in range(NB):
            src = (x0 if b < BPS else x1)[0, (b % BPS) * P:(b % BPS + 1) * P, :]
            sp.dma_start(x_nat[:, b, :], src).then_inc(x_loaded[b], 16)
            if b == 1:
                sp.dma_start(g1b[:, :], norm1_g[0:1, :].to_broadcast([P, D])).then_inc(g1_loaded, 16)
        for g, (_, _, col) in enumerate(GROUPS):
            if g:
                sp.wait_ge(wlo_done, g)
            sp.dma_start(w_raw[:, :, :], w_in[0, :, col:col + GW].rearrange("(k p) n -> p k n", p=P)).then_inc(wraw_loaded, 16)

        sp.wait_ge(scan_done, CT)
        sp.dma_start(cos_sin[:, 0, :, :], rope_cos.rearrange("(b p) d -> p b d", p=P)).then_inc(tabs_loaded, 16)
        sp.dma_start(cos_sin[:, 1, :, :], rope_sin.rearrange("(b p) d -> p b d", p=P)).then_inc(tabs_loaded, 16)
        for i, g in enumerate((q_norm_g, k_norm_g)):
            sp.dma_start(gains[:, 2 * i, :], g[0:1, :].to_broadcast([P, HD])).then_inc(tabs_loaded, 16)

        sp.wait_ge(pv_done, BPS * HEADS)
        for k in range(KC):
            if k == 2:
                sp.dma_start(x_again[:, 0, :], x0[0, 0:P, :]).then_inc(xa_loaded[0], 16)
                sp.dma_start(x_again[:, 1, :], x0[0, P:2 * P, :]).then_inc(xa_loaded[1], 16)
                sp.wait_ge(mixL_lo_done, 1)
                sp.dma_start(g2b[:, :], norm2_g[0:1, :].to_broadcast([P, D])).then_inc(consts3_loaded, 16)
                sp.dma_start(router[:, :, :], router_w[0].rearrange("(k p) e -> p k e", p=P)).then_inc(consts3_loaded, 16)
            if k >= 2:
                sp.wait_ge(wo_lo_done, k - 1)
            sp.dma_start(wo_raw[:, k % 2, :], w_out[0, k * P:(k + 1) * P, :]).then_inc(wo_loaded[k % 2], 16)
        def load(raw, i, w, e, loaded):
            sp.dma_start(raw[:, i, :, :], w[0, e, 2 * i * P:2 * (i + 1) * P, :].rearrange("(r p) n -> p r n", p=P)
                         if isinstance(e, int) else
                         w[0, bass.ds(e, 1), 2 * i * P:2 * (i + 1) * P, :].rearrange("o (r p) n -> p (o r) n", p=P)).then_inc(loaded[i], 16)

        for b in range(NB):
            if b + 2 < NB:
                sp.wait_ge(x2_done, b + 1)
                nb = b + 2
                sp.dma_start(x_again[:, b % 2, :], (x0 if nb < BPS else x1)[0, (nb % BPS) * P:(nb % BPS + 1) * P, :]).then_inc(xa_loaded[b % 2], 16)
            sp.wait_ge(x2_done, b + 1)
            sp.dma_start(y[b * P:(b + 1) * P, :], x2[:, b % 2, :]).then_inc(x2_stored[b % 2], 16)
            sp.wait_ge(h2_done, b + 1)
            sp.dma_start(h2_rows[b * P:(b + 1) * P, :], h2[:, b % 2, :]).then_inc(h2_stored[b % 2], 16)
            if b == 1:
                for i in range(4):
                    load(raw_gate, i, w_gate, 0, gate_loaded)

        sp.wait_ge(outproj_done, NB)
        for i in range(4):
            load(raw_up, i, w_up, 0, up_loaded)
        def step_loads(e):
            for i in range(4):
                sp.wait_ge(row_lo, e * 24 + (2 * i + 2))
                load(raw_gate, i, w_gate, e + 1, gate_loaded)
            for i in range(4):
                sp.wait_ge(row_lo, e * 24 + (8 + 2 * i + 2))
                load(raw_down, i, w_down, e, down_loaded)
            for i in range(4):
                sp.wait_ge(row_lo, e * 24 + (16 + 2 * i + 2))
                load(raw_up, i, w_up, e + 1, up_loaded)
        with sp.Fori(0, E - 1) as e:
            step_loads(e)
        for i in range(4):
            sp.wait_ge(row_lo, (E - 1) * 24 + 8 + 2 * i + 2)
            load(raw_down, i, w_down, E - 1, down_loaded)

    @block.gpsimd
    def _(pool):
        pool.memset(ident[:, :], 0.0).then_inc(ident_zeroed, 1)
        pool.memset(eps, EPS).then_inc(pool_ready, 1)
        pool.memset(bd_raw[:, :, :], 0.0).then_inc(pool_ready, 1)
        pool.memset(xr_pad[:, :, :, 0:CONV_LEFT], 0.0).then_inc(pool_ready, 1)
        pool.memset(xr_pad[:, :, :, CONV_LEFT + S:XP], 0.0).then_inc(pool_ready, 1)
        pool.wait_ge(ident_zeroed, 1)
        pool.affine_select(out=ident[:, :], in_=ident[:, :], compare_op=ALU.not_equal, fill=1.0, base=0,
                           pattern=[[-1, P]], channel_multiplier=1).then_inc(pool_ready, 1)

        pool.wait_ge(proj_done, NG * JOBS)
        pool.wait_ge(scan_done, CT)
        pool.memset(v_hi[:, :, :].bitcast(F32), 0.0).then_inc(v_zeroed, 1)
        pool.memset(v_lo[:, :, :].bitcast(F32), 0.0).then_inc(v_zeroed, 1)
        pool.wait_ge(tabs_loaded, 4 * 16)
        quarter = HD // 4
        for i in range(2):
            for a in range(4):
                o = a ^ 1
                pool.tensor_copy(gains[:, 2 * i + 1, a * quarter:(a + 1) * quarter],
                                 gains[:, 2 * i, o * quarter:(o + 1) * quarter]).then_inc(tabs_done, 1)
        pool.wait_ge(tabs_done, 8)
        for i in range(2):
            for j in range(2):
                pool.tensor_tensor(tab[:, 2 * i + j, :, :], cos_sin[:, j, :, :],
                                   gains[:, 2 * i + j:2 * i + j + 1, :].to_broadcast([P, BPS, HD]), ALU.mult).then_inc(tabs_done, 1)
        pool.wait_ge(tabs_done, 12)
        pool.tensor_scalar(tab[:, 0:2, :, :], tab[:, 0:2, :, :], HD ** -0.5, 1.0, ALU.mult, ALU.mult).then_inc(tabs_done, 1)
        pool.wait_ge(tabs_done, 13)
        for step in attn:
            kind, n = step
            if kind == "prepare":
                b = n
                pool.wait_ge(qkv_out, 3 * JOBS)
                if b:
                    pool.wait_ge(qk_norm_done, b)
                for i, (c0, h) in enumerate(((0, HQ), (ATTN_W, KVH))):
                    pool.tensor_tensor(turned[:, c0:c0 + h * HD].rearrange("p (h d) -> p h d", h=h),
                                       qkv[:, b, c0:c0 + h * HD].rearrange("p (h d) -> p h d", h=h),
                                       tab[:, 2 * i, b % BPS:b % BPS + 1, :].to_broadcast([P, h, HD]), ALU.mult).then_inc(turned_done, 1)
            elif kind == "head" and n < HEADS:
                for qb in range(BPS):
                    u = BPS * n + qb
                    pool.wait_ge(recip_done, u + 1)
                    pool.tensor_scalar(prob[:, n % 2, qb, :], prob[:, n % 2, qb, :], row_stat[:, 2, u:u + 1], 1.0, ALU.mult, ALU.mult).then_inc(prob_done, 1)

        pool.wait_ge(mixL_lo_done, 1)
        pool.memset(aff_pad[:, :, :], 0.0).then_inc(pad_zeroed, 1)

        pool.wait_ge(routed, 2)
        for i in range(2):
            pool.wait_ge(h2_stored[i], 16 * (NB // 2))
            pool.wait_ge(x2_stored[i], 16 * (NB // 2))
        for e in range(2):
            pool.tensor_copy(idx_now[:, e:e + 1], idx_all[:, e:e + 1]).then_inc(idx_copied, 1)
            pool.wait_ge(idx_copied, e + 1)
            pool.indirect_dma_start(xs[:, e, :], None, h2_rows, bass.IndirectOffsetOnAxis(ap=idx_now[:, e:e + 1], axis=0)).then_inc(xs_loaded[e], 16)

        def scatter_step(e, copied):
            pool.tensor_copy(idx_now[:, 2:3], idx_all[:, bass.ds(e, 1)] if not isinstance(e, int) else idx_all[:, e:e + 1]).then_inc(idx_copied, 1)
            pool.wait_ge(idx_copied, copied)
            pool.wait_ge(ys_done, e + 1)
            pool.sem_inc(scatter_ready, 1)
            pool.indirect_dma_start(y, bass.IndirectOffsetOnAxis(ap=idx_now[:, 2:3], axis=0), ys[:, :], None, compute_op=ALU.add).then_inc(scattered, 16)
            pool.wait_ge(scattered, e * 16 + 16)
            pool.sem_inc(ys_free, 1)

        pool.sem_inc(ys_free, 1)
        with pool.Fori(0, (E - 2) // 2) as pair:
            e = pair * 2
            for parity in range(2):
                pool.wait_ge(xsT_done, e * 2 + (2 * parity + 2))
                pool.tensor_copy(idx_now[:, parity:parity + 1], idx_all[:, bass.ds(e + (parity + 2), 1)]).then_inc(idx_copied, 1)
                pool.wait_ge(idx_copied, e * 2 + (3 + 2 * parity))
                pool.sem_inc(gather_ready, 1)
                pool.indirect_dma_start(xs[:, parity, :], None, h2_rows,
                                        bass.IndirectOffsetOnAxis(ap=idx_now[:, parity:parity + 1], axis=0)).then_inc(xs_loaded[parity], 16)
                scatter_step(e + parity, e * 2 + (4 + 2 * parity))
        for e in (E - 2, E - 1):
            scatter_step(e, 2 * e + 3 - (e - (E - 2)))

    @block.scalar
    def _(act):
        own = [0]

        def link(ins):
            own[0] += 1
            ins.then_inc(act_step, 1)
            act.wait_ge(act_step, own[0])

        def load_bd(ct):
            for d in range(2):
                for m, w in enumerate((lru_w_r, lru_w_i)):
                    for n in range(P // BD):
                        act.dma_start(bd_raw[n * BD:(n + 1) * BD, 2 * d + m, n * BD:(n + 1) * BD],
                                      w[0, d, ct * (P // BD) + n, :, :]).then_inc(bd_loaded, 16)

        rows = [(0, conv_w[0].rearrange("t (c p) -> (t c) p", p=P)), (16, conv_b[0].rearrange("(c p) -> c p", p=P)),
                (20, lru_b_r[0].rearrange("d (c p) -> (d c) p", p=P)), (28, lru_b_i[0].rearrange("d (c p) -> (d c) p", p=P)),
                (36, lru_lambda[0].rearrange("d (c p) -> (d c) p", p=P))]
        for at_row, src in rows:
            act.dma_start(vec_rows[at_row:at_row + src.shape[0], :], src).then_inc(vec_loaded, 16)
        act.wait_ge(pool_ready, 5)
        load_bd(0)
        for b in range(NB):
            act.wait_ge(x_loaded[b], 16)
            if b:
                act.wait_ge(sumsq_ready, b)
            act.activation(junk[:, :], x_nat[:, b, :], ACT.Square, accum_out=sumsq1[:, b:b + 1]).then_inc(sumsq_ready, 1)
            if b % BPS == BPS - 1:
                act.wait_ge(sumsq_ready, b + 1)
                act.activation(root1[:, b + 1 - BPS:b + 1], sumsq1[:, b + 1 - BPS:b + 1], ACT.Sqrt,
                               scale=1.0 / D, bias=eps).then_inc(root_ready, 1)
        for step in steps:
            kind, arg = step[0], step[1:]
            if kind == "normalise":
                b, = arg
                for h in range(2):
                    act.wait_ge(xt_done, 2 * b + h + 1)
                    act.activation(hT_hi[:, 4 * h:4 * h + 4, b * P:(b + 1) * P],
                                   bank[:, 4 + 2 * (b % 2) + h, :].rearrange("p (k t) -> p k t", k=4), ACT.Copy).then_inc(ht_hi_done, 1)
            elif kind == "split_w":
                g, = arg
                act.wait_ge(wraw_loaded, 16 * (g + 1))
                if g >= 2:
                    act.wait_ge(proj_done, JOBS * (g - 1))
                act.activation(w_hi[:, g % 2, :, :], w_raw[:, :, :], ACT.Copy).then_inc(whi_done, 1)
            elif kind == "vectors":
                act.wait_ge(dve_step, 2)
                act.activation(sp_exp, sp_abs, ACT.Exp, scale=-1.0).then_inc(sp_exp_done, 1)
            elif kind == "empty":
                g, j = arg
                what, c0, _ = GROUPS[g]
                if what == "gate":
                    act.wait_ge(proj_done, JOBS * g + j + 1)
                    act.activation(lru_out[:, c0 + j // 2, (j % 2) * S:(j % 2 + 1) * S], bank[:, j, :],
                                   ACT.Gelu_apprx_tanh).then_inc(gate_out, 1)
                elif what == "qkv":
                    act.wait_ge(proj_done, JOBS * g + j + 1)
                    act.activation(qkv[:, 2 * j:2 * j + 2, c0:c0 + GW],
                                   bank[:, j, :].rearrange("p (b n) -> p b n", b=2), ACT.Copy).then_inc(qkv_out, 1)
            elif kind == "conv":
                ct, = arg
                act.wait_ge(bd_loaded, 8 * 16 * (ct + 1))
                if ct:
                    act.wait_ge(gates_done, 2 * ct)
                act.activation(bd_hi[:, :, :], bd_raw[:, :, :], ACT.Copy).then_inc(bd_hi_done, 1)
                act.wait_ge(xc_done, ct + 1)
                if ct:
                    act.wait_ge(scan_done, ct)
                act.activation(xc_hi[:, :], xc[:, :], ACT.Copy).then_inc(xc_hi_done, 1)
                if ct + 1 < CT:
                    act.wait_ge(bd_lo_done, ct + 1)
                    load_bd(ct + 1)
            elif kind == "gates":
                ct, d = arg
                act.wait_ge(gates_done, 2 * ct + d + 1)
                if ct:
                    act.wait_ge(scan_done, ct)
                act.activation(rt[d][:, :], bank[:, 4:6, :].rearrange("p a b -> p (a b)"), ACT.Sigmoid,
                               bias=vecs[:, V_BR + CT * d + ct:V_BR + CT * d + ct + 1]).then_inc(sigm_done, 1)
                act.activation(ib[d][:, :], bank[:, 6:8, :].rearrange("p a b -> p (a b)"), ACT.Sigmoid,
                               bias=vecs[:, V_BI + CT * d + ct:V_BI + CT * d + ct + 1]).then_inc(sigm_done, 1)
            elif kind == "decay":
                ct, = arg
                act.wait_ge(sigm_done, 4 * ct + 4)
                act.wait_ge(gates_done, 2 * ct + 2)
                act.wait_ge(lru_c_done, 1)
                for d in range(2):
                    c = CT * d + ct
                    act.activation(decay[d][:, :], rt[d][:, :], ACT.Exp, scale=neg_c[:, c:c + 1])
                    act.activation(mult[d][:, :], rt[d][:, :], ACT.Exp, scale=neg_2c[:, c:c + 1]).then_inc(exps_done, 1)
                    act.wait_ge(exps_done, 2 * ct + d + 1)
                    act.activation(rt[d][:, :], rt[d][:, :], ACT.Tanh, scale=lru_c[:, c:c + 1]).then_inc(tanh_done, 1)
            elif kind == "scan":
                ct, = arg
                for d in range(2):
                    act.wait_ge(mult2_done, 2 * ct + d + 1)
                    act.activation(mult[d][:, :], mult[d][:, :], ACT.Sqrt).then_inc(root_done, 1)

        act.wait_ge(scan_done, CT)
        for kind, n in attn:
            if kind == "stats":
                act.wait_ge(qkv_out, 3 * JOBS)
                for b in range(n * BPS, (n + 1) * BPS):
                    if b % 2 == 0 and b >= 2:
                        act.wait_ge(qk_sum_done, b - 1)
                    if b % 2 and b >= 2:
                        act.wait_ge(qk_sum_done, b - 1)
                    act.wait_ge(qk_norm_done, n * BPS) if n else None
                    act.activation((qk_sq, swapped)[b % 2][:, :], qkv[:, b, 0:QK], ACT.Square).then_inc(qk_sq_done, 1)
                cols = slice(n * BPS * NH, (n + 1) * BPS * NH)
                act.wait_ge(qk_sum_done, (n + 1) * BPS)
                act.activation(qk_stat[:, 2, cols], qk_stat[:, 0, cols], ACT.Sqrt, scale=1.0 / HD, bias=eps).then_inc(qk_root_done, 1)
            elif kind == "prepare":
                b = n
                vs = v_hi[:, b, HD:HD + 2 * HD * KVH].rearrange("p (g w) -> p g w", g=KVH)[:, :, 0:HD]
                act.wait_ge(v_zeroed, 2)
                act.activation(vs, qkv[:, b, QK:QKV].rearrange("p (g w) -> p g w", g=KVH), ACT.Copy).then_inc(v_hi_done, 1)
                act.wait_ge(qk_norm_done, b + 1)
                if b:
                    act.wait_ge(qkT_done, USES * b)
                act.activation(q_pair[:, :, 0, :].bitcast(F32R), qk_norm[:, 0:ATTN_W].rearrange("p (h d) -> p h d", h=HQ), ACT.Copy)
                for copy in range(2):
                    ins = act.activation(k_pair[:, :, 0, copy, :].bitcast(F32R),
                                         qk_norm[:, ATTN_W:QK].rearrange("p (h d) -> p h d", h=KVH), ACT.Copy)
                ins.then_inc(qk_hi_done, 1)
            elif kind == "turn":
                b = n
                s, tok = b // BPS, slice((b % BPS) * P, (b % BPS + 1) * P)
                for i in range(USES):
                    u = USES * b + i
                    act.wait_ge(qkT_done, u + 1)
                    if i < 2:
                        out = qT[:, s, 4 * i:4 * i + 4, tok]
                    else:
                        out = kT[:, s, :, :, tok].rearrange("p g v t -> p (g v) t")
                    act.activation(out, bank[:, prep_bank(u), :].rearrange("p (h t) -> p h t", h=4), ACT.Copy).then_inc(qkT_out, 1)
            elif kind == "head":
                m = n - 3
                if m >= 0 and m % 2:
                    act.wait_ge(pv_done, BPS * (m + 1))
                    act.activation(mixA_hi[:, m % HQ // 2, m // HQ * S:(m // HQ + 1) * S], bank[:, 6, :], ACT.Copy).then_inc(mixA_hi_done, 1)
                for i in range(BPS):
                    m = n - 2
                    if 0 <= m < HEADS:
                        act.wait_ge(probT_done, BPS * (m + 1))
                        if m:
                            act.wait_ge(pv_done, BPS * (m - 1) + i + 1)
                        act.activation(probT_hi[:, i, :], bank[:, 2 + i, :], ACT.Copy).then_inc(probT_hi_done, 1)
                    if n < HEADS:
                        u = BPS * n + i
                        act.wait_ge(max_done, u + 1)
                        if n >= 2:
                            act.wait_ge(probT_done, u - 2 * BPS + 1)
                        act.activation(prob[:, n % 2, i, :], bank[:, u % 2, :], ACT.Exp, bias=row_stat[:, 0, u:u + 1],
                                       accum_out=row_stat[:, 1, u:u + 1]).then_inc(exp_done, 1)

        act.wait_ge(scores_done, BPS * HEADS)
        act.activation(mixL_hi[:, :, :], lru_out[:, :, :], ACT.Copy).then_inc(mixL_hi_done, 1)
        for k in range(KC):
            act.wait_ge(wo_loaded[k % 2], 16 * (k // 2 + 1))
            if k == 0:
                act.wait_ge(pv_done, BPS * HEADS)
            act.activation(wo_hi[:, k, :], wo_raw[:, k % 2, :], ACT.Copy).then_inc(wo_hi_done, 1)
        for b in range(NB + 1):
            if b < NB:
                act.wait_ge(x2_done, b + 1)
                if b:
                    act.wait_ge(h2_done, b)
                if b >= 2:
                    act.wait_ge(h2_stored[b % 2], 16 * (b // 2))
                    act.wait_ge(h2T_done, 2 * (b - 1))
                act.activation(h2[:, b % 2, :], x2[:, b % 2, :], ACT.Square, accum_out=sumsq1[:, b:b + 1]).then_inc(sumsq2_done, 1)
                act.wait_ge(sumsq2_done, b + 1)
                act.activation(root1[:, b:b + 1], sumsq1[:, b:b + 1], ACT.Sqrt, scale=1.0 / D, bias=eps).then_inc(root2_done, 1)
            if b:
                c = b - 1
                for h in range(2):
                    act.wait_ge(h2T_done, 2 * c + h + 1)
                    if c >= 2:
                        act.wait_ge(logits_done, c - 1)
                    act.activation(h2T[:, c % 2, 4 * h:4 * h + 4, :], bank[:, 4 + h, :].rearrange("p (k t) -> p k t", k=4),
                                   ACT.Copy).then_inc(h2T_out, 1)
        act.wait_ge(aff_shifted, 1)
        act.activation(aff_e[:, :, :], aff_e[:, :, :], ACT.Exp).then_inc(aff_exp_done, 1)

        def hi_row(n, raw, loaded, value, j, inc=1):
            act.wait_ge(loaded[j // 2], value)
            if not (isinstance(n, int) and n < 4):
                act.wait_ge(row_used, n - 3)
            act.activation(e_hi[:, j % 4, :], raw[:, j // 2, j % 2, :], ACT.Copy).then_inc(row_hi, inc)

        def turn_hi(out, done, count, out_done):
            for h in range(2):
                act.wait_ge(done, count + (h + 1))
                act.activation(out[:, 4 * h:4 * h + 4, :], bank[:, 6 + h, :].rearrange("p (k t) -> p k t", k=4), ACT.Copy).then_inc(out_done, 1)

        def silu_of(e):
            act.activation(silu[:, :], bank[:, 0:2, :].rearrange("p a b -> p (a b)"), ACT.Silu).then_inc(silu_done, 1)

        def results(e):
            act.wait_ge(ys_free, e + 1)
            act.activation(ys[:, :], bank[:, 4:6, :].rearrange("p a b -> p (a b)"), ACT.Copy,
                           scale=gate_all[:, e:e + 1] if isinstance(e, int) else gate_all[:, bass.ds(e, 1)]).then_inc(ys_done, 1)

        def step_hi(e, parity):
            n = (e + 1) * 24
            for j in range(8):
                hi_row(n + j, raw_gate, gate_loaded, (e + 2) * 16, j)
            turn_hi(hidT_hi, hidT_done, e * 2, hidT_hi_done)
            for j in range(8):
                hi_row(n + 8 + j, raw_down, down_loaded, (e + 1) * 16, j)
                if j == 4:
                    act.wait_ge(hid_done, e + 1)
                    silu_of(e + 1)
            return n

        act.wait_ge(routed, 2)
        for h in range(2):
            act.wait_ge(outproj_done, NB)
        turn_hi(xsT_hi[:, 0, :, :], xsT_done, 0, xsT_hi_done)
        for j in range(8):
            hi_row(j, raw_gate, gate_loaded, 16, j, 9 if j == 7 else 1)
        turn_hi(xsT_hi[:, 1, :, :], xsT_done, 2, xsT_hi_done)
        for j in range(8):
            hi_row(16 + j, raw_up, up_loaded, 16, j)
            if j == 4:
                silu_of(0)

        def step_act(e, parity, more):
            n = step_hi(e, parity)
            if more:
                turn_hi(xsT_hi[:, parity, :, :], xsT_done, (e + 2) * 2, xsT_hi_done)
            for j in range(8):
                hi_row(n + 16 + j, raw_up, up_loaded, (e + 2) * 16, j)
                if j == 4:
                    results(e)
        with act.Fori(0, (E - 2) // 2) as pair:
            e = pair * 2
            step_act(e, 0, True)
            step_act(e + 1, 1, True)
        step_act(E - 2, 0, False)
        turn_hi(hidT_hi, hidT_done, 2 * (E - 1), hidT_hi_done)
        for j in range(8):
            hi_row(24 * E + j, raw_down, down_loaded, 16 * E, j)
        act.wait_ge(row_used, 24 * E + 8)
        results(E - 1)

    @block.tensor
    def _(pe):
        def product(out, l_hi, l_lo, r_hi, r_lo, first, last):
            pe.matmul(out, l_hi, r_hi, start=first, stop=False)
            pe.matmul(out, l_hi, r_lo, start=False, stop=False)
            return pe.matmul(out, l_lo, r_hi, start=False, stop=last)

        pe.wait_ge(pool_ready, 5)
        for step in steps:
            kind, arg = step[0], step[1:]
            if kind == "normalise":
                b, = arg
                pe.wait_ge(xn_ready, b + 1)
                if b >= 2:
                    pe.wait_ge(ht_lo_done, 2 * (b - 1))
                for h in range(2):
                    for k in range(4):
                        ins = pe.transpose(bank[:, 4 + 2 * (b % 2) + h, k * P:(k + 1) * P],
                                           x_norm[:, b % 2, (4 * h + k) * P:(4 * h + k + 1) * P], ident[:, :])
                    ins.then_inc(xt_done, 1)
            elif kind == "vectors":
                pe.wait_ge(vec_loaded, 5 * 16)
                pe.transpose(bank[:, 0, 0:44], vec_rows[:, :], ident[0:44, 0:44]).then_inc(vec_t, 1)
                pe.wait_ge(vec_copied, 1)
            elif kind == "project":
                g, j = arg
                what, c0, _ = GROUPS[g]
                if g == 0 and j == 0:
                    pe.wait_ge(ht_lo_done, 2 * NB)
                if j == 0:
                    pe.wait_ge(wlo_done, g + 1)
                if g:
                    pe.wait_ge(*evacuated(g - 1, j))
                wh, wl = w_hi[:, g % 2, :, :], w_lo[:, g % 2, :, :]
                if what == "qkv":
                    for i in range(2):
                        tok = slice((2 * j + i) * P, (2 * j + i + 1) * P)
                        for k in range(KC):
                            ins = product(bank[:, j, i * GW:(i + 1) * GW], hT_hi[:, k, tok], hT_lo[:, k, tok],
                                          wh[:, k, :], wl[:, k, :], k == 0, k == KC - 1)
                else:
                    ch = slice((j // 2) * P, (j // 2 + 1) * P)
                    tok = slice((j % 2) * S, (j % 2 + 1) * S)
                    for k in range(KC):
                        ins = product(bank[:, j, :], wh[:, k, ch], wl[:, k, ch], hT_hi[:, k, tok], hT_lo[:, k, tok],
                                      k == 0, k == KC - 1)
                ins.then_inc(proj_done, 1)
            elif kind == "gates":
                ct, d = arg
                pe.wait_ge(bd_lo_done, ct + 1)
                pe.wait_ge(xc_lo_done, ct + 1)
                if ct or d:
                    pe.wait_ge(sigm_done, 4 * ct + 2 * d)
                for m in range(2):
                    for s in range(SEQS):
                        tok = slice(s * S, (s + 1) * S)
                        ins = product(bank[:, 4 + 2 * m + s, :], bd_hi[:, 2 * d + m, :], bd_lo[:, 2 * d + m, :],
                                      xc_hi[:, tok], xc_lo[:, tok], True, True)
                ins.then_inc(gates_done, 1)

        def transposes(out_bank, pieces, done):
            for i, piece in enumerate(pieces):
                ins = pe.transpose(bank[:, out_bank, i * P:(i + 1) * P], piece, ident[:, :])
            ins.then_inc(done, 1)

        for kind, n in attn:
            if kind == "turn":
                b = n
                pe.wait_ge(qk_lo_done, 2 * (b + 1))
                for i in range(USES):
                    u = USES * b + i
                    if prep_free(u) > 0:
                        pe.wait_ge(qkT_out, prep_free(u))
                    if i < 2:
                        pieces = [q_pair[:, 4 * i + h, :, :].rearrange("p a d -> p (a d)") for h in range(4)]
                    else:
                        pieces = [k_pair[:, g, v, :, :].rearrange("p a d -> p (a d)") for g in range(KVH) for v in range(2)]
                    transposes(prep_bank(u), pieces, qkT_done)
            elif kind == "head":
                if n < HEADS:
                    s, h = divmod(n, HQ)
                    kv = h // (HQ // KVH)
                    pe.wait_ge(qkT_out, USES * BPS * (s + 1))
                    for qb in range(BPS):
                        u = BPS * n + qb
                        if u >= 2:
                            pe.wait_ge(exp_done, u - 1)
                        q = qT[:, s, h, qb * P:(qb + 1) * P]
                        pe.matmul(bank[:, u % 2, :], q, kT[:, s, kv, 0, :], start=True, stop=False)
                        pe.matmul(bank[:, u % 2, :], q, kT[:, s, kv, 1, :], start=False, stop=True).then_inc(scores_done, 1)
                m = n - 2
                if 0 <= m < HEADS:
                    s = m // HQ
                    pe.wait_ge(v_lo_done, BPS * (s + 1))
                    if m % 2 == 0 and m:
                        pe.wait_ge(mixA_lo_done, m // 2)
                    for kc in range(BPS):
                        pe.wait_ge(probT_lo_done, BPS * m + kc + 1)
                        blk, cols = BPS * s + kc, pair_cols(m)
                        product(bank[:, 6, :], v_hi[:, blk, cols], v_lo[:, blk, cols], probT_hi[:, kc, :], probT_lo[:, kc, :],
                                m % 2 == 0 and kc == 0, m % 2 == 1 and kc == BPS - 1).then_inc(pv_done, 1)
                m = n - 1
                if 0 <= m < HEADS:
                    if m:
                        pe.wait_ge(probT_lo_done, BPS * m)
                    for qb in range(BPS):
                        pe.wait_ge(prob_done, BPS * m + qb + 1)
                        for kc in range(BPS):
                            ins = pe.transpose(bank[:, 2 + kc, qb * P:(qb + 1) * P], prob[:, m % 2, qb, kc * P:(kc + 1) * P], ident[:, :])
                        ins.then_inc(probT_done, 1)

        pe.wait_ge(mixA_lo_done, HEADS // 2)
        pe.wait_ge(mixL_lo_done, 1)
        for b in range(NB + 2):
            if b < NB:
                if b >= 2:
                    pe.wait_ge(x2_done, b - 1)
                tok = slice(b * P, (b + 1) * P)
                for k in range(KC):
                    if b == 0:
                        pe.wait_ge(wo_lo_done, k + 1)
                    hi, lo, i = (mixA_hi, mixA_lo, k) if k < ATTN_W // P else (mixL_hi, mixL_lo, k - ATTN_W // P)
                    for h in range(2):
                        cols = slice(h * 512, (h + 1) * 512)
                        ins = product(bank[:, 2 * (b % 2) + h, :], hi[:, i, tok], lo[:, i, tok], wo_hi[:, k, cols], wo_lo[:, k, cols],
                                      k == 0, k == KC - 1)
                ins.then_inc(outproj_done, 1)
            c = b - 1
            if 0 <= c < NB:
                pe.wait_ge(h2_done, c + 1)
                for h in range(2):
                    if c:
                        pe.wait_ge(h2T_out, 2 * (c - 1) + h + 1)
                    transposes(4 + h, [h2[:, c % 2, (4 * h + i) * P:(4 * h + i + 1) * P] for i in range(4)], h2T_done)
            c = b - 2
            if 0 <= c < NB:
                pe.wait_ge(h2T_out, 2 * (c + 1))
                pe.wait_ge(consts3_loaded, 2 * 16)
                for k in range(KC):
                    ins = pe.matmul(bank[:, 7, c * E:(c + 1) * E], h2T[:, c % 2, k, :], router[:, k, :], start=(k == 0), stop=(k == KC - 1))
                ins.then_inc(logits_done, 1)
        pe.wait_ge(aff_done, 1)
        for b in range(BPS):
            ins = pe.transpose(bank[0:48, 6, b * P:(b + 1) * P], aff_pad[:, b, :], ident[:, :])
        ins.then_inc(affT_done, 1)
        pe.wait_ge(stacked_done, 1)
        for i in range(2):
            ins = pe.transpose(bank[:, 5, i * E:(i + 1) * E], stacked[:, i, :], ident[0:E, 0:E])
        ins.then_inc(stackedT_done, 1)

        def rows(n, first_bank, l_hi, l_lo, between, inc_last=1):
            for j in range(8):
                if j in between:
                    between[j]()
                pe.wait_ge(row_lo, n + (j + 1))
                for h in range(2):
                    cols = slice(h * 512, (h + 1) * 512)
                    ins = product(bank[:, first_bank + h, :], l_hi[:, j, :], l_lo[:, j, :], e_hi[:, j % 4, cols], e_lo[:, j % 4, cols],
                                  j == 0, j == 7)
                ins.then_inc(row_used, inc_last if j == 7 else 1)

        def turn_tokens(loaded, parity):
            pe.wait_ge(xs_loaded[parity], loaded)
            for h in range(2):
                transposes(6 + h, [xs[:, parity, (4 * h + i) * P:(4 * h + i + 1) * P] for i in range(4)], xsT_done)

        def turn_hidden(e):
            pe.wait_ge(hid_done, e + 1)
            for h in range(2):
                transposes(6 + h, [hid[:, (4 * h + i) * P:(4 * h + i + 1) * P] for i in range(4)], hidT_done)

        pe.wait_ge(routed, 2)
        turn_tokens(16, 0)
        pe.wait_ge(xsT_lo_done, 2)
        def tokens_1():
            turn_tokens(16, 1)
        rows(0, 0, xsT_hi[:, 0, :, :], xsT_lo[:, 0, :, :], {6: tokens_1}, 9)
        rows(16, 2, xsT_hi[:, 0, :, :], xsT_lo[:, 0, :, :], {})

        def step_pe(e, parity, more):
            n = (e + 1) * 24
            other = 1 - parity
            def hidden():
                pe.wait_ge(xsT_lo_done, e * 2 + 4)
                turn_hidden(e)
            def tokens():
                turn_tokens(tokens_at(e, parity), parity)
            pe.wait_ge(xsT_lo_done, e * 2 + 4)
            pe.wait_ge(silu_done, e + 1)
            rows(n, 0, xsT_hi[:, other, :, :], xsT_lo[:, other, :, :], {6: hidden})
            pe.wait_ge(hidT_lo_done, e * 2 + 2)
            if not (isinstance(e, int) and e == 0):
                pe.wait_ge(ys_done, e)
            rows(n + 8, 4, hidT_hi, hidT_lo, {4: tokens} if more else {})
            rows(n + 16, 2, xsT_hi[:, other, :, :], xsT_lo[:, other, :, :], {})

        def tokens_at(e, parity):
            return (e - parity) * 8 + 32

        with pe.Fori(0, (E - 2) // 2) as pair:
            e = pair * 2
            step_pe(e, 0, True)
            step_pe(e + 1, 1, True)
        step_pe(E - 2, 0, False)
        turn_hidden(E - 1)
        pe.wait_ge(hidT_lo_done, 2 * E)
        pe.wait_ge(ys_done, E - 1)
        rows(24 * E, 4, hidT_hi, hidT_lo, {})

    @block.vector
    def _(dve):
        own = [0]

        def link(ins):
            own[0] += 1
            ins.then_inc(dve_step, 1)
            dve.wait_ge(dve_step, own[0])

        dve.wait_ge(g1_loaded, 16)
        for half in range(SEQS):
            cols = slice(half * BPS, (half + 1) * BPS)
            dve.wait_ge(root_ready, half + 1)
            dve.reciprocal(rstd1[:, cols], root1[:, cols]).then_inc(rstd_ready, 1)
        dve.wait_ge(rstd_ready, SEQS)
        for step in steps:
            kind, arg = step[0], step[1:]
            if kind == "normalise":
                b, = arg
                if b >= 2:
                    dve.wait_ge(xt_done, 2 * (b - 1))
                dve.scalar_tensor_tensor(out=x_norm[:, b % 2, :], in0=x_nat[:, b, :], scalar=rstd1[:, b:b + 1],
                                         in1=g1b[:, :], op0=ALU.mult, op1=ALU.mult).then_inc(xn_ready, 1)
                for bb in ([b - 1] if b else []) + ([b] if b == NB - 1 else []):
                    for h in range(2):
                        dve.wait_ge(ht_hi_done, 2 * bb + h + 1)
                        out = hT_lo[:, 4 * h:4 * h + 4, bb * P:(bb + 1) * P]
                        dve.tensor_tensor(out, bank[:, 4 + 2 * (bb % 2) + h, :].rearrange("p (k t) -> p k t", k=4),
                                          hT_hi[:, 4 * h:4 * h + 4, bb * P:(bb + 1) * P].bitcast(F32),
                                          ALU.subtract).then_inc(ht_lo_done, 1)
            elif kind == "split_w":
                g, = arg
                dve.wait_ge(whi_done, g + 1)
                dve.tensor_tensor(w_lo[:, g % 2, :, :], w_raw[:, :, :], w_hi[:, g % 2, :, :].bitcast(F32),
                                  ALU.subtract).then_inc(wlo_done, 1)
            elif kind == "vectors":
                dve.wait_ge(vec_t, 1)
                dve.tensor_copy(vecs[:, :], bank[:, 0, 0:44]).then_inc(vec_copied, 1)
                dve.wait_ge(vec_copied, 1)
                lam = vecs[:, V_LAM:V_LAM + 2 * CT]
                link(dve.tensor_scalar(sp_neg, lam, -1.0, None, ALU.mult))
                link(dve.tensor_tensor(sp_abs, lam, sp_neg, ALU.max))
                dve.tensor_scalar(sp_pos, sp_neg, 0.0, None, ALU.max)
                dve.wait_ge(sp_exp_done, 1)
                link(dve.tensor_scalar(sp_den, sp_exp, 2.0, None, ALU.add))
                link(dve.reciprocal(sp_z, sp_den))
                link(dve.tensor_tensor(sp_z, sp_z, sp_exp, ALU.mult))
                link(dve.tensor_tensor(sp_z2, sp_z, sp_z, ALU.mult))
                link(dve.tensor_scalar(sp_p, sp_z2, 1.0 / 17, None, ALU.mult))
                for n in range(15, 1, -2):
                    link(dve.scalar_tensor_tensor(out=sp_p, in0=sp_p, scalar=1.0 / n, in1=sp_z2, op0=ALU.add, op1=ALU.mult))
                link(dve.scalar_tensor_tensor(out=sp_p, in0=sp_p, scalar=1.0, in1=sp_z, op0=ALU.add, op1=ALU.mult))
                link(dve.scalar_tensor_tensor(out=sp_p, in0=sp_p, scalar=2.0, in1=sp_pos, op0=ALU.mult, op1=ALU.add))
                dve.tensor_scalar(lru_c, sp_p, LRU_C, None, ALU.mult)
                dve.tensor_scalar(neg_c, sp_p, -LRU_C, None, ALU.mult)
                dve.tensor_scalar(neg_2c, sp_p, -2 * LRU_C, None, ALU.mult).then_inc(lru_c_done, 1)
            elif kind == "empty":
                g, j = arg
                what, c0, _ = GROUPS[g]
                if what == "xr":
                    dve.wait_ge(proj_done, JOBS * g + j + 1)
                    dve.tensor_copy(xr_pad[:, c0 + j // 2, j % 2, CONV_LEFT:CONV_LEFT + S], bank[:, j, :]).then_inc(xr_out, 1)
            elif kind == "conv":
                ct, = arg
                xcs = xc[:, :].rearrange("p (s t) -> p s t", s=SEQS)
                taps = [xr_pad[:, ct, :, i:i + S] for i in range(TAPS)]
                w = [vecs[:, V_CONVW + CT * i + ct:V_CONVW + CT * i + ct + 1] for i in range(TAPS)]
                dve.wait_ge(xr_out, 2 * ct + 2)
                link(dve.tensor_scalar(xcs, taps[0], w[0], vecs[:, V_CONVB + ct:V_CONVB + ct + 1], ALU.mult, ALU.add))
                for i in range(1, TAPS):
                    ins = dve.scalar_tensor_tensor(out=xcs, in0=taps[i], scalar=w[i], in1=xcs, op0=ALU.mult, op1=ALU.add)
                    if i < TAPS - 1:
                        link(ins)
                ins.then_inc(xc_done, 1)
                dve.wait_ge(bd_hi_done, ct + 1)
                dve.tensor_tensor(bd_lo[:, :, :], bd_raw[:, :, :], bd_hi[:, :, :].bitcast(F32), ALU.subtract).then_inc(bd_lo_done, 1)
                dve.wait_ge(xc_hi_done, ct + 1)
                dve.tensor_tensor(xc_lo[:, :], xc[:, :], xc_hi[:, :].bitcast(F32), ALU.subtract).then_inc(xc_lo_done, 1)
            elif kind == "decay":
                ct, = arg
                for d in range(2):
                    dve.wait_ge(sigm_done, 4 * ct + 2 * d + 2)
                    link(dve.tensor_tensor(ib[d][:, :], ib[d][:, :], xc[:, :], ALU.mult))
                for d in range(2):
                    dve.wait_ge(tanh_done, 2 * ct + d + 1)
                    dve.scalar_tensor_tensor(out=mult[d][:, :], in0=mult[d][:, :], scalar=1.0, in1=rt[d][:, :],
                                             op0=ALU.add, op1=ALU.mult).then_inc(mult2_done, 1)
            elif kind == "scan":
                ct, = arg
                for d in range(2):
                    dve.wait_ge(root_done, 2 * ct + d + 1)
                    link(dve.tensor_tensor(ib[d][:, :], ib[d][:, :], mult[d][:, :], ALU.mult))
                    for s in range(SEQS):
                        a, b, h = (v[:, s * S:(s + 1) * S] for v in (decay[d], ib[d], rt[d]))
                        if d:
                            a, b, h = (v[d][:, (s + 1) * S - 1:s * S - 1 if s else None:-1] for v in (decay, ib, rt))
                        ins = dve.tensor_tensor_scan(h, a, b, 0.0, ALU.mult, ALU.add)
                    link(ins)
                link(dve.tensor_tensor(rt[0][:, :], rt[0][:, :], rt[1][:, :], ALU.add))
                dve.wait_ge(gate_out, 2 * ct + 2)
                dve.tensor_tensor(lru_out[:, ct, :], lru_out[:, ct, :], rt[0][:, :], ALU.mult).then_inc(scan_done, 1)

        def newton(rstd, mean_sq, tmp):
            link(dve.tensor_tensor(tmp, rstd, rstd, ALU.mult))
            link(dve.tensor_tensor(tmp, tmp, mean_sq, ALU.mult))
            link(dve.tensor_scalar(tmp, tmp, -0.5, 1.5, ALU.mult, ALU.add))
            return dve.tensor_tensor(rstd, rstd, tmp, ALU.mult)

        dve.wait_ge(proj_done, NG * JOBS)
        for kind, n in attn:
            if kind == "stats":
                for b in range(n * BPS, (n + 1) * BPS):
                    dve.wait_ge(qk_sq_done, b + 1)
                    dve.tensor_reduce(qk_stat[:, 0, b * NH:(b + 1) * NH],
                                      (qk_sq, swapped)[b % 2][:, :].rearrange("p (h d) -> p h d", h=NH), AX_X, ALU.add).then_inc(qk_sum_done, 1)
                cols = slice(n * BPS * NH, (n + 1) * BPS * NH)
                dve.wait_ge(qk_sum_done, (n + 1) * BPS)
                dve.tensor_scalar(qk_stat[:, 1, cols], qk_stat[:, 0, cols], 1.0 / HD, EPS, ALU.mult, ALU.add)
                dve.wait_ge(qk_root_done, n + 1)
                link(dve.reciprocal(qk_stat[:, 3, cols], qk_stat[:, 2, cols]))
                newton(qk_stat[:, 3, cols], qk_stat[:, 1, cols], qk_stat[:, 2, cols]).then_inc(qk_rstd_done, 1)
                dve.wait_ge(qk_rstd_done, n + 1)
            elif kind == "prepare":
                b = n
                dve.wait_ge(v_hi_done, b + 1)
                v_at = lambda v: v[:, b, HD:HD + 2 * HD * KVH].rearrange("p (g w) -> p g w", g=KVH)[:, :, 0:HD]
                dve.tensor_tensor(v_at(v_lo), qkv[:, b, QK:QKV].rearrange("p (g w) -> p g w", g=KVH), v_at(v_hi).bitcast(F32),
                                  ALU.subtract).then_inc(v_lo_done, 1)
                dve.wait_ge(tabs_done, 13)
                quarter = HD // 4
                for i, (c0, h) in enumerate(((0, HQ), (ATTN_W, KVH))):
                    for a in range(2):
                        src = qkv[:, b, c0:c0 + h * HD].rearrange("p (h a o d) -> p h a o d", h=h, a=2, o=2)[:, :, a, ::-1, :]
                        out = swapped[:, c0:c0 + h * HD].rearrange("p (h a o d) -> p h a o d", h=h, a=2, o=2)[:, :, a, :, :]
                        sin = tab[:, 2 * i + 1, b % BPS:b % BPS + 1, a * 2 * quarter:(a + 1) * 2 * quarter].rearrange(
                            "p b (o d) -> p b o d", o=2).to_broadcast([P, h, 2, quarter])
                        ins = dve.tensor_tensor(out, src, sin, ALU.mult)
                ins.then_inc(swapped_done, 1)
                dve.wait_ge(swapped_done, b + 1)
                dve.wait_ge(turned_done, 2 * (b + 1))
                if b:
                    dve.wait_ge(qk_hi_done, b)
                link(dve.tensor_tensor(qk_norm[:, :], turned[:, :], swapped[:, :], ALU.add))
                qn = qk_norm[:, :].rearrange("p (h d) -> p h d", h=NH)
                dve.tensor_tensor(qn, qn, qk_stat[:, 3, b * NH:(b + 1) * NH].unsqueeze(2).to_broadcast([P, NH, HD]),
                                  ALU.mult).then_inc(qk_norm_done, 1)
                dve.wait_ge(qk_norm_done, b + 1)
                dve.wait_ge(qk_hi_done, b + 1)
                dve.tensor_tensor(q_pair[:, :, 1, :].bitcast(F32R), qn[:, 0:HQ, :], q_pair[:, :, 0, :], ALU.subtract).then_inc(qk_lo_done, 1)
                for copy in range(2):
                    ins = dve.tensor_tensor(k_pair[:, :, 1, copy, :].bitcast(F32R), qn[:, HQ:NH, :], k_pair[:, :, 0, 0, :], ALU.subtract)
                ins.then_inc(qk_lo_done, 1)
            elif kind == "head":
                m = n - 3
                if m >= 0 and m % 2:
                    dve.wait_ge(mixA_hi_done, (m + 1) // 2)
                    where = (slice(None), m % HQ // 2, slice(m // HQ * S, (m // HQ + 1) * S))
                    dve.tensor_tensor(mixA_lo[where], bank[:, 6, :], mixA_hi[where].bitcast(F32), ALU.subtract).then_inc(mixA_lo_done, 1)
                for i in range(BPS + 1):
                    m = n - 2
                    if i < BPS and 0 <= m < HEADS:
                        dve.wait_ge(probT_hi_done, BPS * m + i + 1)
                        dve.tensor_tensor(probT_lo[:, i, :], bank[:, 2 + i, :], probT_hi[:, i, :].bitcast(F32), ALU.subtract).then_inc(probT_lo_done, 1)
                    if n < HEADS:
                        u = BPS * n + i
                        if i < BPS:
                            dve.wait_ge(scores_done, u + 1)
                            dve.tensor_reduce(row_stat[:, 0, u:u + 1], bank[:, u % 2, :], AX_X, ALU.max, negate=True).then_inc(max_done, 1)
                        if i:
                            dve.wait_ge(exp_done, u)
                            dve.reciprocal(row_stat[:, 2, u - 1:u], row_stat[:, 1, u - 1:u]).then_inc(recip_done, 1)

        dve.wait_ge(mixL_hi_done, 1)
        dve.tensor_tensor(mixL_lo[:, :, :], lru_out[:, :, :], mixL_hi[:, :, :].bitcast(F32), ALU.subtract).then_inc(mixL_lo_done, 1)
        for k in range(KC):
            dve.wait_ge(wo_hi_done, k + 1)
            dve.tensor_tensor(wo_lo[:, k, :], wo_raw[:, k % 2, :], wo_hi[:, k, :].bitcast(F32), ALU.subtract).then_inc(wo_lo_done, 1)
        for b in range(NB):
            dve.wait_ge(outproj_done, b + 1)
            dve.wait_ge(xa_loaded[b % 2], 16 * (b // 2 + 1))
            if b >= 2:
                dve.wait_ge(x2_stored[b % 2], 16 * (b // 2))
            dve.tensor_tensor(x2[:, b % 2, :], bank[:, 2 * (b % 2):2 * (b % 2) + 2, :].rearrange("p a b -> p (a b)"),
                              x_again[:, b % 2, :], ALU.add).then_inc(x2_done, 1)
            dve.wait_ge(sumsq2_done, b + 1)
            r, v, t = rstd1[:, b:b + 1], small[:, 120:121], small[:, 121:122]
            link(dve.tensor_scalar(v, sumsq1[:, b:b + 1], 1.0 / D, EPS, ALU.mult, ALU.add))
            dve.wait_ge(root2_done, b + 1)
            link(dve.reciprocal(r, root1[:, b:b + 1]))
            link(newton(r, v, t))
            if b == 0:
                dve.wait_ge(consts3_loaded, 2 * 16)
            dve.scalar_tensor_tensor(out=h2[:, b % 2, :], in0=x2[:, b % 2, :], scalar=r, in1=g2b[:, :],
                                     op0=ALU.mult, op1=ALU.mult).then_inc(h2_done, 1)
        logits = bank[:, 7, 0:NB * E].rearrange("p (b e) -> p b e", b=NB)
        spread = lambda v: v.unsqueeze(2).to_broadcast([P, NB, E])
        dve.wait_ge(logits_done, NB)
        link(dve.tensor_reduce(aff_stat[:, 0, :], logits, AX_X, ALU.max))
        dve.tensor_tensor(aff_e[:, :, :], logits, spread(aff_stat[:, 0, :]), ALU.subtract).then_inc(aff_shifted, 1)
        dve.wait_ge(aff_exp_done, 1)
        link(dve.tensor_reduce(aff_stat[:, 1, :], aff_e[:, :, :], AX_X, ALU.add))
        link(dve.reciprocal(aff_stat[:, 2, :], aff_stat[:, 1, :]))
        dve.wait_ge(pad_zeroed, 1)
        for s in range(SEQS):
            blocks = slice(s * BPS, (s + 1) * BPS)
            ins = dve.tensor_tensor(aff_pad[:, :, 32 * s:32 * s + E], aff_e[:, blocks, :],
                                    spread(aff_stat[:, 2, :])[:, blocks, :], ALU.mult)
        ins.then_inc(aff_done, 1)
        dve.wait_ge(affT_done, 1)
        dve.wait_ge(outproj_done, NB)
        link(dve.tensor_copy(aff_work[:, 0, :], bank[0:48, 6, :]))
        for r in range(CAP // 8):
            now, then = aff_work[:, r % 2, :], aff_work[:, (r + 1) % 2, :]
            eight = slice(8 * r, 8 * r + 8)
            link(dve.max(top_val[:, eight], now))
            link(dve.max_index(top_idx[:, eight], top_val[:, eight], now))
            if r < CAP // 8 - 1:
                link(dve.match_replace(then, top_val[:, eight], now, -1.0))
        link(dve.tensor_copy(stacked[:, 0, 0:CAP], top_idx[0:E, :]))
        dve.tensor_scalar(stacked[:, 0, CAP:P], top_idx[32:32 + E, :], float(S), None, ALU.add)
        dve.tensor_copy(stacked[:, 1, 0:CAP], top_val[0:E, :])
        dve.tensor_copy(stacked[:, 1, CAP:P], top_val[32:32 + E, :]).then_inc(stacked_done, 1)
        dve.wait_ge(stackedT_done, 1)
        dve.tensor_copy(idx_all[:, :], bank[:, 5, 0:E]).then_inc(routed, 1)
        dve.tensor_copy(gate_all[:, :], bank[:, 5, E:2 * E]).then_inc(routed, 1)

        def lo_row(n, raw, j, inc=1):
            dve.wait_ge(row_hi, n + (j + 1))
            dve.tensor_tensor(e_lo[:, j % 4, :], raw[:, j // 2, j % 2, :], e_hi[:, j % 4, :].bitcast(F32), ALU.subtract).then_inc(row_lo, inc)

        def turn_lo(out, hi, hi_done, count, done):
            for h in range(2):
                dve.wait_ge(hi_done, count + (h + 1))
                dve.tensor_tensor(out[:, 4 * h:4 * h + 4, :], bank[:, 6 + h, :].rearrange("p (k t) -> p k t", k=4),
                                  hi[:, 4 * h:4 * h + 4, :].bitcast(F32), ALU.subtract).then_inc(done, 1)

        def hidden(e):
            dve.wait_ge(row_used, e * 24 + 24)
            dve.wait_ge(silu_done, e + 1)
            dve.tensor_tensor(hid[:, :], bank[:, 2:4, :].rearrange("p a b -> p (a b)"), silu[:, :], ALU.mult).then_inc(hid_done, 1)

        turn_lo(xsT_lo[:, 0, :, :], xsT_hi[:, 0, :, :], xsT_hi_done, 0, xsT_lo_done)
        for j in range(8):
            lo_row(0, raw_gate, j, 9 if j == 7 else 1)
        turn_lo(xsT_lo[:, 1, :, :], xsT_hi[:, 1, :, :], xsT_hi_done, 2, xsT_lo_done)
        for j in range(8):
            lo_row(16, raw_up, j)

        def step_dve(e, parity, more):
            n = (e + 1) * 24
            for j in range(8):
                lo_row(n, raw_gate, j)
                if j == 3:
                    hidden(e)
            turn_lo(hidT_lo, hidT_hi, hidT_hi_done, e * 2, hidT_lo_done)
            for j in range(8):
                lo_row(n + 8, raw_down, j)
            if more:
                turn_lo(xsT_lo[:, parity, :, :], xsT_hi[:, parity, :, :], xsT_hi_done, (e + 2) * 2, xsT_lo_done)
            for j in range(8):
                lo_row(n + 16, raw_up, j)
        with dve.Fori(0, (E - 2) // 2) as pair:
            e = pair * 2
            step_dve(e, 0, True)
            step_dve(e + 1, 1, True)
        step_dve(E - 2, 0, False)
        hidden(E - 1)
        turn_lo(hidT_lo, hidT_hi, hidT_hi_done, 2 * (E - 1), hidT_lo_done)
        for j in range(8):
            lo_row(24 * E, raw_down, j)

    ctx.close()


_INS = ["x_prompt", "x_sample", "norm1_g", "w_in", "q_norm_g", "k_norm_g", "conv_w", "conv_b", "lru_w_r", "lru_b_r",
        "lru_w_i", "lru_b_i", "lru_lambda", "w_out", "norm2_g", "router_w", "exp_w_gate", "exp_w_up", "exp_w_down"]


def rope_tables(S, head_dim):
    import numpy as np
    pos = np.arange(S)
    axis_dim = head_dim // 2
    inv_freq = (np.float32(ROPE_THETA) ** (-np.arange(0, axis_dim, 2, dtype=np.float32) / np.float32(axis_dim))).astype(np.float32)
    row = (pos // GRID_W).astype(np.float32)[:, None] * inv_freq
    col = (pos % GRID_W).astype(np.float32)[:, None] * inv_freq
    cos = np.concatenate([np.cos(row), np.cos(row), np.cos(col), np.cos(col)], axis=1).astype(np.float32)
    sin = np.concatenate([-np.sin(row), np.sin(row), -np.sin(col), np.sin(col)], axis=1).astype(np.float32)
    return cos, sin


def kernel(**inputs):
    import numpy as np
    import concourse.bacc as bacc
    from concourse.bass_utils import run_bass_kernel_spmd

    nc = bacc.Bacc("TRN2", target_bir_lowering=False, num_devices=1)
    arrays, args = {}, []
    S, D = inputs["x_prompt"].shape[1:]
    cos, sin = rope_tables(S, inputs["q_norm_g"].shape[1])
    given = {name: np.ascontiguousarray(inputs[name]) for name in _INS} | {"rope_cos": cos, "rope_sin": sin}
    for name, a in given.items():
        arrays[f"in_{name}_dram"] = a
        args.append(nc.dram_tensor(f"in_{name}_dram", a.shape, mybir.dt.from_np(a.dtype), kind="ExternalInput").ap())
    args.append(nc.dram_tensor("y_dram", (SEQS * S, D), F32, kind="ExternalOutput").ap())
    layer_program(nc, *args)
    y = run_bass_kernel_spmd(nc, [arrays], core_ids=[0]).results[0]["y_dram"].reshape(SEQS, 1, S, D)
    return y[0], y[1]
```

```python
from contextlib import ExitStack

import concourse.bass as bass
from concourse import mybir

F32 = mybir.dt.float32
F32R = mybir.dt.float32r
U32 = mybir.dt.uint32
ALU = mybir.AluOpType
ACT = mybir.ActivationFunctionType
AX_X = mybir.AxisListType.X

P = 128
SEQS = 2
GRID_W = 64
ROPE_THETA = 10000.0
EPS = 1e-6
LRU_C = 8.0
CONV_LEFT = 2


def layer_program(nc, x0, x1, norm1_g, w_in, q_norm_g, k_norm_g, conv_w, conv_b, lru_w_r, lru_b_r,
                  lru_w_i, lru_b_i, lru_lambda, w_out, norm2_g, router_w, w_gate, w_up, w_down,
                  rope_cos, rope_sin, y):
    S, D = x0.shape[1], x0.shape[2]
    T = SEQS * S
    NB = T // P
    BPS = S // P
    KC = D // P
    HD = q_norm_g.shape[1]
    LRU_W = lru_lambda.shape[2]
    CT = LRU_W // P
    ATTN_W = D - LRU_W
    HQ = ATTN_W // HD
    KV_W = (w_in.shape[2] - ATTN_W - 2 * LRU_W) // 2
    QKV = ATTN_W + 2 * KV_W
    TAPS = conv_w.shape[1]
    BD = lru_w_r.shape[3]
    KVH = KV_W // HD
    E = router_w.shape[2]
    CAP = 2 * S // E
    assert SEQS * CAP == P and HD * 2 == P
    h2_rows = nc.dram_tensor("h2_rows", (T, D), F32, kind="Internal").ap()

    GW = 256
    XR0, GATE0 = QKV, QKV + LRU_W
    GROUPS = [("xr", 0, XR0), ("gate", 0, GATE0), ("xr", 2, XR0 + GW), ("gate", 2, GATE0 + GW),
              ("qkv", 0, 0), ("qkv", GW, GW), ("qkv", 2 * GW, 2 * GW)]
    NG = len(GROUPS)
    JOBS = 4

    ctx = ExitStack()
    sem = lambda name: ctx.enter_context(nc.semaphore(name))

    base = -(-nc.sbuf_base // 64) * 64
    K = 1024

    def at(name, offset, shape, dt):
        return nc.alloc_sbuf_tensor_at(name, shape, dt, offset=base + offset)

    ident = at("ident", 0, [P, P], F32)
    small = at("small", 512, [P, 256], F32)
    vec_rows = at("vec_rows", 1536, [44, P], F32)
    vecs = at("vecs", 2048, [P, 44], F32)
    SM = 2560
    eps = small[:, 0:1]
    sumsq1 = small[:, 8:16]
    root1 = small[:, 16:24]
    rstd1 = small[:, 24:32]
    sp_neg, sp_abs, sp_exp, sp_den, sp_z, sp_z2, sp_p, sp_pos = (small[:, 32 + 8 * i:40 + 8 * i] for i in range(8))
    lru_c, neg_c, neg_2c = (small[:, 96 + 8 * i:104 + 8 * i] for i in range(3))
    V_CONVW, V_CONVB, V_BR, V_BI, V_LAM = 0, 16, 20, 28, 36

    lru_out = at("lru_out", SM, [P, CT, T], F32)
    qkv = at("qkv", SM + 16 * K, [P, NB, QKV], F32)
    R1 = SM + 40 * K
    hT_hi = at("hT_hi", R1, [P, KC, T], F32R)
    hT_lo = at("hT_lo", R1 + 32 * K, [P, KC, T], F32R)
    w_raw = at("w_raw", R1 + 64 * K, [P, KC, GW], F32)
    w_hi = at("w_hi", R1 + 72 * K, [P, 2, KC, GW], F32R)
    w_lo = at("w_lo", R1 + 88 * K, [P, 2, KC, GW], F32R)
    XP = S + TAPS - 1
    xr_pad = at("xr_pad", R1 + 104 * K, [P, CT, SEQS, XP], F32)
    R2 = R1 + 104 * K + 16480
    bd_raw = at("bd_raw", R2, [P, 4, P], F32)
    bd_hi = at("bd_hi", R2 + 2 * K, [P, 4, P], F32R)
    bd_lo = at("bd_lo", R2 + 4 * K, [P, 4, P], F32R)
    R3 = R2 + 6 * K
    xc = at("xc", R3, [P, T], F32)
    rt = [at(f"rt{d}", R3 + (4 + 16 * d) * K, [P, T], F32) for d in range(2)]
    ib = [at(f"ib{d}", R3 + (8 + 16 * d) * K, [P, T], F32) for d in range(2)]
    decay = [at(f"decay{d}", R3 + (12 + 16 * d) * K, [P, T], F32) for d in range(2)]
    mult = [at(f"mult{d}", R3 + (16 + 16 * d) * K, [P, T], F32) for d in range(2)]
    xc_hi = at("xc_hi", R3 + 12 * K, [P, T], F32R)
    xc_lo = at("xc_lo", R3 + 28 * K, [P, T], F32R)
    x_nat = at("x_nat", R3, [P, NB, D], F32)
    g1b = at("g1b", SM + 16 * K, [P, D], F32)
    x_norm = at("x_norm", SM + 20 * K, [P, 2, D], F32)
    junk = at("junk", SM + 28 * K, [P, D], F32)

    mixA_hi = at("mixA_hi", R1, [P, ATTN_W // P, T], F32R)
    mixA_lo = at("mixA_lo", R1 + 16 * K, [P, ATTN_W // P, T], F32R)
    qT = at("qT", R1 + 32 * K, [P, SEQS, HQ, S], F32R)
    kT = at("kT", R1 + 64 * K, [P, SEQS, KVH, 2, S], F32R)
    VW = (2 * KVH + 1) * HD
    v_hi = at("v_hi", R1 + 80 * K, [P, NB, VW], F32R)
    v_lo = at("v_lo", R1 + 90 * K, [P, NB, VW], F32R)
    QK = ATTN_W + KV_W
    NH = HQ + KVH
    R4 = R1 + 100 * K
    cos_sin = at("cos_sin", R4 + 4 * K, [P, 2, BPS, HD], F32)
    tab = at("tab", R4 + 6 * K, [P, 4, BPS, HD], F32)
    gains = at("gains", R4 + 10 * K, [P, 4, HD], F32)
    qk_stat = at("qk_stat", R4 + 11 * K, [P, 4, NB * NH], F32)
    PROB_SLOTS = 10
    R6 = R1 + 126 * K + 512
    prob = at("prob", R6, [P, PROB_SLOTS, S], F32)
    probT_hi = at("probT_hi", R6 + 20 * K, [P, BPS, S], F32R)
    probT_lo = at("probT_lo", R6 + 28 * K, [P, BPS, S], F32R)
    row_stat = at("row_stat", R6 + 36 * K, [P, 3, SEQS * HQ * BPS], F32)
    qk_sq = at("qk_sq", R6 + 20 * K, [P, BPS, QK], F32)
    qk_sq1 = at("qk_sq1", R4, [P, QK], F32)
    sets = [R4 + 12 * K + 512, R6]
    turned = [at(f"turned{i}", o, [P, QK], F32) for i, o in enumerate(sets)]
    swapped = [at(f"swapped{i}", o + 2560, [P, QK], F32) for i, o in enumerate(sets)]
    qk_norm = [at(f"qk_norm{i}", o + 5120, [P, QK], F32) for i, o in enumerate(sets)]
    q_pair = [at(f"q_pair{i}", o + 7680, [P, HQ, 2, HD], F32) for i, o in enumerate(sets)]
    k_pair = [at(f"k_pair{i}", o + 7680 + 4 * K, [P, KVH, 2, 2, HD], F32) for i, o in enumerate(sets)]
    assert R6 + 36 * K + 768 <= nc.sbuf_usable_end - base
    assert QK * 4 == 2560 and VW * NB * 4 == 10 * K

    g2b = at("g2b", SM + 8 * K, [P, D], F32)
    router = at("router", SM + 12 * K, [P, KC, E], F32)
    h2T = at("h2T", SM, [P, 2, KC, P], F32)
    x_again = at("x_again", SM + 16 * K, [P, 2, D], F32)
    x2 = at("x2", SM + 24 * K, [P, 2, D], F32)
    h2 = at("h2", SM + 32 * K, [P, 2, D], F32)
    mixL_hi = at("mixL_hi", R1 + 32 * K, [P, CT, T], F32R)
    mixL_lo = at("mixL_lo", R1 + 48 * K, [P, CT, T], F32R)
    wo_hi = at("wo_hi", R1 + 64 * K, [P, KC, D], F32R)
    wo_lo = at("wo_lo", R1 + 96 * K, [P, KC, D], F32R)
    wo_raw = at("wo_raw", R1 + 128 * K, [P, 2, D], F32)
    R5 = SM + 12 * K + 512
    aff_e = at("aff_e", R5, [P, NB, E], F32)
    aff_pad = at("aff_pad", R5 + 512, [P, BPS, 48], F32)
    aff_stat = at("aff_stat", R5 + 512 + 768, [P, 3, NB], F32)
    aff_work = at("aff_work", R1, [48, 2, S], F32)
    top_val = at("top_val", R1 + 4 * K, [48, CAP], F32)
    top_idx = at("top_idx", R1 + 4 * K + 256, [48, CAP], U32)
    stacked = at("stacked", R1 + 4 * K + 512, [E, 2, P], F32)
    idx_all = at("idx_all", SM - 256, [P, E], U32)
    gate_all = at("gate_all", SM - 128, [P, E], F32)

    RAW0 = nc.sbuf_usable_end - base - 32 * K
    RAW0 -= RAW0 % 64
    raw_gate = at("raw_gate", RAW0, [P, 4, 2, D], F32)
    raw_down = at("raw_down", R1 + 64 * K, [P, 4, 2, D], F32)
    raw_up = at("raw_up", R1 + 96 * K, [P, 4, 2, D], F32)
    e_hi = at("e_hi", R1 + 8 * K, [P, 4, D], F32R)
    e_lo = at("e_lo", R1 + 24 * K, [P, 4, D], F32R)
    xs = at("xs", R1 + 40 * K, [P, 2, D], F32)
    xsT_hi = at("xsT_hi", SM, [P, 2, KC, P], F32R)
    xsT_lo = at("xsT_lo", SM + 8 * K, [P, 2, KC, P], F32R)
    silu = at("silu", SM + 16 * K, [P, D], F32)
    hid = at("hid", SM + 20 * K, [P, D], F32)
    hidT_hi = at("hidT_hi", SM + 24 * K, [P, KC, P], F32R)
    hidT_lo = at("hidT_lo", SM + 28 * K, [P, KC, P], F32R)
    ys = at("ys", SM + 32 * K, [P, D], F32)
    idx_now = at("idx_now", SM + 36 * K, [P, 4], U32)
    assert RAW0 >= R1 + 128 * K

    assert R3 + 36 * K <= nc.sbuf_usable_end - base, (R3 + 36 * K, nc.sbuf_usable_end - base)

    bank = nc.alloc_psum_tensor("bank", [P, 8, 512], F32)

    x_loaded = [sem(f"x_loaded{b}") for b in range(NB)]
    g1_loaded, vec_loaded = sem("g1_loaded"), sem("vec_loaded")
    pool_ready, ident_zeroed = sem("pool_ready"), sem("ident_zeroed")
    sumsq_ready, root_ready, rstd_ready = sem("sumsq_ready"), sem("root_ready"), sem("rstd_ready")
    xn_ready, xt_done, ht_hi_done, ht_lo_done = sem("xn_ready"), sem("xt_done"), sem("ht_hi_done"), sem("ht_lo_done")
    wraw_loaded, whi_done, wlo_done = sem("wraw_loaded"), sem("whi_done"), sem("wlo_done")
    proj_done = sem("proj_done")
    xr_out, gate_out, qkv_out = sem("xr_out"), sem("gate_out"), sem("qkv_out")
    vec_t, vec_copied = sem("vec_t"), sem("vec_copied")
    dve_step, sp_exp_done, lru_c_done = sem("dve_step"), sem("sp_exp_done"), sem("lru_c_done")
    bd_loaded, bd_hi_done, bd_lo_done = sem("bd_loaded"), sem("bd_hi_done"), sem("bd_lo_done")
    xc_done, xc_hi_done, xc_lo_done = sem("xc_done"), sem("xc_hi_done"), sem("xc_lo_done")
    gates_done, sigm_done = sem("gates_done"), sem("sigm_done")
    exps_done, tanh_done, mult2_done, root_done, scan_done = (
        sem("exps_done"), sem("tanh_done"), sem("mult2_done"), sem("root_done"), sem("scan_done"))
    act_step = sem("act_step")
    tabs_loaded, tabs_done, v_zeroed = sem("tabs_loaded"), sem("tabs_done"), sem("v_zeroed")
    qk_sq_done, qk_sum_done, qk_root_done, qk_rstd_done = (
        sem("qk_sq_done"), sem("qk_sum_done"), sem("qk_root_done"), sem("qk_rstd_done"))
    turned_done, swapped_done, summed_done, qk_norm_done = (
        sem("turned_done"), sem("swapped_done"), sem("summed_done"), sem("qk_norm_done"))
    qk_hi_done, qk_lo_done, v_hi_done, v_lo_done = sem("qk_hi_done"), sem("qk_lo_done"), sem("v_hi_done"), sem("v_lo_done")
    qkT_done, qkT_out = sem("qkT_done"), sem("qkT_out")
    scores_done, max_done, exp_done, recip_done, prob_done = (
        sem("scores_done"), sem("max_done"), sem("exp_done"), sem("recip_done"), sem("prob_done"))
    probT_done, probT_hi_done, probT_lo_done = sem("probT_done"), sem("probT_hi_done"), sem("probT_lo_done")
    pv_done, mixA_hi_done, mixA_lo_done = sem("pv_done"), sem("mixA_hi_done"), sem("mixA_lo_done")
    consts3_loaded, mixL_hi_done, mixL_lo_done = sem("consts3_loaded"), sem("mixL_hi_done"), sem("mixL_lo_done")
    wo_loaded = [sem(f"wo_loaded{i}") for i in range(2)]
    wo_hi_done, wo_lo_done = sem("wo_hi_done"), sem("wo_lo_done")
    xa_loaded = [sem(f"xa_loaded{i}") for i in range(2)]
    outproj_done, x2_done, sumsq2_done, root2_done, h2_done = (
        sem("outproj_done"), sem("x2_done"), sem("sumsq2_done"), sem("root2_done"), sem("h2_done"))
    x2_stored = [sem(f"x2_stored{i}") for i in range(2)]
    h2_stored = [sem(f"h2_stored{i}") for i in range(2)]
    h2T_done, h2T_out, logits_done = sem("h2T_done"), sem("h2T_out"), sem("logits_done")
    aff_shifted, aff_exp_done, aff_done, affT_done = sem("aff_shifted"), sem("aff_exp_done"), sem("aff_done"), sem("affT_done")
    stacked_done, stackedT_done, routed = sem("stacked_done"), sem("stackedT_done"), sem("routed")
    pad_zeroed = sem("pad_zeroed")
    gate_loaded = [sem(f"gate_loaded{i}") for i in range(4)]
    down_loaded = [sem(f"down_loaded{i}") for i in range(4)]
    up_loaded = [sem(f"up_loaded{i}") for i in range(4)]
    row_hi, row_lo, row_used = sem("row_hi"), sem("row_lo"), sem("row_used")
    idx_copied, xs_loaded, xsT_done, xsT_hi_done, xsT_lo_done = (
        sem("idx_copied"), [sem(f"xs_loaded{i}") for i in range(2)], sem("xsT_done"), sem("xsT_hi_done"), sem("xsT_lo_done"))
    silu_done, hid_done, hidT_done, hidT_hi_done, hidT_lo_done = (
        sem("silu_done"), sem("hid_done"), sem("hidT_done"), sem("hidT_hi_done"), sem("hidT_lo_done"))
    ys_done, scattered, ys_free = sem("ys_done"), sem("scattered"), sem("ys_free")
    gather_ready, scatter_ready = sem("gather_ready"), sem("scatter_ready")

    SEMS_OF = {"xr": xr_out, "gate": gate_out, "qkv": qkv_out}

    def evacuated(g, j):
        kind = GROUPS[g][0]
        before = sum(GROUPS[i][0] == kind for i in range(g))
        return SEMS_OF[kind], JOBS * before + j + 1

    steps = []
    for b in range(NB):
        steps.append(("normalise", b))
        if b == 3:
            steps.append(("split_w", 0))
    steps.append(("vectors",))
    LRU_AT = {2: ("conv", 0), 4: ("gates", 0, 0), 5: ("gates", 0, 1), 6: ("decay", 0), 7: ("scan", 0),
              9: ("conv", 1), 10: ("gates", 1, 0), 11: ("gates", 1, 1), 12: ("decay", 1), 13: ("scan", 1),
              14: ("conv", 2), 15: ("gates", 2, 0), 16: ("gates", 2, 1), 17: ("decay", 2), 18: ("scan", 2),
              19: ("conv", 3), 20: ("gates", 3, 0), 21: ("gates", 3, 1), 22: ("decay", 3), 23: ("scan", 3)}
    for n in range(NG * JOBS):
        g, j = divmod(n, JOBS)
        steps.append(("project", g, j))
        if n:
            steps.append(("empty", (n - 1) // JOBS, (n - 1) % JOBS))
        if j == 0 and g + 1 < NG:
            steps.append(("split_w", g + 1))
        if n in LRU_AT:
            steps.append(LRU_AT[n])
    steps.append(("empty", NG - 1, JOBS - 1))

    HEADS = SEQS * HQ
    UNITS = HEADS * BPS
    T_LAG, V_LAG = 6, 8
    USES = 3
    attn = [("square", b) for b in range(BPS)] + [("sum", b) for b in range(BPS)] + [("rstd", 0)]
    for b in range(BPS + 1):
        if b < BPS:
            attn.append(("turn", b))
        if b:
            attn.append(("lo", b - 1))
        if b < BPS:
            attn += [("norm", b), ("hi", b)]
        if b:
            attn += [("transpose", USES * (b - 1) + i) for i in range(USES)]
            attn += [("out", USES * (b - 1) + i) for i in range(USES)]
    beside = {}
    for i in range(BPS):
        b = BPS + i
        beside.setdefault(i, []).append(("square", b))
        beside.setdefault(i + 1, []).append(("sum", b))
        first = 4 + 6 * i
        for stage, at_slot in (("turn", 0), ("norm", 2), ("hi", 3), ("lo", 4)):
            beside.setdefault(first + at_slot, []).append((stage, b))
        for j in range(USES):
            beside.setdefault(first + 5 + j, []).append(("transpose", USES * b + j))
            beside.setdefault(first + 6 + j, []).append(("out", USES * b + j))
    beside.setdefault(BPS + 1, []).insert(0, ("rstd", 1))
    for u in range(UNITS + V_LAG + 2):
        attn.append(("slot", u))
        attn += beside.get(u, [])

    def prep_set(b):
        return b % 2 if b < BPS else 0

    def prep_before(b):
        return b - 1 if b <= BPS else b

    def prep_bank(n):
        return 4 + n % 4 if n < USES * BPS else 7

    def prep_free(n):
        return n - 3 if n < USES * BPS else n

    PAIRS_ONE_BANK = 3

    def out_bank(pair):
        return 6 if pair < PAIRS_ONE_BANK or pair % 2 == 0 else 7

    def pair_cols(head):
        kv = head % HQ // (HQ // KVH)
        first = 2 * HD * kv + (HD if head % 2 == 0 else 0)
        return slice(first, first + 2 * HD)

    block = ctx.enter_context(nc.Block())

    @block.sync
    def _(sp):
        for b in range(NB):
            src = (x0 if b < BPS else x1)[0, (b % BPS) * P:(b % BPS + 1) * P, :]
            sp.dma_start(x_nat[:, b, :], src).then_inc(x_loaded[b], 16)
            if b == 1:
                sp.dma_start(g1b[:, :], norm1_g[0:1, :].to_broadcast([P, D])).then_inc(g1_loaded, 16)
        for g, (_, _, col) in enumerate(GROUPS):
            if g:
                sp.wait_ge(wlo_done, g)
            sp.dma_start(w_raw[:, :, :], w_in[0, :, col:col + GW].rearrange("(k p) n -> p k n", p=P)).then_inc(wraw_loaded, 16)

        sp.wait_ge(xc_done, CT)
        sp.dma_start(cos_sin[:, 0, :, :], rope_cos.rearrange("(b p) d -> p b d", p=P)).then_inc(tabs_loaded, 16)
        sp.dma_start(cos_sin[:, 1, :, :], rope_sin.rearrange("(b p) d -> p b d", p=P)).then_inc(tabs_loaded, 16)
        for i, g in enumerate((q_norm_g, k_norm_g)):
            sp.dma_start(gains[:, 2 * i, :], g[0:1, :].to_broadcast([P, HD])).then_inc(tabs_loaded, 16)

        sp.wait_ge(pv_done, BPS * HEADS)
        for k in range(KC):
            if k == 2:
                sp.dma_start(x_again[:, 0, :], x0[0, 0:P, :]).then_inc(xa_loaded[0], 16)
                sp.dma_start(x_again[:, 1, :], x0[0, P:2 * P, :]).then_inc(xa_loaded[1], 16)
                sp.wait_ge(mixL_lo_done, 1)
                sp.dma_start(g2b[:, :], norm2_g[0:1, :].to_broadcast([P, D])).then_inc(consts3_loaded, 16)
                sp.dma_start(router[:, :, :], router_w[0].rearrange("(k p) e -> p k e", p=P)).then_inc(consts3_loaded, 16)
            if k >= 2:
                sp.wait_ge(wo_lo_done, k - 1)
            sp.dma_start(wo_raw[:, k % 2, :], w_out[0, k * P:(k + 1) * P, :]).then_inc(wo_loaded[k % 2], 16)
        def load(raw, i, w, e, loaded):
            sp.dma_start(raw[:, i, :, :], w[0, e, 2 * i * P:2 * (i + 1) * P, :].rearrange("(r p) n -> p r n", p=P)
                         if isinstance(e, int) else
                         w[0, bass.ds(e, 1), 2 * i * P:2 * (i + 1) * P, :].rearrange("o (r p) n -> p (o r) n", p=P)).then_inc(loaded[i], 16)

        for b in range(NB):
            if b + 2 < NB:
                sp.wait_ge(x2_done, b + 1)
                nb = b + 2
                sp.dma_start(x_again[:, b % 2, :], (x0 if nb < BPS else x1)[0, (nb % BPS) * P:(nb % BPS + 1) * P, :]).then_inc(xa_loaded[b % 2], 16)
            sp.wait_ge(x2_done, b + 1)
            sp.dma_start(y[b * P:(b + 1) * P, :], x2[:, b % 2, :]).then_inc(x2_stored[b % 2], 16)
            sp.wait_ge(h2_done, b + 1)
            sp.dma_start(h2_rows[b * P:(b + 1) * P, :], h2[:, b % 2, :]).then_inc(h2_stored[b % 2], 16)
            if b == 1:
                for i in range(4):
                    load(raw_gate, i, w_gate, 0, gate_loaded)

        sp.wait_ge(outproj_done, NB)
        for i in range(4):
            load(raw_up, i, w_up, 0, up_loaded)
        def step_loads(e):
            for i in range(4):
                sp.wait_ge(row_lo, e * 24 + (2 * i + 2))
                load(raw_gate, i, w_gate, e + 1, gate_loaded)
            for i in range(4):
                sp.wait_ge(row_lo, e * 24 + (8 + 2 * i + 2))
                load(raw_down, i, w_down, e, down_loaded)
            for i in range(4):
                sp.wait_ge(row_lo, e * 24 + (16 + 2 * i + 2))
                load(raw_up, i, w_up, e + 1, up_loaded)
        with sp.Fori(0, E - 1) as e:
            step_loads(e)
        for i in range(4):
            sp.wait_ge(row_lo, (E - 1) * 24 + 8 + 2 * i + 2)
            load(raw_down, i, w_down, E - 1, down_loaded)

    @block.gpsimd
    def _(pool):
        pool.memset(ident[:, :], 0.0).then_inc(ident_zeroed, 1)
        pool.memset(eps, EPS).then_inc(pool_ready, 1)
        pool.memset(bd_raw[:, :, :], 0.0).then_inc(pool_ready, 1)
        pool.memset(xr_pad[:, :, :, 0:CONV_LEFT], 0.0).then_inc(pool_ready, 1)
        pool.memset(xr_pad[:, :, :, CONV_LEFT + S:XP], 0.0).then_inc(pool_ready, 1)
        pool.wait_ge(ident_zeroed, 1)
        pool.affine_select(out=ident[:, :], in_=ident[:, :], compare_op=ALU.not_equal, fill=1.0, base=0,
                           pattern=[[-1, P]], channel_multiplier=1).then_inc(pool_ready, 1)

        pool.wait_ge(proj_done, NG * JOBS)
        pool.memset(v_hi[:, :, :].bitcast(F32), 0.0).then_inc(v_zeroed, 1)
        pool.memset(v_lo[:, :, :].bitcast(F32), 0.0).then_inc(v_zeroed, 1)
        pool.wait_ge(tabs_loaded, 4 * 16)
        quarter = HD // 4
        for i in range(2):
            for a in range(4):
                o = a ^ 1
                pool.tensor_copy(gains[:, 2 * i + 1, a * quarter:(a + 1) * quarter],
                                 gains[:, 2 * i, o * quarter:(o + 1) * quarter]).then_inc(tabs_done, 1)
        pool.wait_ge(tabs_done, 8)
        for i in range(2):
            for j in range(2):
                pool.tensor_tensor(tab[:, 2 * i + j, :, :], cos_sin[:, j, :, :],
                                   gains[:, 2 * i + j:2 * i + j + 1, :].to_broadcast([P, BPS, HD]), ALU.mult).then_inc(tabs_done, 1)
        pool.wait_ge(tabs_done, 12)
        pool.tensor_scalar(tab[:, 0:2, :, :], tab[:, 0:2, :, :], HD ** -0.5, 1.0, ALU.mult, ALU.mult).then_inc(tabs_done, 1)
        pool.wait_ge(tabs_done, 13)
        pool.wait_ge(gates_done, 2 * CT)
        pool.wait_ge(qkv_out, 3 * JOBS)
        for kind, n in attn:
            if kind == "square" and n >= BPS:
                if n > BPS:
                    pool.wait_ge(qk_sum_done, n)
                pool.tensor_tensor(qk_sq1[:, :], qkv[:, n, 0:QK], qkv[:, n, 0:QK], ALU.mult).then_inc(qk_sq_done, 1)
            elif kind == "turn":
                b = n
                if b == 1:
                    pool.wait_ge(scan_done, CT)
                for i, (c0, h) in enumerate(((0, HQ), (ATTN_W, KVH))):
                    pool.tensor_tensor(turned[prep_set(b)][:, c0:c0 + h * HD].rearrange("p (h d) -> p h d", h=h),
                                       qkv[:, b, c0:c0 + h * HD].rearrange("p (h d) -> p h d", h=h),
                                       tab[:, 2 * i, b % BPS:b % BPS + 1, :].to_broadcast([P, h, HD]), ALU.mult).then_inc(turned_done, 1)
                pool.wait_ge(turned_done, 2 * (b + 1))
                pool.wait_ge(swapped_done, b + 1)
                if prep_before(b) > 0:
                    pool.wait_ge(qk_lo_done, 2 * prep_before(b))
                pool.tensor_tensor(qk_norm[prep_set(b)][:, :], turned[prep_set(b)][:, :], swapped[prep_set(b)][:, :],
                                   ALU.add).then_inc(summed_done, 1)
            elif kind == "slot" and 0 <= n - 1 < UNITS:
                u = n - 1
                pool.wait_ge(recip_done, u + 1)
                pool.tensor_scalar(prob[:, u % PROB_SLOTS, :], prob[:, u % PROB_SLOTS, :], row_stat[:, 2, u:u + 1], 1.0,
                                   ALU.mult, ALU.mult).then_inc(prob_done, 1)

        pool.wait_ge(mixL_lo_done, 1)
        pool.memset(aff_pad[:, :, :], 0.0).then_inc(pad_zeroed, 1)

        pool.wait_ge(routed, 2)
        for i in range(2):
            pool.wait_ge(h2_stored[i], 16 * (NB // 2))
            pool.wait_ge(x2_stored[i], 16 * (NB // 2))
        for e in range(2):
            pool.tensor_copy(idx_now[:, e:e + 1], idx_all[:, e:e + 1]).then_inc(idx_copied, 1)
            pool.wait_ge(idx_copied, e + 1)
            pool.indirect_dma_start(xs[:, e, :], None, h2_rows, bass.IndirectOffsetOnAxis(ap=idx_now[:, e:e + 1], axis=0)).then_inc(xs_loaded[e], 16)

        def scatter_step(e, copied):
            pool.tensor_copy(idx_now[:, 2:3], idx_all[:, bass.ds(e, 1)] if not isinstance(e, int) else idx_all[:, e:e + 1]).then_inc(idx_copied, 1)
            pool.wait_ge(idx_copied, copied)
            pool.wait_ge(ys_done, e + 1)
            pool.sem_inc(scatter_ready, 1)
            pool.indirect_dma_start(y, bass.IndirectOffsetOnAxis(ap=idx_now[:, 2:3], axis=0), ys[:, :], None, compute_op=ALU.add).then_inc(scattered, 16)
            pool.wait_ge(scattered, e * 16 + 16)
            pool.sem_inc(ys_free, 1)

        pool.sem_inc(ys_free, 1)
        with pool.Fori(0, (E - 2) // 2) as pair:
            e = pair * 2
            for parity in range(2):
                pool.wait_ge(xsT_done, e * 2 + (2 * parity + 2))
                pool.tensor_copy(idx_now[:, parity:parity + 1], idx_all[:, bass.ds(e + (parity + 2), 1)]).then_inc(idx_copied, 1)
                pool.wait_ge(idx_copied, e * 2 + (3 + 2 * parity))
                pool.sem_inc(gather_ready, 1)
                pool.indirect_dma_start(xs[:, parity, :], None, h2_rows,
                                        bass.IndirectOffsetOnAxis(ap=idx_now[:, parity:parity + 1], axis=0)).then_inc(xs_loaded[parity], 16)
                scatter_step(e + parity, e * 2 + (4 + 2 * parity))
        for e in (E - 2, E - 1):
            scatter_step(e, 2 * e + 3 - (e - (E - 2)))

    @block.scalar
    def _(act):
        own = [0]

        def link(ins):
            own[0] += 1
            ins.then_inc(act_step, 1)
            act.wait_ge(act_step, own[0])

        def load_bd(ct):
            for d in range(2):
                for m, w in enumerate((lru_w_r, lru_w_i)):
                    for n in range(P // BD):
                        act.dma_start(bd_raw[n * BD:(n + 1) * BD, 2 * d + m, n * BD:(n + 1) * BD],
                                      w[0, d, ct * (P // BD) + n, :, :]).then_inc(bd_loaded, 16)

        rows = [(0, conv_w[0].rearrange("t (c p) -> (t c) p", p=P)), (16, conv_b[0].rearrange("(c p) -> c p", p=P)),
                (20, lru_b_r[0].rearrange("d (c p) -> (d c) p", p=P)), (28, lru_b_i[0].rearrange("d (c p) -> (d c) p", p=P)),
                (36, lru_lambda[0].rearrange("d (c p) -> (d c) p", p=P))]
        for at_row, src in rows:
            act.dma_start(vec_rows[at_row:at_row + src.shape[0], :], src).then_inc(vec_loaded, 16)
        act.wait_ge(pool_ready, 5)
        load_bd(0)
        for b in range(NB):
            act.wait_ge(x_loaded[b], 16)
            if b:
                act.wait_ge(sumsq_ready, b)
            act.activation(junk[:, :], x_nat[:, b, :], ACT.Square, accum_out=sumsq1[:, b:b + 1]).then_inc(sumsq_ready, 1)
            if b % BPS == BPS - 1:
                act.wait_ge(sumsq_ready, b + 1)
                act.activation(root1[:, b + 1 - BPS:b + 1], sumsq1[:, b + 1 - BPS:b + 1], ACT.Sqrt,
                               scale=1.0 / D, bias=eps).then_inc(root_ready, 1)
        for step in steps:
            kind, arg = step[0], step[1:]
            if kind == "normalise":
                b, = arg
                for h in range(2):
                    act.wait_ge(xt_done, 2 * b + h + 1)
                    act.activation(hT_hi[:, 4 * h:4 * h + 4, b * P:(b + 1) * P],
                                   bank[:, 4 + 2 * (b % 2) + h, :].rearrange("p (k t) -> p k t", k=4), ACT.Copy).then_inc(ht_hi_done, 1)
            elif kind == "split_w":
                g, = arg
                act.wait_ge(wraw_loaded, 16 * (g + 1))
                if g >= 2:
                    act.wait_ge(proj_done, JOBS * (g - 1))
                act.activation(w_hi[:, g % 2, :, :], w_raw[:, :, :], ACT.Copy).then_inc(whi_done, 1)
            elif kind == "vectors":
                act.wait_ge(dve_step, 2)
                act.activation(sp_exp, sp_abs, ACT.Exp, scale=-1.0).then_inc(sp_exp_done, 1)
            elif kind == "empty":
                g, j = arg
                what, c0, _ = GROUPS[g]
                if what == "gate":
                    act.wait_ge(proj_done, JOBS * g + j + 1)
                    act.activation(lru_out[:, c0 + j // 2, (j % 2) * S:(j % 2 + 1) * S], bank[:, j, :],
                                   ACT.Gelu_apprx_tanh).then_inc(gate_out, 1)
                elif what == "qkv":
                    act.wait_ge(proj_done, JOBS * g + j + 1)
                    act.activation(qkv[:, 2 * j:2 * j + 2, c0:c0 + GW],
                                   bank[:, j, :].rearrange("p (b n) -> p b n", b=2), ACT.Copy).then_inc(qkv_out, 1)
            elif kind == "conv":
                ct, = arg
                act.wait_ge(bd_loaded, 8 * 16 * (ct + 1))
                if ct:
                    act.wait_ge(gates_done, 2 * ct)
                act.activation(bd_hi[:, :, :], bd_raw[:, :, :], ACT.Copy).then_inc(bd_hi_done, 1)
                act.wait_ge(xc_done, ct + 1)
                if ct:
                    act.wait_ge(scan_done, ct)
                act.activation(xc_hi[:, :], xc[:, :], ACT.Copy).then_inc(xc_hi_done, 1)
                if ct + 1 < CT:
                    act.wait_ge(bd_lo_done, ct + 1)
                    load_bd(ct + 1)
            elif kind == "gates":
                ct, d = arg
                act.wait_ge(gates_done, 2 * ct + d + 1)
                if ct:
                    act.wait_ge(scan_done, ct)
                act.activation(rt[d][:, :], bank[:, 4:6, :].rearrange("p a b -> p (a b)"), ACT.Sigmoid,
                               bias=vecs[:, V_BR + CT * d + ct:V_BR + CT * d + ct + 1]).then_inc(sigm_done, 1)
                act.activation(ib[d][:, :], bank[:, 6:8, :].rearrange("p a b -> p (a b)"), ACT.Sigmoid,
                               bias=vecs[:, V_BI + CT * d + ct:V_BI + CT * d + ct + 1]).then_inc(sigm_done, 1)
            elif kind == "decay":
                ct, = arg
                act.wait_ge(sigm_done, 4 * ct + 4)
                act.wait_ge(gates_done, 2 * ct + 2)
                act.wait_ge(lru_c_done, 1)
                for d in range(2):
                    c = CT * d + ct
                    act.activation(decay[d][:, :], rt[d][:, :], ACT.Exp, scale=neg_c[:, c:c + 1])
                    act.activation(mult[d][:, :], rt[d][:, :], ACT.Exp, scale=neg_2c[:, c:c + 1]).then_inc(exps_done, 1)
                    act.wait_ge(exps_done, 2 * ct + d + 1)
                    act.activation(rt[d][:, :], rt[d][:, :], ACT.Tanh, scale=lru_c[:, c:c + 1]).then_inc(tanh_done, 1)
            elif kind == "scan":
                ct, = arg
                for d in range(2):
                    act.wait_ge(mult2_done, 2 * ct + d + 1)
                    act.activation(mult[d][:, :], mult[d][:, :], ACT.Sqrt).then_inc(root_done, 1)

        act.wait_ge(scan_done, CT)
        act.wait_ge(qkv_out, 3 * JOBS)
        for kind, n in attn:
            if kind == "square" and n < BPS:
                act.activation(qk_sq[:, n, :], qkv[:, n, 0:QK], ACT.Square).then_inc(qk_sq_done, 1)
            elif kind == "rstd":
                cols = slice(n * BPS * NH, (n + 1) * BPS * NH)
                act.wait_ge(qk_sum_done, (n + 1) * BPS)
                act.activation(qk_stat[:, 2, cols], qk_stat[:, 0, cols], ACT.Sqrt, scale=1.0 / HD, bias=eps).then_inc(qk_root_done, 1)
            elif kind == "turn":
                if n == 0:
                    act.wait_ge(v_zeroed, 2)
                act.activation(v_hi[:, n, HD:HD + 2 * HD * KVH].rearrange("p (g w) -> p g w", g=KVH)[:, :, 0:HD],
                               qkv[:, n, QK:QKV].rearrange("p (g w) -> p g w", g=KVH), ACT.Copy).then_inc(v_hi_done, 1)
            elif kind == "hi":
                i = prep_set(n)
                act.wait_ge(qk_norm_done, n + 1)
                if prep_before(n) > 0:
                    act.wait_ge(qkT_done, USES * prep_before(n))
                act.activation(q_pair[i][:, :, 0, :].bitcast(F32R), qk_norm[i][:, 0:ATTN_W].rearrange("p (h d) -> p h d", h=HQ), ACT.Copy)
                for copy in range(2):
                    ins = act.activation(k_pair[i][:, :, 0, copy, :].bitcast(F32R),
                                         qk_norm[i][:, ATTN_W:QK].rearrange("p (h d) -> p h d", h=KVH), ACT.Copy)
                ins.then_inc(qk_hi_done, 1)
            elif kind == "out":
                b, i = divmod(n, USES)
                s, tok = b // BPS, slice((b % BPS) * P, (b % BPS + 1) * P)
                act.wait_ge(qkT_done, n + 1)
                out = qT[:, s, 4 * i:4 * i + 4, tok] if i < 2 else kT[:, s, :, :, tok].rearrange("p g v t -> p (g v) t")
                act.activation(out, bank[:, prep_bank(n), :].rearrange("p (h t) -> p h t", h=4), ACT.Copy).then_inc(qkT_out, 1)
            elif kind == "slot":
                u, t, v = n, n - T_LAG, n - V_LAG - 1
                if v >= 0 and v % (2 * BPS) == 2 * BPS - 1:
                    pair = v // (2 * BPS)
                    head = 2 * pair
                    act.wait_ge(pv_done, v + 1)
                    act.activation(mixA_hi[:, head % HQ // 2, head // HQ * S:(head // HQ + 1) * S], bank[:, out_bank(pair), :],
                                   ACT.Copy).then_inc(mixA_hi_done, 1)
                if 0 <= t < UNITS:
                    act.wait_ge(probT_done, t + 1)
                    if t >= BPS:
                        act.wait_ge(pv_done, t - BPS + 1)
                    act.activation(probT_hi[:, t % BPS, :], bank[:, 2 + t % BPS, :], ACT.Copy).then_inc(probT_hi_done, 1)
                if u < UNITS:
                    act.wait_ge(max_done, u + 1)
                    if u >= PROB_SLOTS:
                        act.wait_ge(probT_done, BPS * ((u - PROB_SLOTS) // BPS + 1))
                    act.activation(prob[:, u % PROB_SLOTS, :], bank[:, u % 2, :], ACT.Exp, bias=row_stat[:, 0, u:u + 1],
                                   accum_out=row_stat[:, 1, u:u + 1]).then_inc(exp_done, 1)

        act.wait_ge(scores_done, BPS * HEADS)
        act.activation(mixL_hi[:, :, :], lru_out[:, :, :], ACT.Copy).then_inc(mixL_hi_done, 1)
        for k in range(KC):
            act.wait_ge(wo_loaded[k % 2], 16 * (k // 2 + 1))
            if k == 0:
                act.wait_ge(pv_done, BPS * HEADS)
            act.activation(wo_hi[:, k, :], wo_raw[:, k % 2, :], ACT.Copy).then_inc(wo_hi_done, 1)
        for b in range(NB + 1):
            if b < NB:
                act.wait_ge(x2_done, b + 1)
                if b:
                    act.wait_ge(h2_done, b)
                if b >= 2:
                    act.wait_ge(h2_stored[b % 2], 16 * (b // 2))
                    act.wait_ge(h2T_done, 2 * (b - 1))
                act.activation(h2[:, b % 2, :], x2[:, b % 2, :], ACT.Square, accum_out=sumsq1[:, b:b + 1]).then_inc(sumsq2_done, 1)
                act.wait_ge(sumsq2_done, b + 1)
                act.activation(root1[:, b:b + 1], sumsq1[:, b:b + 1], ACT.Sqrt, scale=1.0 / D, bias=eps).then_inc(root2_done, 1)
            if b:
                c = b - 1
                for h in range(2):
                    act.wait_ge(h2T_done, 2 * c + h + 1)
                    if c >= 2:
                        act.wait_ge(logits_done, c - 1)
                    act.activation(h2T[:, c % 2, 4 * h:4 * h + 4, :], bank[:, 4 + h, :].rearrange("p (k t) -> p k t", k=4),
                                   ACT.Copy).then_inc(h2T_out, 1)
        act.wait_ge(aff_shifted, 1)
        act.activation(aff_e[:, :, :], aff_e[:, :, :], ACT.Exp).then_inc(aff_exp_done, 1)

        def hi_row(n, raw, loaded, value, j, inc=1):
            act.wait_ge(loaded[j // 2], value)
            if not (isinstance(n, int) and n < 4):
                act.wait_ge(row_used, n - 3)
            act.activation(e_hi[:, j % 4, :], raw[:, j // 2, j % 2, :], ACT.Copy).then_inc(row_hi, inc)

        def turn_hi(out, done, count, out_done):
            for h in range(2):
                act.wait_ge(done, count + (h + 1))
                act.activation(out[:, 4 * h:4 * h + 4, :], bank[:, 6 + h, :].rearrange("p (k t) -> p k t", k=4), ACT.Copy).then_inc(out_done, 1)

        def silu_of(e):
            act.activation(silu[:, :], bank[:, 0:2, :].rearrange("p a b -> p (a b)"), ACT.Silu).then_inc(silu_done, 1)

        def results(e):
            act.wait_ge(ys_free, e + 1)
            act.activation(ys[:, :], bank[:, 4:6, :].rearrange("p a b -> p (a b)"), ACT.Copy,
                           scale=gate_all[:, e:e + 1] if isinstance(e, int) else gate_all[:, bass.ds(e, 1)]).then_inc(ys_done, 1)

        def step_hi(e, parity):
            n = (e + 1) * 24
            for j in range(8):
                hi_row(n + j, raw_gate, gate_loaded, (e + 2) * 16, j)
            turn_hi(hidT_hi, hidT_done, e * 2, hidT_hi_done)
            for j in range(8):
                hi_row(n + 8 + j, raw_down, down_loaded, (e + 1) * 16, j)
                if j == 4:
                    act.wait_ge(hid_done, e + 1)
                    silu_of(e + 1)
            return n

        act.wait_ge(routed, 2)
        for h in range(2):
            act.wait_ge(outproj_done, NB)
        turn_hi(xsT_hi[:, 0, :, :], xsT_done, 0, xsT_hi_done)
        for j in range(8):
            hi_row(j, raw_gate, gate_loaded, 16, j, 9 if j == 7 else 1)
        turn_hi(xsT_hi[:, 1, :, :], xsT_done, 2, xsT_hi_done)
        for j in range(8):
            hi_row(16 + j, raw_up, up_loaded, 16, j)
            if j == 4:
                silu_of(0)

        def step_act(e, parity, more):
            n = step_hi(e, parity)
            if more:
                turn_hi(xsT_hi[:, parity, :, :], xsT_done, (e + 2) * 2, xsT_hi_done)
            for j in range(8):
                hi_row(n + 16 + j, raw_up, up_loaded, (e + 2) * 16, j)
                if j == 4:
                    results(e)
        with act.Fori(0, (E - 2) // 2) as pair:
            e = pair * 2
            step_act(e, 0, True)
            step_act(e + 1, 1, True)
        step_act(E - 2, 0, False)
        turn_hi(hidT_hi, hidT_done, 2 * (E - 1), hidT_hi_done)
        for j in range(8):
            hi_row(24 * E + j, raw_down, down_loaded, 16 * E, j)
        act.wait_ge(row_used, 24 * E + 8)
        results(E - 1)

    @block.tensor
    def _(pe):
        def product(out, l_hi, l_lo, r_hi, r_lo, first, last):
            pe.matmul(out, l_hi, r_hi, start=first, stop=False)
            pe.matmul(out, l_hi, r_lo, start=False, stop=False)
            return pe.matmul(out, l_lo, r_hi, start=False, stop=last)

        pe.wait_ge(pool_ready, 5)
        for step in steps:
            kind, arg = step[0], step[1:]
            if kind == "normalise":
                b, = arg
                pe.wait_ge(xn_ready, b + 1)
                if b >= 2:
                    pe.wait_ge(ht_lo_done, 2 * (b - 1))
                for h in range(2):
                    for k in range(4):
                        ins = pe.transpose(bank[:, 4 + 2 * (b % 2) + h, k * P:(k + 1) * P],
                                           x_norm[:, b % 2, (4 * h + k) * P:(4 * h + k + 1) * P], ident[:, :])
                    ins.then_inc(xt_done, 1)
            elif kind == "vectors":
                pe.wait_ge(vec_loaded, 5 * 16)
                pe.transpose(bank[:, 0, 0:44], vec_rows[:, :], ident[0:44, 0:44]).then_inc(vec_t, 1)
                pe.wait_ge(vec_copied, 1)
            elif kind == "project":
                g, j = arg
                what, c0, _ = GROUPS[g]
                if g == 0 and j == 0:
                    pe.wait_ge(ht_lo_done, 2 * NB)
                if j == 0:
                    pe.wait_ge(wlo_done, g + 1)
                if g:
                    pe.wait_ge(*evacuated(g - 1, j))
                wh, wl = w_hi[:, g % 2, :, :], w_lo[:, g % 2, :, :]
                if what == "qkv":
                    for i in range(2):
                        tok = slice((2 * j + i) * P, (2 * j + i + 1) * P)
                        for k in range(KC):
                            ins = product(bank[:, j, i * GW:(i + 1) * GW], hT_hi[:, k, tok], hT_lo[:, k, tok],
                                          wh[:, k, :], wl[:, k, :], k == 0, k == KC - 1)
                else:
                    ch = slice((j // 2) * P, (j // 2 + 1) * P)
                    tok = slice((j % 2) * S, (j % 2 + 1) * S)
                    for k in range(KC):
                        ins = product(bank[:, j, :], wh[:, k, ch], wl[:, k, ch], hT_hi[:, k, tok], hT_lo[:, k, tok],
                                      k == 0, k == KC - 1)
                ins.then_inc(proj_done, 1)
            elif kind == "gates":
                ct, d = arg
                pe.wait_ge(bd_lo_done, ct + 1)
                pe.wait_ge(xc_lo_done, ct + 1)
                if ct or d:
                    pe.wait_ge(sigm_done, 4 * ct + 2 * d)
                for m in range(2):
                    for s in range(SEQS):
                        tok = slice(s * S, (s + 1) * S)
                        ins = product(bank[:, 4 + 2 * m + s, :], bd_hi[:, 2 * d + m, :], bd_lo[:, 2 * d + m, :],
                                      xc_hi[:, tok], xc_lo[:, tok], True, True)
                ins.then_inc(gates_done, 1)

        def transposes(out_bank, pieces, done):
            for i, piece in enumerate(pieces):
                ins = pe.transpose(bank[:, out_bank, i * P:(i + 1) * P], piece, ident[:, :])
            ins.then_inc(done, 1)

        for kind, n in attn:
            if kind == "transpose":
                b, i = divmod(n, USES)
                pe.wait_ge(qk_lo_done, 2 * (b + 1))
                if prep_free(n) > 0:
                    pe.wait_ge(qkT_out, prep_free(n))
                if i < 2:
                    pieces = [q_pair[prep_set(b)][:, 4 * i + h, :, :].rearrange("p a d -> p (a d)") for h in range(4)]
                else:
                    pieces = [k_pair[prep_set(b)][:, g, v, :, :].rearrange("p a d -> p (a d)") for g in range(KVH) for v in range(2)]
                transposes(prep_bank(n), pieces, qkT_done)
            elif kind == "slot":
                u, t, v = n, n - T_LAG, n - V_LAG
                if u < UNITS:
                    head, qb = divmod(u, BPS)
                    s, h = divmod(head, HQ)
                    kv = h // (HQ // KVH)
                    pe.wait_ge(qkT_out, USES * BPS * (s + 1))
                    if u >= 2:
                        pe.wait_ge(exp_done, u - 1)
                    q = qT[:, s, h, qb * P:(qb + 1) * P]
                    pe.matmul(bank[:, u % 2, :], q, kT[:, s, kv, 0, :], start=True, stop=False)
                    pe.matmul(bank[:, u % 2, :], q, kT[:, s, kv, 1, :], start=False, stop=True).then_inc(scores_done, 1)
                if 0 <= t < UNITS:
                    head, kc = divmod(t, BPS)
                    pe.wait_ge(prob_done, BPS * (head + 1))
                    if t >= BPS:
                        pe.wait_ge(probT_lo_done, t - BPS + 1)
                    transposes(2 + kc, [prob[:, (BPS * head + qb) % PROB_SLOTS, kc * P:(kc + 1) * P] for qb in range(BPS)], probT_done)
                if 0 <= v < UNITS:
                    head, kc = divmod(v, BPS)
                    pair, s = head // 2, head // HQ
                    if kc == 0 and head % 2 == 0 and pair:
                        pe.wait_ge(mixA_lo_done, pair if pair < PAIRS_ONE_BANK else pair - 1)
                    pe.wait_ge(v_lo_done, BPS * (s + 1))
                    pe.wait_ge(probT_lo_done, v + 1)
                    blk, cols = BPS * s + kc, pair_cols(head)
                    product(bank[:, out_bank(pair), :], v_hi[:, blk, cols], v_lo[:, blk, cols], probT_hi[:, kc, :], probT_lo[:, kc, :],
                            head % 2 == 0 and kc == 0, head % 2 == 1 and kc == BPS - 1).then_inc(pv_done, 1)

        pe.wait_ge(mixA_lo_done, HEADS // 2)
        pe.wait_ge(mixL_lo_done, 1)
        for b in range(NB + 2):
            if b < NB:
                if b >= 2:
                    pe.wait_ge(x2_done, b - 1)
                tok = slice(b * P, (b + 1) * P)
                for k in range(KC):
                    if b == 0:
                        pe.wait_ge(wo_lo_done, k + 1)
                    hi, lo, i = (mixA_hi, mixA_lo, k) if k < ATTN_W // P else (mixL_hi, mixL_lo, k - ATTN_W // P)
                    for h in range(2):
                        cols = slice(h * 512, (h + 1) * 512)
                        ins = product(bank[:, 2 * (b % 2) + h, :], hi[:, i, tok], lo[:, i, tok], wo_hi[:, k, cols], wo_lo[:, k, cols],
                                      k == 0, k == KC - 1)
                ins.then_inc(outproj_done, 1)
            c = b - 1
            if 0 <= c < NB:
                pe.wait_ge(h2_done, c + 1)
                for h in range(2):
                    if c:
                        pe.wait_ge(h2T_out, 2 * (c - 1) + h + 1)
                    transposes(4 + h, [h2[:, c % 2, (4 * h + i) * P:(4 * h + i + 1) * P] for i in range(4)], h2T_done)
            c = b - 2
            if 0 <= c < NB:
                pe.wait_ge(h2T_out, 2 * (c + 1))
                pe.wait_ge(consts3_loaded, 2 * 16)
                for k in range(KC):
                    ins = pe.matmul(bank[:, 7, c * E:(c + 1) * E], h2T[:, c % 2, k, :], router[:, k, :], start=(k == 0), stop=(k == KC - 1))
                ins.then_inc(logits_done, 1)
        pe.wait_ge(aff_done, 1)
        for b in range(BPS):
            ins = pe.transpose(bank[0:48, 6, b * P:(b + 1) * P], aff_pad[:, b, :], ident[:, :])
        ins.then_inc(affT_done, 1)
        pe.wait_ge(stacked_done, 1)
        for i in range(2):
            ins = pe.transpose(bank[:, 5, i * E:(i + 1) * E], stacked[:, i, :], ident[0:E, 0:E])
        ins.then_inc(stackedT_done, 1)

        def rows(n, first_bank, l_hi, l_lo, between, inc_last=1):
            for j in range(8):
                if j in between:
                    between[j]()
                pe.wait_ge(row_lo, n + (j + 1))
                for h in range(2):
                    cols = slice(h * 512, (h + 1) * 512)
                    ins = product(bank[:, first_bank + h, :], l_hi[:, j, :], l_lo[:, j, :], e_hi[:, j % 4, cols], e_lo[:, j % 4, cols],
                                  j == 0, j == 7)
                ins.then_inc(row_used, inc_last if j == 7 else 1)

        def turn_tokens(loaded, parity):
            pe.wait_ge(xs_loaded[parity], loaded)
            for h in range(2):
                transposes(6 + h, [xs[:, parity, (4 * h + i) * P:(4 * h + i + 1) * P] for i in range(4)], xsT_done)

        def turn_hidden(e):
            pe.wait_ge(hid_done, e + 1)
            for h in range(2):
                transposes(6 + h, [hid[:, (4 * h + i) * P:(4 * h + i + 1) * P] for i in range(4)], hidT_done)

        pe.wait_ge(routed, 2)
        turn_tokens(16, 0)
        pe.wait_ge(xsT_lo_done, 2)
        def tokens_1():
            turn_tokens(16, 1)
        rows(0, 0, xsT_hi[:, 0, :, :], xsT_lo[:, 0, :, :], {6: tokens_1}, 9)
        rows(16, 2, xsT_hi[:, 0, :, :], xsT_lo[:, 0, :, :], {})

        def step_pe(e, parity, more):
            n = (e + 1) * 24
            other = 1 - parity
            def hidden():
                pe.wait_ge(xsT_lo_done, e * 2 + 4)
                turn_hidden(e)
            def tokens():
                turn_tokens(tokens_at(e, parity), parity)
            pe.wait_ge(xsT_lo_done, e * 2 + 4)
            pe.wait_ge(silu_done, e + 1)
            rows(n, 0, xsT_hi[:, other, :, :], xsT_lo[:, other, :, :], {6: hidden})
            pe.wait_ge(hidT_lo_done, e * 2 + 2)
            if not (isinstance(e, int) and e == 0):
                pe.wait_ge(ys_done, e)
            rows(n + 8, 4, hidT_hi, hidT_lo, {4: tokens} if more else {})
            rows(n + 16, 2, xsT_hi[:, other, :, :], xsT_lo[:, other, :, :], {})

        def tokens_at(e, parity):
            return (e - parity) * 8 + 32

        with pe.Fori(0, (E - 2) // 2) as pair:
            e = pair * 2
            step_pe(e, 0, True)
            step_pe(e + 1, 1, True)
        step_pe(E - 2, 0, False)
        turn_hidden(E - 1)
        pe.wait_ge(hidT_lo_done, 2 * E)
        pe.wait_ge(ys_done, E - 1)
        rows(24 * E, 4, hidT_hi, hidT_lo, {})

    @block.vector
    def _(dve):
        own = [0]

        def link(ins):
            own[0] += 1
            ins.then_inc(dve_step, 1)
            dve.wait_ge(dve_step, own[0])

        dve.wait_ge(g1_loaded, 16)
        for half in range(SEQS):
            cols = slice(half * BPS, (half + 1) * BPS)
            dve.wait_ge(root_ready, half + 1)
            dve.reciprocal(rstd1[:, cols], root1[:, cols]).then_inc(rstd_ready, 1)
        dve.wait_ge(rstd_ready, SEQS)
        for step in steps:
            kind, arg = step[0], step[1:]
            if kind == "normalise":
                b, = arg
                if b >= 2:
                    dve.wait_ge(xt_done, 2 * (b - 1))
                dve.scalar_tensor_tensor(out=x_norm[:, b % 2, :], in0=x_nat[:, b, :], scalar=rstd1[:, b:b + 1],
                                         in1=g1b[:, :], op0=ALU.mult, op1=ALU.mult).then_inc(xn_ready, 1)
                for bb in ([b - 1] if b else []) + ([b] if b == NB - 1 else []):
                    for h in range(2):
                        dve.wait_ge(ht_hi_done, 2 * bb + h + 1)
                        out = hT_lo[:, 4 * h:4 * h + 4, bb * P:(bb + 1) * P]
                        dve.tensor_tensor(out, bank[:, 4 + 2 * (bb % 2) + h, :].rearrange("p (k t) -> p k t", k=4),
                                          hT_hi[:, 4 * h:4 * h + 4, bb * P:(bb + 1) * P].bitcast(F32),
                                          ALU.subtract).then_inc(ht_lo_done, 1)
            elif kind == "split_w":
                g, = arg
                dve.wait_ge(whi_done, g + 1)
                dve.tensor_tensor(w_lo[:, g % 2, :, :], w_raw[:, :, :], w_hi[:, g % 2, :, :].bitcast(F32),
                                  ALU.subtract).then_inc(wlo_done, 1)
            elif kind == "vectors":
                dve.wait_ge(vec_t, 1)
                dve.tensor_copy(vecs[:, :], bank[:, 0, 0:44]).then_inc(vec_copied, 1)
                dve.wait_ge(vec_copied, 1)
                lam = vecs[:, V_LAM:V_LAM + 2 * CT]
                link(dve.tensor_scalar(sp_neg, lam, -1.0, None, ALU.mult))
                link(dve.tensor_tensor(sp_abs, lam, sp_neg, ALU.max))
                dve.tensor_scalar(sp_pos, sp_neg, 0.0, None, ALU.max)
                dve.wait_ge(sp_exp_done, 1)
                link(dve.tensor_scalar(sp_den, sp_exp, 2.0, None, ALU.add))
                link(dve.reciprocal(sp_z, sp_den))
                link(dve.tensor_tensor(sp_z, sp_z, sp_exp, ALU.mult))
                link(dve.tensor_tensor(sp_z2, sp_z, sp_z, ALU.mult))
                link(dve.tensor_scalar(sp_p, sp_z2, 1.0 / 17, None, ALU.mult))
                for n in range(15, 1, -2):
                    link(dve.scalar_tensor_tensor(out=sp_p, in0=sp_p, scalar=1.0 / n, in1=sp_z2, op0=ALU.add, op1=ALU.mult))
                link(dve.scalar_tensor_tensor(out=sp_p, in0=sp_p, scalar=1.0, in1=sp_z, op0=ALU.add, op1=ALU.mult))
                link(dve.scalar_tensor_tensor(out=sp_p, in0=sp_p, scalar=2.0, in1=sp_pos, op0=ALU.mult, op1=ALU.add))
                dve.tensor_scalar(lru_c, sp_p, LRU_C, None, ALU.mult)
                dve.tensor_scalar(neg_c, sp_p, -LRU_C, None, ALU.mult)
                dve.tensor_scalar(neg_2c, sp_p, -2 * LRU_C, None, ALU.mult).then_inc(lru_c_done, 1)
            elif kind == "empty":
                g, j = arg
                what, c0, _ = GROUPS[g]
                if what == "xr":
                    dve.wait_ge(proj_done, JOBS * g + j + 1)
                    dve.tensor_copy(xr_pad[:, c0 + j // 2, j % 2, CONV_LEFT:CONV_LEFT + S], bank[:, j, :]).then_inc(xr_out, 1)
            elif kind == "conv":
                ct, = arg
                xcs = xc[:, :].rearrange("p (s t) -> p s t", s=SEQS)
                taps = [xr_pad[:, ct, :, i:i + S] for i in range(TAPS)]
                w = [vecs[:, V_CONVW + CT * i + ct:V_CONVW + CT * i + ct + 1] for i in range(TAPS)]
                dve.wait_ge(xr_out, 2 * ct + 2)
                link(dve.tensor_scalar(xcs, taps[0], w[0], vecs[:, V_CONVB + ct:V_CONVB + ct + 1], ALU.mult, ALU.add))
                for i in range(1, TAPS):
                    ins = dve.scalar_tensor_tensor(out=xcs, in0=taps[i], scalar=w[i], in1=xcs, op0=ALU.mult, op1=ALU.add)
                    if i < TAPS - 1:
                        link(ins)
                ins.then_inc(xc_done, 1)
                dve.wait_ge(bd_hi_done, ct + 1)
                dve.tensor_tensor(bd_lo[:, :, :], bd_raw[:, :, :], bd_hi[:, :, :].bitcast(F32), ALU.subtract).then_inc(bd_lo_done, 1)
                dve.wait_ge(xc_hi_done, ct + 1)
                dve.tensor_tensor(xc_lo[:, :], xc[:, :], xc_hi[:, :].bitcast(F32), ALU.subtract).then_inc(xc_lo_done, 1)
            elif kind == "decay":
                ct, = arg
                for d in range(2):
                    dve.wait_ge(sigm_done, 4 * ct + 2 * d + 2)
                    link(dve.tensor_tensor(ib[d][:, :], ib[d][:, :], xc[:, :], ALU.mult))
                for d in range(2):
                    dve.wait_ge(tanh_done, 2 * ct + d + 1)
                    dve.scalar_tensor_tensor(out=mult[d][:, :], in0=mult[d][:, :], scalar=1.0, in1=rt[d][:, :],
                                             op0=ALU.add, op1=ALU.mult).then_inc(mult2_done, 1)
            elif kind == "scan":
                ct, = arg
                for d in range(2):
                    dve.wait_ge(root_done, 2 * ct + d + 1)
                    link(dve.tensor_tensor(ib[d][:, :], ib[d][:, :], mult[d][:, :], ALU.mult))
                    for s in range(SEQS):
                        a, b, h = (v[:, s * S:(s + 1) * S] for v in (decay[d], ib[d], rt[d]))
                        if d:
                            a, b, h = (v[d][:, (s + 1) * S - 1:s * S - 1 if s else None:-1] for v in (decay, ib, rt))
                        ins = dve.tensor_tensor_scan(h, a, b, 0.0, ALU.mult, ALU.add)
                    link(ins)
                link(dve.tensor_tensor(rt[0][:, :], rt[0][:, :], rt[1][:, :], ALU.add))
                dve.wait_ge(gate_out, 2 * ct + 2)
                dve.tensor_tensor(lru_out[:, ct, :], lru_out[:, ct, :], rt[0][:, :], ALU.mult).then_inc(scan_done, 1)

        def newton(rstd, mean_sq, tmp):
            link(dve.tensor_tensor(tmp, rstd, rstd, ALU.mult))
            link(dve.tensor_tensor(tmp, tmp, mean_sq, ALU.mult))
            link(dve.tensor_scalar(tmp, tmp, -0.5, 1.5, ALU.mult, ALU.add))
            return dve.tensor_tensor(rstd, rstd, tmp, ALU.mult)

        dve.wait_ge(proj_done, NG * JOBS)
        quarter = HD // 4
        dve.wait_ge(tabs_done, 13)
        dve.wait_ge(gates_done, 2 * CT)
        for kind, n in attn:
            if kind == "sum":
                dve.wait_ge(qk_sq_done, n + 1)
                sq = qk_sq[:, n, :] if n < BPS else qk_sq1[:, :]
                dve.tensor_reduce(qk_stat[:, 0, n * NH:(n + 1) * NH], sq.rearrange("p (h d) -> p h d", h=NH), AX_X, ALU.add).then_inc(qk_sum_done, 1)
            elif kind == "rstd":
                cols = slice(n * BPS * NH, (n + 1) * BPS * NH)
                dve.wait_ge(qk_sum_done, (n + 1) * BPS)
                dve.tensor_scalar(qk_stat[:, 1, cols], qk_stat[:, 0, cols], 1.0 / HD, EPS, ALU.mult, ALU.add)
                dve.wait_ge(qk_root_done, n + 1)
                link(dve.reciprocal(qk_stat[:, 3, cols], qk_stat[:, 2, cols]))
                newton(qk_stat[:, 3, cols], qk_stat[:, 1, cols], qk_stat[:, 2, cols]).then_inc(qk_rstd_done, 1)
                dve.wait_ge(qk_rstd_done, n + 1)
            elif kind == "turn":
                b = n
                if prep_before(b) > 0:
                    dve.wait_ge(summed_done, prep_before(b))
                for i, (c0, h) in enumerate(((0, HQ), (ATTN_W, KVH))):
                    for a in range(2):
                        src = qkv[:, b, c0:c0 + h * HD].rearrange("p (h a o d) -> p h a o d", h=h, a=2, o=2)[:, :, a, ::-1, :]
                        out = swapped[prep_set(b)][:, c0:c0 + h * HD].rearrange("p (h a o d) -> p h a o d", h=h, a=2, o=2)[:, :, a, :, :]
                        sin = tab[:, 2 * i + 1, b % BPS:b % BPS + 1, a * 2 * quarter:(a + 1) * 2 * quarter].rearrange(
                            "p b (o d) -> p b o d", o=2).to_broadcast([P, h, 2, quarter])
                        ins = dve.tensor_tensor(out, src, sin, ALU.mult)
                ins.then_inc(swapped_done, 1)
                dve.wait_ge(v_hi_done, b + 1)
                v_at = lambda v: v[:, b, HD:HD + 2 * HD * KVH].rearrange("p (g w) -> p g w", g=KVH)[:, :, 0:HD]
                dve.tensor_tensor(v_at(v_lo), qkv[:, b, QK:QKV].rearrange("p (g w) -> p g w", g=KVH), v_at(v_hi).bitcast(F32),
                                  ALU.subtract).then_inc(v_lo_done, 1)
            elif kind == "norm":
                b = n
                dve.wait_ge(summed_done, b + 1)
                qn = qk_norm[prep_set(b)][:, :].rearrange("p (h d) -> p h d", h=NH)
                dve.tensor_tensor(qn, qn, qk_stat[:, 3, b * NH:(b + 1) * NH].unsqueeze(2).to_broadcast([P, NH, HD]),
                                  ALU.mult).then_inc(qk_norm_done, 1)
            elif kind == "lo":
                b, i = n, prep_set(n)
                qn = qk_norm[i][:, :].rearrange("p (h d) -> p h d", h=NH)
                dve.wait_ge(qk_norm_done, b + 1)
                dve.wait_ge(qk_hi_done, b + 1)
                dve.tensor_tensor(q_pair[i][:, :, 1, :].bitcast(F32R), qn[:, 0:HQ, :], q_pair[i][:, :, 0, :], ALU.subtract).then_inc(qk_lo_done, 1)
                for copy in range(2):
                    ins = dve.tensor_tensor(k_pair[i][:, :, 1, copy, :].bitcast(F32R), qn[:, HQ:NH, :], k_pair[i][:, :, 0, 0, :], ALU.subtract)
                ins.then_inc(qk_lo_done, 1)
            elif kind == "slot":
                u, t, v = n, n - T_LAG, n - V_LAG - 1
                if u < UNITS:
                    dve.wait_ge(scores_done, u + 1)
                    dve.tensor_reduce(row_stat[:, 0, u:u + 1], bank[:, u % 2, :], AX_X, ALU.max, negate=True).then_inc(max_done, 1)
                if v >= 0 and v % (2 * BPS) == 2 * BPS - 1:
                    pair = v // (2 * BPS)
                    head = 2 * pair
                    dve.wait_ge(mixA_hi_done, pair + 1)
                    where = (slice(None), head % HQ // 2, slice(head // HQ * S, (head // HQ + 1) * S))
                    dve.tensor_tensor(mixA_lo[where], bank[:, out_bank(pair), :], mixA_hi[where].bitcast(F32), ALU.subtract).then_inc(mixA_lo_done, 1)
                if 0 <= u - 1 < UNITS:
                    dve.wait_ge(exp_done, u)
                    dve.reciprocal(row_stat[:, 2, u - 1:u], row_stat[:, 1, u - 1:u]).then_inc(recip_done, 1)
                if 0 <= t < UNITS:
                    dve.wait_ge(probT_hi_done, t + 1)
                    dve.tensor_tensor(probT_lo[:, t % BPS, :], bank[:, 2 + t % BPS, :], probT_hi[:, t % BPS, :].bitcast(F32),
                                      ALU.subtract).then_inc(probT_lo_done, 1)

        dve.wait_ge(mixL_hi_done, 1)
        dve.tensor_tensor(mixL_lo[:, :, :], lru_out[:, :, :], mixL_hi[:, :, :].bitcast(F32), ALU.subtract).then_inc(mixL_lo_done, 1)
        for k in range(KC):
            dve.wait_ge(wo_hi_done, k + 1)
            dve.tensor_tensor(wo_lo[:, k, :], wo_raw[:, k % 2, :], wo_hi[:, k, :].bitcast(F32), ALU.subtract).then_inc(wo_lo_done, 1)
        for b in range(NB):
            dve.wait_ge(outproj_done, b + 1)
            dve.wait_ge(xa_loaded[b % 2], 16 * (b // 2 + 1))
            if b >= 2:
                dve.wait_ge(x2_stored[b % 2], 16 * (b // 2))
            dve.tensor_tensor(x2[:, b % 2, :], bank[:, 2 * (b % 2):2 * (b % 2) + 2, :].rearrange("p a b -> p (a b)"),
                              x_again[:, b % 2, :], ALU.add).then_inc(x2_done, 1)
            dve.wait_ge(sumsq2_done, b + 1)
            r, v, t = rstd1[:, b:b + 1], small[:, 120:121], small[:, 121:122]
            link(dve.tensor_scalar(v, sumsq1[:, b:b + 1], 1.0 / D, EPS, ALU.mult, ALU.add))
            dve.wait_ge(root2_done, b + 1)
            link(dve.reciprocal(r, root1[:, b:b + 1]))
            link(newton(r, v, t))
            if b == 0:
                dve.wait_ge(consts3_loaded, 2 * 16)
            dve.scalar_tensor_tensor(out=h2[:, b % 2, :], in0=x2[:, b % 2, :], scalar=r, in1=g2b[:, :],
                                     op0=ALU.mult, op1=ALU.mult).then_inc(h2_done, 1)
        logits = bank[:, 7, 0:NB * E].rearrange("p (b e) -> p b e", b=NB)
        spread = lambda v: v.unsqueeze(2).to_broadcast([P, NB, E])
        dve.wait_ge(logits_done, NB)
        link(dve.tensor_reduce(aff_stat[:, 0, :], logits, AX_X, ALU.max))
        dve.tensor_tensor(aff_e[:, :, :], logits, spread(aff_stat[:, 0, :]), ALU.subtract).then_inc(aff_shifted, 1)
        dve.wait_ge(aff_exp_done, 1)
        link(dve.tensor_reduce(aff_stat[:, 1, :], aff_e[:, :, :], AX_X, ALU.add))
        link(dve.reciprocal(aff_stat[:, 2, :], aff_stat[:, 1, :]))
        dve.wait_ge(pad_zeroed, 1)
        for s in range(SEQS):
            blocks = slice(s * BPS, (s + 1) * BPS)
            ins = dve.tensor_tensor(aff_pad[:, :, 32 * s:32 * s + E], aff_e[:, blocks, :],
                                    spread(aff_stat[:, 2, :])[:, blocks, :], ALU.mult)
        ins.then_inc(aff_done, 1)
        dve.wait_ge(affT_done, 1)
        dve.wait_ge(outproj_done, NB)
        link(dve.tensor_copy(aff_work[:, 0, :], bank[0:48, 6, :]))
        for r in range(CAP // 8):
            now, then = aff_work[:, r % 2, :], aff_work[:, (r + 1) % 2, :]
            eight = slice(8 * r, 8 * r + 8)
            link(dve.max(top_val[:, eight], now))
            link(dve.max_index(top_idx[:, eight], top_val[:, eight], now))
            if r < CAP // 8 - 1:
                link(dve.match_replace(then, top_val[:, eight], now, -1.0))
        link(dve.tensor_copy(stacked[:, 0, 0:CAP], top_idx[0:E, :]))
        dve.tensor_scalar(stacked[:, 0, CAP:P], top_idx[32:32 + E, :], float(S), None, ALU.add)
        dve.tensor_copy(stacked[:, 1, 0:CAP], top_val[0:E, :])
        dve.tensor_copy(stacked[:, 1, CAP:P], top_val[32:32 + E, :]).then_inc(stacked_done, 1)
        dve.wait_ge(stackedT_done, 1)
        dve.tensor_copy(idx_all[:, :], bank[:, 5, 0:E]).then_inc(routed, 1)
        dve.tensor_copy(gate_all[:, :], bank[:, 5, E:2 * E]).then_inc(routed, 1)

        def lo_row(n, raw, j, inc=1):
            dve.wait_ge(row_hi, n + (j + 1))
            dve.tensor_tensor(e_lo[:, j % 4, :], raw[:, j // 2, j % 2, :], e_hi[:, j % 4, :].bitcast(F32), ALU.subtract).then_inc(row_lo, inc)

        def turn_lo(out, hi, hi_done, count, done):
            for h in range(2):
                dve.wait_ge(hi_done, count + (h + 1))
                dve.tensor_tensor(out[:, 4 * h:4 * h + 4, :], bank[:, 6 + h, :].rearrange("p (k t) -> p k t", k=4),
                                  hi[:, 4 * h:4 * h + 4, :].bitcast(F32), ALU.subtract).then_inc(done, 1)

        def hidden(e):
            dve.wait_ge(row_used, e * 24 + 24)
            dve.wait_ge(silu_done, e + 1)
            dve.tensor_tensor(hid[:, :], bank[:, 2:4, :].rearrange("p a b -> p (a b)"), silu[:, :], ALU.mult).then_inc(hid_done, 1)

        turn_lo(xsT_lo[:, 0, :, :], xsT_hi[:, 0, :, :], xsT_hi_done, 0, xsT_lo_done)
        for j in range(8):
            lo_row(0, raw_gate, j, 9 if j == 7 else 1)
        turn_lo(xsT_lo[:, 1, :, :], xsT_hi[:, 1, :, :], xsT_hi_done, 2, xsT_lo_done)
        for j in range(8):
            lo_row(16, raw_up, j)

        def step_dve(e, parity, more):
            n = (e + 1) * 24
            for j in range(8):
                lo_row(n, raw_gate, j)
                if j == 3:
                    hidden(e)
            turn_lo(hidT_lo, hidT_hi, hidT_hi_done, e * 2, hidT_lo_done)
            for j in range(8):
                lo_row(n + 8, raw_down, j)
            if more:
                turn_lo(xsT_lo[:, parity, :, :], xsT_hi[:, parity, :, :], xsT_hi_done, (e + 2) * 2, xsT_lo_done)
            for j in range(8):
                lo_row(n + 16, raw_up, j)
        with dve.Fori(0, (E - 2) // 2) as pair:
            e = pair * 2
            step_dve(e, 0, True)
            step_dve(e + 1, 1, True)
        step_dve(E - 2, 0, False)
        hidden(E - 1)
        turn_lo(hidT_lo, hidT_hi, hidT_hi_done, 2 * (E - 1), hidT_lo_done)
        for j in range(8):
            lo_row(24 * E, raw_down, j)

    ctx.close()


_INS = ["x_prompt", "x_sample", "norm1_g", "w_in", "q_norm_g", "k_norm_g", "conv_w", "conv_b", "lru_w_r", "lru_b_r",
        "lru_w_i", "lru_b_i", "lru_lambda", "w_out", "norm2_g", "router_w", "exp_w_gate", "exp_w_up", "exp_w_down"]


def rope_tables(S, head_dim):
    import numpy as np
    pos = np.arange(S)
    axis_dim = head_dim // 2
    inv_freq = (np.float32(ROPE_THETA) ** (-np.arange(0, axis_dim, 2, dtype=np.float32) / np.float32(axis_dim))).astype(np.float32)
    row = (pos // GRID_W).astype(np.float32)[:, None] * inv_freq
    col = (pos % GRID_W).astype(np.float32)[:, None] * inv_freq
    cos = np.concatenate([np.cos(row), np.cos(row), np.cos(col), np.cos(col)], axis=1).astype(np.float32)
    sin = np.concatenate([-np.sin(row), np.sin(row), -np.sin(col), np.sin(col)], axis=1).astype(np.float32)
    return cos, sin


def kernel(**inputs):
    import numpy as np
    import concourse.bacc as bacc
    from concourse.bass_utils import run_bass_kernel_spmd

    nc = bacc.Bacc("TRN2", target_bir_lowering=False, num_devices=1)
    arrays, args = {}, []
    S, D = inputs["x_prompt"].shape[1:]
    cos, sin = rope_tables(S, inputs["q_norm_g"].shape[1])
    given = {name: np.ascontiguousarray(inputs[name]) for name in _INS} | {"rope_cos": cos, "rope_sin": sin}
    for name, a in given.items():
        arrays[f"in_{name}_dram"] = a
        args.append(nc.dram_tensor(f"in_{name}_dram", a.shape, mybir.dt.from_np(a.dtype), kind="ExternalInput").ap())
    args.append(nc.dram_tensor("y_dram", (SEQS * S, D), F32, kind="ExternalOutput").ap())
    layer_program(nc, *args)
    y = run_bass_kernel_spmd(nc, [arrays], core_ids=[0]).results[0]["y_dram"].reshape(SEQS, 1, S, D)
    return y[0], y[1]
```

```python
from contextlib import ExitStack

import concourse.bass as bass
from concourse import mybir

F32 = mybir.dt.float32
F32R = mybir.dt.float32r
U32 = mybir.dt.uint32
ALU = mybir.AluOpType
ACT = mybir.ActivationFunctionType
AX_X = mybir.AxisListType.X

P = 128
SEQS = 2
GRID_W = 64
ROPE_THETA = 10000.0
EPS = 1e-6
LRU_C = 8.0
CONV_LEFT = 2


def layer_program(nc, x0, x1, norm1_g, w_in, q_norm_g, k_norm_g, conv_w, conv_b, lru_w_r, lru_b_r,
                  lru_w_i, lru_b_i, lru_lambda, w_out, norm2_g, router_w, w_gate, w_up, w_down,
                  rope_cos, rope_sin, y):
    S, D = x0.shape[1], x0.shape[2]
    T = SEQS * S
    NB = T // P
    BPS = S // P
    KC = D // P
    HD = q_norm_g.shape[1]
    LRU_W = lru_lambda.shape[2]
    CT = LRU_W // P
    ATTN_W = D - LRU_W
    HQ = ATTN_W // HD
    KV_W = (w_in.shape[2] - ATTN_W - 2 * LRU_W) // 2
    QKV = ATTN_W + 2 * KV_W
    TAPS = conv_w.shape[1]
    BD = lru_w_r.shape[3]
    KVH = KV_W // HD
    E = router_w.shape[2]
    CAP = 2 * S // E
    assert SEQS * CAP == P and HD * 2 == P
    h2_rows = nc.dram_tensor("h2_rows", (T, D), F32, kind="Internal").ap()

    GW = 256
    XR0, GATE0 = QKV, QKV + LRU_W
    GROUPS = [("xr", 0, XR0), ("xr", 2, XR0 + GW), ("qkv", 2 * GW, 2 * GW), ("qkv", 0, 0), ("qkv", GW, GW),
              ("gate", 0, GATE0), ("gate", 2, GATE0 + GW)]
    NG = len(GROUPS)
    GATE_G = NG - 2
    JOBS = 4

    ctx = ExitStack()
    sem = lambda name: ctx.enter_context(nc.semaphore(name))

    base = -(-nc.sbuf_base // 64) * 64
    K = 1024

    def at(name, offset, shape, dt):
        return nc.alloc_sbuf_tensor_at(name, shape, dt, offset=base + offset)

    ident = at("ident", 0, [P, P], F32)
    small = at("small", 512, [P, 256], F32)
    vec_rows = at("vec_rows", 1536, [44, P], F32)
    vecs = at("vecs", 2048, [P, 44], F32)
    SM = 2560
    eps = small[:, 0:1]
    sumsq1 = small[:, 8:16]
    root1 = small[:, 16:24]
    rstd1 = small[:, 24:32]
    sp_neg, sp_abs, sp_exp, sp_den, sp_z, sp_z2, sp_p, sp_pos = (small[:, 32 + 8 * i:40 + 8 * i] for i in range(8))
    lru_c, neg_c, neg_2c = (small[:, 96 + 8 * i:104 + 8 * i] for i in range(3))
    V_CONVW, V_CONVB, V_BR, V_BI, V_LAM = 0, 16, 20, 28, 36

    lru_out = at("lru_out", SM, [P, CT, T], F32)
    qkv = at("qkv", SM + 16 * K, [P, NB, QKV], F32)
    R1 = SM + 40 * K
    hT_hi = at("hT_hi", R1, [P, KC, T], F32R)
    hT_lo = at("hT_lo", R1 + 32 * K, [P, KC, T], F32R)
    w_raw = at("w_raw", R1 + 64 * K, [P, KC, GW], F32)
    w_hi = at("w_hi", R1 + 72 * K, [P, 2, KC, GW], F32R)
    w_lo = at("w_lo", R1 + 88 * K, [P, 2, KC, GW], F32R)
    XP = S + TAPS - 1
    xr_pad = at("xr_pad", R1 + 104 * K, [P, CT, SEQS, XP], F32)
    R2 = R1 + 104 * K + 16480
    bd_raw = at("bd_raw", R2, [P, 4, P], F32)
    bd_hi = at("bd_hi", R2 + 2 * K, [P, 4, P], F32R)
    bd_lo = at("bd_lo", R2 + 4 * K, [P, 4, P], F32R)
    R3 = R2 + 6 * K
    xc = at("xc", R3, [P, T], F32)
    rt = [at(f"rt{d}", R3 + (4 + 16 * d) * K, [P, T], F32) for d in range(2)]
    ib = [at(f"ib{d}", R3 + (8 + 16 * d) * K, [P, T], F32) for d in range(2)]
    decay = [at(f"decay{d}", R3 + (12 + 16 * d) * K, [P, T], F32) for d in range(2)]
    mult = [at(f"mult{d}", R3 + (16 + 16 * d) * K, [P, T], F32) for d in range(2)]
    xc_hi = at("xc_hi", SM + 12 * K, [P, T], F32R)
    xc_lo = [at(f"xc_lo{ct}", SM + 8 * K if ct < CT - 1 else R1 + 113 * K, [P, T], F32R) for ct in range(CT)]
    x_nat = at("x_nat", R3, [P, NB, D], F32)
    g1b = at("g1b", SM + 16 * K, [P, D], F32)
    x_norm = at("x_norm", SM + 20 * K, [P, 2, D], F32)
    junk = at("junk", SM + 28 * K, [P, D], F32)

    mixA_hi = at("mixA_hi", R1, [P, ATTN_W // P, T], F32R)
    mixA_lo = at("mixA_lo", R1 + 16 * K, [P, ATTN_W // P, T], F32R)
    qT = at("qT", R1 + 32 * K, [P, SEQS, HQ, S], F32R)
    kT = at("kT", R1 + 64 * K, [P, SEQS, KVH, 2, S], F32R)
    VW = (2 * KVH + 1) * HD
    v_hi = at("v_hi", R1 + 80 * K, [P, NB, VW], F32R)
    v_lo = at("v_lo", R1 + 90 * K, [P, NB, VW], F32R)
    QK = ATTN_W + KV_W
    NH = HQ + KVH
    R4 = R1 + 100 * K
    cos_sin = at("cos_sin", R4 + 4 * K, [P, 2, BPS, HD], F32)
    tab = at("tab", R4 + 6 * K, [P, 4, BPS, HD], F32)
    gains = at("gains", R4 + 10 * K, [P, 4, HD], F32)
    qk_stat = at("qk_stat", R4 + 11 * K, [P, 4, NB * NH], F32)
    PROB_SLOTS = 10
    R6 = R1 + 126 * K + 512
    prob = at("prob", R6, [P, PROB_SLOTS, S], F32)
    probT_hi = at("probT_hi", R6 + 20 * K, [P, BPS, S], F32R)
    probT_lo = at("probT_lo", R6 + 28 * K, [P, BPS, S], F32R)
    row_stat = at("row_stat", R6 + 36 * K, [P, 3, SEQS * HQ * BPS], F32)
    gate_now = at("gate_now", R6, [P, 2, S], F32)
    qk_sq = at("qk_sq", R1 + 120 * K + 512, [P, 2, QK], F32)
    sets = [R4 + 12 * K + 512, R6 + 4 * K]
    turned = [at(f"turned{i}", o, [P, QK], F32) for i, o in enumerate(sets)]
    swapped = [at(f"swapped{i}", o + 2560, [P, QK], F32) for i, o in enumerate(sets)]
    pairs = [R6 + 12 * K + 6 * K * i for i in range(BPS)] + [R1 + 120 * K + 512]
    q_pair = [at(f"q_pair{i}", o, [P, HQ, 2, HD], F32) for i, o in enumerate(pairs)]
    k_pair = [at(f"k_pair{i}", o + 4 * K, [P, KVH, 2, 2, HD], F32) for i, o in enumerate(pairs)]
    assert R6 + 36 * K + 768 <= nc.sbuf_usable_end - base
    assert QK * 4 == 2560 and VW * NB * 4 == 10 * K

    QUIET = R1 + 48 * K
    h2T = at("h2T", QUIET, [P, 2, KC, P], F32)
    g2b = at("g2b", QUIET + 8 * K, [P, D], F32)
    router = at("router", QUIET + 12 * K, [P, KC, E], F32)
    R5 = QUIET + 12 * K + 512
    aff_e = at("aff_e", R5, [P, NB, E], F32)
    aff_pad = at("aff_pad", R5 + 512, [P, BPS, 48], F32)
    aff_stat = at("aff_stat", R5 + 512 + 768, [P, 3, NB], F32)
    mixL_hi = at("mixL_hi", R1 + 32 * K, [P, CT, T], F32R)
    mixL_lo = at("mixL_lo", SM, [P, CT, T], F32R)
    wo_at = [SM + 16 * K + 8 * K * k for k in range(3)] + [R1 + 102 * K + 8 * K * k for k in range(3)] + [
        R1 + 64 * K + 8 * K * k for k in range(2)]
    wo_hi = [at(f"wo_hi{k}", o, [P, D], F32R) for k, o in enumerate(wo_at)]
    wo_lo = [at(f"wo_lo{k}", o + 4 * K, [P, D], F32R) for k, o in enumerate(wo_at)]
    wo_raw = [at(f"wo_raw{k}", o + 4 * K, [P, D], F32) for k, o in enumerate(wo_at)]
    x_again = at("x_again", R1 + 80 * K, [P, D], F32)
    x2 = at("x2", R1 + 84 * K, [P, 2, D], F32)
    h2 = at("h2", R1 + 92 * K, [P, 2, D], F32)
    aff_work = at("aff_work", R1, [48, 2, S], F32)
    top_val = at("top_val", R1 + 4 * K, [48, CAP], F32)
    top_idx = at("top_idx", R1 + 4 * K + 256, [48, CAP], U32)
    stacked = at("stacked", R1 + 4 * K + 512, [E, 2, P], F32)
    idx_all = at("idx_all", SM - 256, [P, E], U32)
    gate_all = at("gate_all", SM - 128, [P, E], F32)

    RAW0 = nc.sbuf_usable_end - base - 32 * K
    RAW0 -= RAW0 % 64
    raw_gate = at("raw_gate", RAW0, [P, 4, 2, D], F32)
    raw_down = at("raw_down", R1 + 64 * K, [P, 4, 2, D], F32)
    raw_up = at("raw_up", R1 + 96 * K, [P, 4, 2, D], F32)
    SPLIT = 6
    e_hi = at("e_hi", R1 + 8 * K, [P, SPLIT, D], F32R)
    e_lo = at("e_lo", R1 + 32 * K, [P, SPLIT, D], F32R)
    xs = at("xs", R1 + 56 * K, [P, 2, D], F32)
    xsT_hi = at("xsT_hi", SM, [P, 2, KC, P], F32R)
    xsT_lo = at("xsT_lo", SM + 8 * K, [P, 2, KC, P], F32R)
    silu = at("silu", SM + 16 * K, [P, D], F32)
    hid = at("hid", SM + 20 * K, [P, D], F32)
    hidT_hi = at("hidT_hi", SM + 24 * K, [P, KC, P], F32R)
    hidT_lo = at("hidT_lo", SM + 28 * K, [P, KC, P], F32R)
    ys = at("ys", SM + 32 * K, [P, D], F32)
    idx_now = at("idx_now", SM + 36 * K, [P, 4], U32)
    assert RAW0 >= R1 + 128 * K

    assert R3 + 36 * K <= nc.sbuf_usable_end - base, (R3 + 36 * K, nc.sbuf_usable_end - base)

    bank = nc.alloc_psum_tensor("bank", [P, 8, 512], F32)

    x_loaded = [sem(f"x_loaded{b}") for b in range(NB)]
    g1_loaded, vec_loaded = sem("g1_loaded"), sem("vec_loaded")
    pool_ready, ident_zeroed = sem("pool_ready"), sem("ident_zeroed")
    sumsq_ready, root_ready, rstd_ready = sem("sumsq_ready"), sem("root_ready"), sem("rstd_ready")
    xn_ready, xt_done, ht_hi_done, ht_lo_done = sem("xn_ready"), sem("xt_done"), sem("ht_hi_done"), sem("ht_lo_done")
    wraw_loaded, whi_done, wlo_done = sem("wraw_loaded"), sem("whi_done"), sem("wlo_done")
    proj_done = sem("proj_done")
    xr_out, gate_out, qkv_out = sem("xr_out"), sem("gate_out"), sem("qkv_out")
    vec_t, vec_copied = sem("vec_t"), sem("vec_copied")
    dve_step, sp_exp_done, lru_c_done = sem("dve_step"), sem("sp_exp_done"), sem("lru_c_done")
    bd_loaded, bd_hi_done, bd_lo_done = sem("bd_loaded"), sem("bd_hi_done"), sem("bd_lo_done")
    xc_done, xc_hi_done, xc_lo_done = sem("xc_done"), sem("xc_hi_done"), sem("xc_lo_done")
    gates_done, sigm_done, gated = sem("gates_done"), sem("sigm_done"), sem("gated")
    exps_done, tanh_done, mult2_done, root_done, scan_done = (
        sem("exps_done"), sem("tanh_done"), sem("mult2_done"), sem("root_done"), sem("scan_done"))
    sp_abs_done = sem("sp_abs_done")
    tabs_loaded, tabs_done, v_zeroed = sem("tabs_loaded"), sem("tabs_done"), sem("v_zeroed")
    qk_sq_done, qk_sum_done, qk_root_done, qk_rstd_done = (
        sem("qk_sq_done"), sem("qk_sum_done"), sem("qk_root_done"), sem("qk_rstd_done"))
    turned_done, swapped_done, qk_norm_done = sem("turned_done"), sem("swapped_done"), sem("qk_norm_done")
    qk_hi_done, qk_lo_done, v_hi_done, v_lo_done = sem("qk_hi_done"), sem("qk_lo_done"), sem("v_hi_done"), sem("v_lo_done")
    qkT_done, qkT_out = sem("qkT_done"), sem("qkT_out")
    scores_done, max_done, exp_done, recip_done, prob_done = (
        sem("scores_done"), sem("max_done"), sem("exp_done"), sem("recip_done"), sem("prob_done"))
    probT_done, probT_hi_done, probT_lo_done = sem("probT_done"), sem("probT_hi_done"), sem("probT_lo_done")
    pv_done, mixA_hi_done, mixA_lo_done = sem("pv_done"), sem("mixA_hi_done"), sem("mixA_lo_done")
    consts3_loaded, mixL_hi_done, mixL_lo_done = sem("consts3_loaded"), sem("mixL_hi_done"), sem("mixL_lo_done")
    wo_loaded = [sem(f"wo_loaded{k}") for k in range(KC)]
    wo_hi_done, wo_lo_done = sem("wo_hi_done"), sem("wo_lo_done")
    xa_loaded = sem("xa_loaded")
    outproj_done, x2_done, sumsq2_done, root2_done, h2_done = (
        sem("outproj_done"), sem("x2_done"), sem("sumsq2_done"), sem("root2_done"), sem("h2_done"))
    x2_stored = [sem(f"x2_stored{i}") for i in range(2)]
    h2_stored = [sem(f"h2_stored{i}") for i in range(2)]
    h2T_done, h2T_out, logits_done = sem("h2T_done"), sem("h2T_out"), sem("logits_done")
    aff_shifted, aff_exp_done, aff_done, affT_done = sem("aff_shifted"), sem("aff_exp_done"), sem("aff_done"), sem("affT_done")
    stacked_done, stackedT_done, routed = sem("stacked_done"), sem("stackedT_done"), sem("routed")
    pad_zeroed = sem("pad_zeroed")
    gate_loaded = [sem(f"gate_loaded{i}") for i in range(4)]
    down_loaded = [sem(f"down_loaded{i}") for i in range(4)]
    up_loaded = [sem(f"up_loaded{i}") for i in range(4)]
    row_hi, row_lo, row_used = sem("row_hi"), sem("row_lo"), sem("row_used")
    idx_copied, xs_loaded, xsT_done, xsT_hi_done, xsT_lo_done = (
        sem("idx_copied"), [sem(f"xs_loaded{i}") for i in range(2)], sem("xsT_done"), sem("xsT_hi_done"), sem("xsT_lo_done"))
    silu_done, hid_done, hidT_done, hidT_hi_done, hidT_lo_done = (
        sem("silu_done"), sem("hid_done"), sem("hidT_done"), sem("hidT_hi_done"), sem("hidT_lo_done"))
    ys_done, scattered, ys_free = sem("ys_done"), sem("scattered"), sem("ys_free")
    gather_ready, scatter_ready = sem("gather_ready"), sem("scatter_ready")

    SEMS_OF = {"xr": xr_out, "gate": gate_out, "qkv": qkv_out}

    def evacuated(g, j):
        kind = GROUPS[g][0]
        before = sum(GROUPS[i][0] == kind for i in range(g))
        return SEMS_OF[kind], JOBS * before + j + 1

    steps = [("sum_squares", 0)]
    for b in range(NB + 1):
        steps.append(("normalise", b))
        if b == BPS - 2:
            steps.append(("w_hi", 0))
        if b == BPS - 1:
            steps += [("w_lo", 0), ("vectors",)]
        if b in (BPS - 1, BPS + 1):
            steps.append(("project", 0, (b - BPS + 1) // 2))
    steps.append(("softplus",))
    BESIDE_JOB = {}
    for ct in range(CT):
        c = 3 + 4 * ct
        for n, step in ((c + 1, ("gates", ct, 0)), (c + 2, ("gates", ct, 1)), (c + 3, ("decay", ct)),
                        (c + 3, ("conv", ct + 1)), (c + 4, ("scan", ct))):
            if step != ("conv", CT):
                BESIDE_JOB.setdefault(n, []).append(step)
    BESIDE_JOB.setdefault(3, []).append(("conv", 0))
    PREPARE = ("square", "sum", "rstd", "turn", "norm", "hi", "lo")
    PREP_FROM = 4 + 4 * CT
    for b in range(NB):
        BESIDE_JOB.setdefault(PREP_FROM + b // 3, []).append(("square", b))
    for b in range(NB):
        BESIDE_JOB.setdefault(PREP_FROM + b // 3, []).append(("sum", b))
    BESIDE_JOB[PREP_FROM + 2].append(("rstd",))
    for i in range(NB + 1):
        n = PREP_FROM + 3 + i // 2
        if i < NB:
            BESIDE_JOB.setdefault(n, []).append(("turn", i))
        if i:
            b = i - 1
            BESIDE_JOB.setdefault(n, []).append(("norm", b))
            if b < BPS:
                BESIDE_JOB[n].append(("hi", b))
        if 2 <= i <= BPS + 1:
            BESIDE_JOB.setdefault(n, []).append(("lo", i - 2))
    for n in range(NG * JOBS):
        g, j = divmod(n, JOBS)
        if n >= 2:
            steps.append(("project", g, j))
        beside_job = BESIDE_JOB.pop(n, [])
        steps += [step for step in beside_job if step[0] == "scan"]
        if n:
            steps.append(("empty", (n - 1) // JOBS, (n - 1) % JOBS))
        if j == 0 and g + 1 < NG:
            steps += [("w_hi", g + 1), ("w_lo", g + 1)]
        steps += [step for step in beside_job if step[0] != "scan"]
    steps.append(("empty", NG - 1, JOBS - 1))
    for n in sorted(BESIDE_JOB):
        steps += BESIDE_JOB[n]

    HEADS = SEQS * HQ
    UNITS = HEADS * BPS
    T_LAG, V_LAG = 6, 8
    USES = 3
    attn = [(stage, n) for n in range(USES * BPS) for stage in ("transpose", "out")]
    beside = {5: [("v", 0)]}
    for i in range(BPS):
        b = BPS + i
        first = 3 + 7 * i
        beside.setdefault(first, []).append(("hi", b))
        beside.setdefault(first + 1, []).append(("lo", b))
        for j in range(USES):
            beside.setdefault(first + 2 + 2 * j, []).append(("transpose", USES * b + j))
            beside.setdefault(first + 3 + 2 * j, []).append(("out", USES * b + j))
    WO_EARLY = 6
    SPLIT_FROM = UNITS // 2 + 2
    for n in range(2 * (WO_EARLY + CT)):
        at_slot = SPLIT_FROM + ((7 * n + 1) // 3 if n < 2 * WO_EARLY else 3 * (n - 2 * WO_EARLY) + 1)
        beside.setdefault(at_slot, []).append(("split_hi", n))
        beside.setdefault(at_slot + 2, []).append(("split_lo", n))
    for u in range(UNITS + V_LAG + 2):
        attn.append(("slot", u))
        attn += beside.get(u, [])
        k = u - (UNITS + 2)
        if 0 <= k < WO_EARLY:
            attn.append(("project_out", k))

    def pair_set(b):
        return min(b, BPS)

    def prep_bank(n):
        return 4 + n % 4 if n < USES * BPS else 7

    def prep_free(n):
        return n - 3 if n < USES * BPS else n

    PAIRS_ONE_BANK = 3

    def out_bank(pair):
        return 6 if pair < PAIRS_ONE_BANK or pair % 2 == 0 else 7

    def pair_cols(head):
        kv = head % HQ // (HQ // KVH)
        first = 2 * HD * kv + (HD if head % 2 == 0 else 0)
        return slice(first, first + 2 * HD)

    def v_of(v):
        return v[:, :, HD:HD + 2 * HD * KVH].rearrange("p b (g w) -> p b g w", g=KVH)[:, :, :, 0:HD]

    def v_in(qkv):
        return qkv[:, :, QK:QKV].rearrange("p b (g w) -> p b g w", g=KVH)

    block = ctx.enter_context(nc.Block())

    @block.sync
    def _(sp):
        rows = [(0, conv_w[0].rearrange("t (c p) -> (t c) p", p=P)), (16, conv_b[0].rearrange("(c p) -> c p", p=P)),
                (20, lru_b_r[0].rearrange("d (c p) -> (d c) p", p=P)), (28, lru_b_i[0].rearrange("d (c p) -> (d c) p", p=P)),
                (36, lru_lambda[0].rearrange("d (c p) -> (d c) p", p=P))]
        def load_bd(ct):
            for d in range(2):
                for m, w in enumerate((lru_w_r, lru_w_i)):
                    for n in range(P // BD):
                        sp.dma_start(bd_raw[n * BD:(n + 1) * BD, 2 * d + m, n * BD:(n + 1) * BD],
                                      w[0, d, ct * (P // BD) + n, :, :]).then_inc(bd_loaded, 16)

        def load_w(g):
            col = GROUPS[g][2]
            sp.dma_start(w_raw[:, :, :], w_in[0, :, col:col + GW].rearrange("(k p) n -> p k n", p=P)).then_inc(wraw_loaded, 16)

        for b in range(NB):
            src = (x0 if b < BPS else x1)[0, (b % BPS) * P:(b % BPS + 1) * P, :]
            sp.dma_start(x_nat[:, b, :], src).then_inc(x_loaded[b], 16)
            if b == 0:
                sp.dma_start(g1b[:, :], norm1_g[0:1, :].to_broadcast([P, D])).then_inc(g1_loaded, 16)
            if b == 1:
                for at_row, rows_in in rows:
                    sp.dma_start(vec_rows[at_row:at_row + rows_in.shape[0], :], rows_in).then_inc(vec_loaded, 16)
            if b == BPS - 2:
                load_w(0)
        sp.wait_ge(pool_ready, 5)
        load_bd(0)
        for g in range(1, NG):
            sp.wait_ge(wlo_done, g)
            load_w(g)
            if 1 <= g - 1 < CT:
                sp.wait_ge(bd_lo_done, g - 1)
                load_bd(g - 1)

        sp.wait_ge(xc_done, CT)
        sp.dma_start(cos_sin[:, 0, :, :], rope_cos.rearrange("(b p) d -> p b d", p=P)).then_inc(tabs_loaded, 16)
        sp.dma_start(cos_sin[:, 1, :, :], rope_sin.rearrange("(b p) d -> p b d", p=P)).then_inc(tabs_loaded, 16)
        for i, g in enumerate((q_norm_g, k_norm_g)):
            sp.dma_start(gains[:, 2 * i, :], g[0:1, :].to_broadcast([P, HD])).then_inc(tabs_loaded, 16)

        def load_wo(k):
            sp.dma_start(wo_raw[k][:, :], w_out[0, k * P:(k + 1) * P, :]).then_inc(wo_loaded[k], 16)

        sp.wait_ge(qk_lo_done, 2 * NB)
        sp.wait_ge(v_lo_done, 1)
        for k in range(3):
            load_wo(k)
        sp.wait_ge(qkT_done, USES * NB)
        for k in range(3, WO_EARLY):
            load_wo(k)
        sp.wait_ge(scores_done, UNITS)
        for k in range(WO_EARLY, KC):
            load_wo(k)
        sp.dma_start(g2b[:, :], norm2_g[0:1, :].to_broadcast([P, D])).then_inc(consts3_loaded, 16)
        sp.dma_start(router[:, :, :], router_w[0].rearrange("(k p) e -> p k e", p=P)).then_inc(consts3_loaded, 16)
        sp.wait_ge(pv_done, UNITS)

        def load(raw, i, w, e, loaded):
            sp.dma_start(raw[:, i, :, :], w[0, e, 2 * i * P:2 * (i + 1) * P, :].rearrange("(r p) n -> p r n", p=P)
                         if isinstance(e, int) else
                         w[0, bass.ds(e, 1), 2 * i * P:2 * (i + 1) * P, :].rearrange("o (r p) n -> p (o r) n", p=P)).then_inc(loaded[i], 16)

        for b in range(NB):
            if b:
                sp.wait_ge(x2_done, b)
            sp.dma_start(x_again[:, :], (x0 if b < BPS else x1)[0, (b % BPS) * P:(b % BPS + 1) * P, :]).then_inc(xa_loaded, 16)
            if b == 0:
                for i in range(4):
                    load(raw_gate, i, w_gate, 0, gate_loaded)
            if b:
                c = b - 1
                sp.dma_start(y[c * P:(c + 1) * P, :], x2[:, c % 2, :]).then_inc(x2_stored[c % 2], 16)
                sp.wait_ge(h2_done, c + 1)
                sp.dma_start(h2_rows[c * P:(c + 1) * P, :], h2[:, c % 2, :]).then_inc(h2_stored[c % 2], 16)
        sp.wait_ge(outproj_done, NB)
        for i in range(1, 4):
            load(raw_up, i, w_up, 0, up_loaded)
        for i in range(2):
            load(raw_down, i, w_down, 0, down_loaded)
        sp.wait_ge(x2_done, NB)
        sp.dma_start(y[(NB - 1) * P:NB * P, :], x2[:, (NB - 1) % 2, :]).then_inc(x2_stored[(NB - 1) % 2], 16)
        sp.wait_ge(h2_done, NB)
        sp.dma_start(h2_rows[(NB - 1) * P:NB * P, :], h2[:, (NB - 1) % 2, :]).then_inc(h2_stored[(NB - 1) % 2], 16)

        for i in range(2):
            sp.wait_ge(x2_stored[i], 16 * (NB // 2))
            sp.wait_ge(h2_stored[i], 16 * (NB // 2))
        sp.wait_ge(h2T_done, 2 * NB)
        load(raw_up, 0, w_up, 0, up_loaded)
        for i in range(2, 4):
            load(raw_down, i, w_down, 0, down_loaded)

        def step_loads(e, first=False):
            for i in range(4):
                if first and i == 2:
                    for p in range(2):
                        sp.wait_ge(xs_loaded[p], 16)
                sp.wait_ge(row_lo, e * 24 + (2 * i + 2))
                load(raw_gate, i, w_gate, e + 1, gate_loaded)
            for i in range(0 if first else 4):
                sp.wait_ge(row_lo, e * 24 + (8 + 2 * i + 2))
                load(raw_down, i, w_down, e, down_loaded)
            for i in range(4):
                sp.wait_ge(row_lo, e * 24 + (16 + 2 * i + 2))
                load(raw_up, i, w_up, e + 1, up_loaded)
        step_loads(0, True)
        with sp.Fori(1, E - 1) as e:
            step_loads(e)
        for i in range(4):
            sp.wait_ge(row_lo, (E - 1) * 24 + 8 + 2 * i + 2)
            load(raw_down, i, w_down, E - 1, down_loaded)

    @block.gpsimd
    def _(pool):
        pool.memset(ident[:, :], 0.0).then_inc(ident_zeroed, 1)
        pool.memset(eps, EPS).then_inc(pool_ready, 1)
        pool.memset(bd_raw[:, :, :], 0.0).then_inc(pool_ready, 1)
        pool.memset(xr_pad[:, :, :, 0:CONV_LEFT], 0.0).then_inc(pool_ready, 1)
        pool.memset(xr_pad[:, :, :, CONV_LEFT + S:XP], 0.0).then_inc(pool_ready, 1)
        pool.wait_ge(ident_zeroed, 1)
        pool.affine_select(out=ident[:, :], in_=ident[:, :], compare_op=ALU.not_equal, fill=1.0, base=0,
                           pattern=[[-1, P]], channel_multiplier=1).then_inc(pool_ready, 1)

        pool.wait_ge(tabs_loaded, 4 * 16)
        quarter = HD // 4
        for i in range(2):
            for a in range(4):
                o = a ^ 1
                pool.tensor_copy(gains[:, 2 * i + 1, a * quarter:(a + 1) * quarter],
                                 gains[:, 2 * i, o * quarter:(o + 1) * quarter]).then_inc(tabs_done, 1)
        pool.wait_ge(tabs_done, 8)
        for i in range(2):
            for j in range(2):
                pool.tensor_tensor(tab[:, 2 * i + j, :, :], cos_sin[:, j, :, :],
                                   gains[:, 2 * i + j:2 * i + j + 1, :].to_broadcast([P, BPS, HD]), ALU.mult).then_inc(tabs_done, 1)
        pool.wait_ge(tabs_done, 12)
        pool.tensor_scalar(tab[:, 0:2, :, :], tab[:, 0:2, :, :], HD ** -0.5, 1.0, ALU.mult, ALU.mult).then_inc(tabs_done, 1)
        pool.wait_ge(tabs_done, 13)
        for step in steps:
            kind, arg = step[0], step[1:]
            if kind == "turn":
                b, = arg
                if b == 0:
                    pool.wait_ge(qkv_out, 3 * JOBS)
                    pool.wait_ge(gates_done, 2 * CT)
                if b == 1:
                    pool.wait_ge(scan_done, CT)
                if b >= 2:
                    pool.wait_ge(qk_norm_done, b - 1)
                for i, (c0, h) in enumerate(((0, HQ), (ATTN_W, KVH))):
                    pool.tensor_tensor(turned[b % 2][:, c0:c0 + h * HD].rearrange("p (h d) -> p h d", h=h),
                                       qkv[:, b, c0:c0 + h * HD].rearrange("p (h d) -> p h d", h=h),
                                       tab[:, 2 * i, b % BPS:b % BPS + 1, :].to_broadcast([P, h, HD]), ALU.mult).then_inc(turned_done, 1)
            elif kind == "empty" and GROUPS[arg[0]][0] == "gate":
                g, j = arg
                n = JOBS * (g - GATE_G) + j
                pool.wait_ge(gate_out, n + 1)
                out = lru_out[:, GROUPS[g][1] + j % 2, (j // 2) * S:(j // 2 + 1) * S]
                pool.tensor_tensor(out, out, gate_now[:, n % 2, :], ALU.mult).then_inc(gated, 1)

        pool.wait_ge(proj_done, NG * JOBS)
        for v in (v_hi, v_lo):
            pool.memset(v[:, :, :].bitcast(F32).rearrange("p b (g d) -> p b g d", d=HD)[:, :, 0::2, :], 0.0).then_inc(v_zeroed, 1)
        for kind, n in attn:
            if kind == "split_lo" and n >= 2 * WO_EARLY:
                i, cols = (n - 2 * WO_EARLY) // 2, slice(n % 2 * S, (n % 2 + 1) * S)
                pool.wait_ge(mixL_hi_done, n - 2 * WO_EARLY + 1)
                pool.tensor_tensor(mixL_lo[:, i, cols], lru_out[:, i, cols], mixL_hi[:, i, cols].bitcast(F32), ALU.subtract).then_inc(mixL_lo_done, 1)
            elif kind == "slot" and 0 <= n - 1 < UNITS:
                u = n - 1
                pool.wait_ge(recip_done, u + 1)
                pool.tensor_scalar(prob[:, u % PROB_SLOTS, :], prob[:, u % PROB_SLOTS, :], row_stat[:, 2, u:u + 1], 1.0,
                                   ALU.mult, ALU.mult).then_inc(prob_done, 1)

        pool.wait_ge(scores_done, UNITS)
        pool.memset(aff_pad[:, :, :], 0.0).then_inc(pad_zeroed, 1)

        pool.wait_ge(outproj_done, NB)
        for j in range(SPLIT):
            pool.wait_ge(row_hi, j + 1)
            pool.tensor_tensor(e_lo[:, j, :], raw_gate[:, j // 2, j % 2, :], e_hi[:, j, :].bitcast(F32), ALU.subtract).then_inc(row_lo, 1)
        pool.wait_ge(routed, 2)
        for i in range(2):
            pool.wait_ge(h2_stored[i], 16 * (NB // 2))
            pool.wait_ge(x2_stored[i], 16 * (NB // 2))
        for e in range(4):
            p = e % 2
            if e >= 2:
                pool.wait_ge(xsT_done, 2 * (e - 1))
            pool.tensor_copy(idx_now[:, p:p + 1], idx_all[:, e:e + 1]).then_inc(idx_copied, 1)
            pool.wait_ge(idx_copied, e + 1)
            pool.sem_inc(gather_ready, 1)
            pool.indirect_dma_start(xs[:, p, :], None, h2_rows, bass.IndirectOffsetOnAxis(ap=idx_now[:, p:p + 1], axis=0)).then_inc(xs_loaded[p], 16)

        def scatter_step(e, copied):
            pool.tensor_copy(idx_now[:, 2:3], idx_all[:, bass.ds(e, 1)] if not isinstance(e, int) else idx_all[:, e:e + 1]).then_inc(idx_copied, 1)
            pool.wait_ge(idx_copied, copied)
            pool.wait_ge(ys_done, e + 2)
            pool.sem_inc(scatter_ready, 1)
            pool.indirect_dma_start(y, bass.IndirectOffsetOnAxis(ap=idx_now[:, 2:3], axis=0), ys[:, :], None, compute_op=ALU.add).then_inc(scattered, 16)
            pool.wait_ge(scattered, e * 16 + 16)
            pool.sem_inc(ys_free, 1)

        pool.sem_inc(ys_free, 1)
        with pool.Fori(0, (E - 4) // 2) as pair:
            e = pair * 2
            for parity in range(2):
                pool.wait_ge(xsT_done, e * 2 + (2 * parity + 6))
                pool.tensor_copy(idx_now[:, parity:parity + 1], idx_all[:, bass.ds(e + (parity + 4), 1)]).then_inc(idx_copied, 1)
                pool.wait_ge(idx_copied, e * 2 + (5 + 2 * parity))
                pool.sem_inc(gather_ready, 1)
                pool.indirect_dma_start(xs[:, parity, :], None, h2_rows,
                                        bass.IndirectOffsetOnAxis(ap=idx_now[:, parity:parity + 1], axis=0)).then_inc(xs_loaded[parity], 16)
                scatter_step(e + parity, e * 2 + (6 + 2 * parity))
        for e in range(E - 4, E):
            scatter_step(e, 4 + 2 * (E - 4) + e - (E - 4) + 1)

    @block.scalar
    def _(act):
        def prepare(kind, n=0):
            if kind == "square":
                if n == 0:
                    act.wait_ge(qkv_out, 3 * JOBS)
                    act.wait_ge(gates_done, 2 * CT)
                if n >= 2:
                    act.wait_ge(qk_sum_done, n - 1)
                act.activation(qk_sq[:, n % 2, :], qkv[:, n, 0:QK], ACT.Square).then_inc(qk_sq_done, 1)
            elif kind == "rstd":
                act.wait_ge(qk_sum_done, NB)
                act.activation(qk_stat[:, 2, :], qk_stat[:, 0, :], ACT.Sqrt, scale=1.0 / HD, bias=eps).then_inc(qk_root_done, 1)
            elif kind == "hi":
                i = pair_set(n)
                act.wait_ge(qk_norm_done, n + 1)
                if n > BPS:
                    act.wait_ge(qkT_done, USES * n)
                act.activation(q_pair[i][:, :, 0, :].bitcast(F32R), qkv[:, n, 0:ATTN_W].rearrange("p (h d) -> p h d", h=HQ), ACT.Copy)
                for copy in range(2):
                    ins = act.activation(k_pair[i][:, :, 0, copy, :].bitcast(F32R),
                                         qkv[:, n, ATTN_W:QK].rearrange("p (h d) -> p h d", h=KVH), ACT.Copy)
                ins.then_inc(qk_hi_done, 1)

        act.wait_ge(pool_ready, 1)
        act.activation(small[:, 122:123], eps, ACT.Sqrt)
        for step in steps:
            kind, arg = step[0], step[1:]
            if kind in ("sum_squares", "normalise"):
                b = arg[0] + (kind == "normalise")
                if b < NB:
                    act.wait_ge(x_loaded[b], 16)
                    act.activation(junk[:, :], x_nat[:, b, :], ACT.Square, accum_out=sumsq1[:, b:b + 1]).then_inc(sumsq_ready, 1)
                    act.wait_ge(sumsq_ready, b + 1)
                    act.activation(root1[:, b:b + 1], sumsq1[:, b:b + 1], ACT.Sqrt, scale=1.0 / D, bias=eps).then_inc(root_ready, 1)
                if b >= 2:
                    b -= 2
                    for h in range(2):
                        act.wait_ge(xt_done, 2 * b + h + 1)
                        act.activation(hT_hi[:, 4 * h:4 * h + 4, b * P:(b + 1) * P],
                                       bank[:, 4 + 2 * (b % 2) + h, :].rearrange("p (k t) -> p k t", k=4), ACT.Copy).then_inc(ht_hi_done, 1)
            elif kind == "w_hi":
                g, = arg
                act.wait_ge(wraw_loaded, 16 * (g + 1))
                if g >= 2:
                    act.wait_ge(proj_done, JOBS * (g - 1))
                act.activation(w_hi[:, g % 2, :, :], w_raw[:, :, :], ACT.Copy).then_inc(whi_done, 1)
            elif kind == "softplus":
                act.wait_ge(sp_abs_done, 1)
                act.activation(sp_exp, sp_abs, ACT.Exp, scale=-1.0).then_inc(sp_exp_done, 1)
            elif kind == "empty":
                g, j = arg
                what, c0, _ = GROUPS[g]
                if what == "gate":
                    n = JOBS * (g - GATE_G) + j
                    act.wait_ge(scan_done, CT)
                    if n >= 2:
                        act.wait_ge(gated, n - 1)
                    act.wait_ge(proj_done, JOBS * g + j + 1)
                    act.activation(gate_now[:, n % 2, :], bank[:, j, :], ACT.Gelu_apprx_tanh).then_inc(gate_out, 1)
                elif what == "qkv":
                    act.wait_ge(proj_done, JOBS * g + j + 1)
                    act.activation(qkv[:, 2 * j:2 * j + 2, c0:c0 + GW],
                                   bank[:, j, :].rearrange("p (b n) -> p b n", b=2), ACT.Copy).then_inc(qkv_out, 1)
            elif kind == "conv":
                ct, = arg
                act.wait_ge(bd_loaded, 8 * 16 * (ct + 1))
                if ct:
                    act.wait_ge(gates_done, 2 * ct)
                act.activation(bd_hi[:, :, :], bd_raw[:, :, :], ACT.Copy).then_inc(bd_hi_done, 1)
                act.wait_ge(xc_done, ct + 1)
                act.activation(xc_hi[:, :], xc[:, :], ACT.Copy).then_inc(xc_hi_done, 1)
            elif kind == "gates":
                ct, d = arg
                act.wait_ge(gates_done, 2 * ct + d + 1)
                if ct:
                    act.wait_ge(mult2_done, 2 * (ct - 1) + d + 1)
                act.activation(rt[d][:, :], bank[:, 4:6, :].rearrange("p a b -> p (a b)"), ACT.Sigmoid,
                               bias=vecs[:, V_BR + CT * d + ct:V_BR + CT * d + ct + 1]).then_inc(sigm_done, 1)
                if ct:
                    act.wait_ge(scan_done, ct)
                act.activation(ib[d][:, :], bank[:, 6:8, :].rearrange("p a b -> p (a b)"), ACT.Sigmoid,
                               bias=vecs[:, V_BI + CT * d + ct:V_BI + CT * d + ct + 1]).then_inc(sigm_done, 1)
            elif kind == "decay":
                ct, = arg
                act.wait_ge(sigm_done, 4 * ct + 4)
                act.wait_ge(gates_done, 2 * ct + 2)
                act.wait_ge(lru_c_done, 1)
                for d in range(2):
                    c = CT * d + ct
                    act.activation(decay[d][:, :], rt[d][:, :], ACT.Exp, scale=neg_c[:, c:c + 1])
                    act.activation(mult[d][:, :], rt[d][:, :], ACT.Exp, scale=neg_2c[:, c:c + 1]).then_inc(exps_done, 1)
                    act.wait_ge(exps_done, 2 * ct + d + 1)
                    act.activation(rt[d][:, :], rt[d][:, :], ACT.Tanh, scale=lru_c[:, c:c + 1]).then_inc(tanh_done, 1)
            elif kind == "scan":
                ct, = arg
                for d in range(2):
                    act.wait_ge(mult2_done, 2 * ct + d + 1)
                    act.activation(mult[d][:, :], mult[d][:, :], ACT.Sqrt).then_inc(root_done, 1)
            elif kind in PREPARE:
                prepare(kind, *arg)

        def split_wo_hi(k, half):
            cols = slice(half * D // 2, (half + 1) * D // 2)
            act.wait_ge(wo_loaded[k], 16)
            act.activation(wo_hi[k][:, cols], wo_raw[k][:, cols], ACT.Copy).then_inc(wo_hi_done, 1)

        act.wait_ge(scan_done, CT)
        for kind, n in attn:
            if kind == "hi":
                prepare(kind, n)
            elif kind == "v":
                act.wait_ge(proj_done, NG * JOBS)
                act.activation(v_of(v_hi), v_in(qkv), ACT.Copy).then_inc(v_hi_done, 1)
            elif kind == "out":
                b, i = divmod(n, USES)
                s, tok = b // BPS, slice((b % BPS) * P, (b % BPS + 1) * P)
                act.wait_ge(qkT_done, n + 1)
                out = qT[:, s, 4 * i:4 * i + 4, tok] if i < 2 else kT[:, s, :, :, tok].rearrange("p g v t -> p (g v) t")
                act.activation(out, bank[:, prep_bank(n), :].rearrange("p (h t) -> p h t", h=4), ACT.Copy).then_inc(qkT_out, 1)
            elif kind == "split_hi":
                if n < 2 * WO_EARLY:
                    split_wo_hi(n // 2, n % 2)
                else:
                    i, cols = (n - 2 * WO_EARLY) // 2, slice(n % 2 * S, (n % 2 + 1) * S)
                    act.wait_ge(scores_done, BPS * HQ)
                    act.wait_ge(gated, SEQS * CT)
                    act.activation(mixL_hi[:, i, cols], lru_out[:, i, cols], ACT.Copy).then_inc(mixL_hi_done, 1)
            elif kind == "slot":
                u, t, v = n, n - T_LAG, n - V_LAG - 1
                if v >= 0 and v % (2 * BPS) == 2 * BPS - 1:
                    pair = v // (2 * BPS)
                    head = 2 * pair
                    act.wait_ge(pv_done, v + 1)
                    act.activation(mixA_hi[:, head % HQ // 2, head // HQ * S:(head // HQ + 1) * S], bank[:, out_bank(pair), :],
                                   ACT.Copy).then_inc(mixA_hi_done, 1)
                if 0 <= t < UNITS:
                    act.wait_ge(probT_done, t + 1)
                    if t >= BPS:
                        act.wait_ge(pv_done, t - BPS + 1)
                    act.activation(probT_hi[:, t % BPS, :], bank[:, 2 + t % BPS, :], ACT.Copy).then_inc(probT_hi_done, 1)
                if u < UNITS:
                    if u == 0:
                        act.wait_ge(gated, SEQS * CT)
                    act.wait_ge(max_done, u + 1)
                    if u >= PROB_SLOTS:
                        act.wait_ge(probT_done, BPS * ((u - PROB_SLOTS) // BPS + 1))
                    act.activation(prob[:, u % PROB_SLOTS, :], bank[:, u % 2, :], ACT.Exp, bias=row_stat[:, 0, u:u + 1],
                                   accum_out=row_stat[:, 1, u:u + 1]).then_inc(exp_done, 1)

        for k in range(WO_EARLY, KC):
            for half in range(2):
                split_wo_hi(k, half)
        for b in range(NB + 1):
            if b < NB:
                act.wait_ge(x2_done, b + 1)
                if b:
                    act.wait_ge(h2_done, b)
                if b >= 2:
                    act.wait_ge(h2_stored[b % 2], 16 * (b // 2))
                    act.wait_ge(h2T_done, 2 * (b - 1))
                act.activation(h2[:, b % 2, :], x2[:, b % 2, :], ACT.Square, accum_out=sumsq1[:, b:b + 1]).then_inc(sumsq2_done, 1)
                act.wait_ge(sumsq2_done, b + 1)
                act.activation(root1[:, b:b + 1], sumsq1[:, b:b + 1], ACT.Sqrt, scale=1.0 / D, bias=eps).then_inc(root2_done, 1)
            if b:
                c = b - 1
                for h in range(2):
                    act.wait_ge(h2T_done, 2 * c + h + 1)
                    if c >= 2:
                        act.wait_ge(logits_done, c - 1)
                    act.activation(h2T[:, c % 2, 4 * h:4 * h + 4, :], bank[:, 4 + h, :].rearrange("p (k t) -> p k t", k=4),
                                   ACT.Copy).then_inc(h2T_out, 1)
        act.wait_ge(aff_shifted, 1)
        act.activation(aff_e[:, :, :], aff_e[:, :, :], ACT.Exp).then_inc(aff_exp_done, 1)

        def hi_row(first, m, raw, loaded, value, j, inc=1):
            row, back = first + (8 * m + j), 8 * m + j - (SPLIT - 1)
            act.wait_ge(loaded[j // 2], value)
            if isinstance(row, int) and 16 <= row < 19:
                act.wait_ge(row_used, row - 11)
            elif not isinstance(row, int) or row >= SPLIT:
                act.wait_ge(row_used, first + back if back >= 0 else first - -back)
            act.activation(e_hi[:, (8 * m + j) % SPLIT, :], raw[:, j // 2, j % 2, :], ACT.Copy).then_inc(row_hi, inc)

        def turn_hi(out, done, count, out_done):
            for h in range(2):
                act.wait_ge(done, count + (h + 1))
                act.activation(out[:, 4 * h:4 * h + 4, :], bank[:, 6 + h, :].rearrange("p (k t) -> p k t", k=4), ACT.Copy).then_inc(out_done, 1)

        def silu_of(e, used):
            act.wait_ge(row_used, used)
            act.activation(silu[:, :], bank[:, 0:2, :].rearrange("p a b -> p (a b)"), ACT.Silu).then_inc(silu_done, 1)

        def results(e):
            act.wait_ge(ys_free, e + 1)
            act.activation(ys[:, :], bank[:, 4:6, :].rearrange("p a b -> p (a b)"), ACT.Copy,
                           scale=gate_all[:, e:e + 1] if isinstance(e, int) else gate_all[:, bass.ds(e, 1)]).then_inc(ys_done, 1)

        def step_hi(e, parity):
            n = (e + 1) * 24
            for j in range(8):
                hi_row(n, 0, raw_gate, gate_loaded, (e + 2) * 16, j)
            turn_hi(hidT_hi, hidT_done, e * 2, hidT_hi_done)
            for j in range(8):
                hi_row(n, 1, raw_down, down_loaded, (e + 1) * 16, j)
                if j == 5:
                    act.wait_ge(hid_done, e + 1)
                    silu_of(e + 1, n + 8)
            return n

        act.sem_inc(ys_done, 1)
        act.wait_ge(outproj_done, NB)
        for j in range(SPLIT):
            hi_row(0, 0, raw_gate, gate_loaded, 16, j)
        turn_hi(xsT_hi[:, 0, :, :], xsT_done, 0, xsT_hi_done)
        for j in range(SPLIT, 8):
            hi_row(0, 0, raw_gate, gate_loaded, 16, j, 9 if j == 7 else 1)
        turn_hi(xsT_hi[:, 1, :, :], xsT_done, 2, xsT_hi_done)
        for j in range(8):
            hi_row(0, 2, raw_up, up_loaded, 16, j)
            if j == 4:
                silu_of(0, 16)

        def step_act(e, parity, more):
            n = step_hi(e, parity)
            if more:
                turn_hi(xsT_hi[:, parity, :, :], xsT_done, (e + 2) * 2, xsT_hi_done)
            for j in range(8):
                hi_row(n, 2, raw_up, up_loaded, (e + 2) * 16, j)
                if j == 5:
                    act.wait_ge(row_used, n + 16)
                    results(e)
        with act.Fori(0, (E - 2) // 2) as pair:
            e = pair * 2
            step_act(e, 0, True)
            step_act(e + 1, 1, True)
        step_act(E - 2, 0, False)
        for j in range(2):
            hi_row(24 * E, 0, raw_down, down_loaded, 16 * E, j)
        turn_hi(hidT_hi, hidT_done, 2 * (E - 1), hidT_hi_done)
        for j in range(2, 8):
            hi_row(24 * E, 0, raw_down, down_loaded, 16 * E, j)
        act.wait_ge(row_used, 24 * E + 8)
        results(E - 1)

    @block.tensor
    def _(pe):
        def product(out, l_hi, l_lo, r_hi, r_lo, first, last):
            pe.matmul(out, l_hi, r_hi, start=first, stop=False)
            pe.matmul(out, l_hi, r_lo, start=False, stop=False)
            return pe.matmul(out, l_lo, r_hi, start=False, stop=last)

        pe.wait_ge(pool_ready, 5)
        for step in steps:
            kind, arg = step[0], step[1:]
            if kind == "normalise":
                b, = arg
                if b == NB:
                    continue
                pe.wait_ge(xn_ready, b + 1)
                if b >= 2:
                    pe.wait_ge(ht_lo_done, 2 * (b - 1))
                for h in range(2):
                    for k in range(4):
                        ins = pe.transpose(bank[:, 4 + 2 * (b % 2) + h, k * P:(k + 1) * P],
                                           x_norm[:, b % 2, (4 * h + k) * P:(4 * h + k + 1) * P], ident[:, :])
                    ins.then_inc(xt_done, 1)
            elif kind == "vectors":
                pe.wait_ge(vec_loaded, 5 * 16)
                pe.transpose(bank[:, 0, 0:44], vec_rows[:, :], ident[0:44, 0:44]).then_inc(vec_t, 1)
                pe.wait_ge(vec_copied, 1)
            elif kind == "project":
                g, j = arg
                what, c0, _ = GROUPS[g]
                if g == 0 and j % 2 == 0:
                    pe.wait_ge(ht_lo_done, BPS * (j + 2))
                if j == 0:
                    pe.wait_ge(wlo_done, g + 1)
                if g:
                    pe.wait_ge(*evacuated(g - 1, j))
                wh, wl = w_hi[:, g % 2, :, :], w_lo[:, g % 2, :, :]
                if what == "qkv":
                    for i in range(2):
                        tok = slice((2 * j + i) * P, (2 * j + i + 1) * P)
                        for k in range(KC):
                            ins = product(bank[:, j, i * GW:(i + 1) * GW], hT_hi[:, k, tok], hT_lo[:, k, tok],
                                          wh[:, k, :], wl[:, k, :], k == 0, k == KC - 1)
                else:
                    ch = slice((j % 2) * P, (j % 2 + 1) * P)
                    tok = slice((j // 2) * S, (j // 2 + 1) * S)
                    for k in range(KC):
                        ins = product(bank[:, j, :], wh[:, k, ch], wl[:, k, ch], hT_hi[:, k, tok], hT_lo[:, k, tok],
                                      k == 0, k == KC - 1)
                ins.then_inc(proj_done, 1)
            elif kind == "gates":
                ct, d = arg
                pe.wait_ge(bd_lo_done, ct + 1)
                pe.wait_ge(xc_lo_done, ct + 1)
                if ct or d:
                    pe.wait_ge(sigm_done, 4 * ct + 2 * d)
                for m in range(2):
                    for s in range(SEQS):
                        tok = slice(s * S, (s + 1) * S)
                        ins = product(bank[:, 4 + 2 * m + s, :], bd_hi[:, 2 * d + m, :], bd_lo[:, 2 * d + m, :],
                                      xc_hi[:, tok], xc_lo[ct][:, tok], True, True)
                ins.then_inc(gates_done, 1)

        def transposes(out_bank, pieces, done):
            for i, piece in enumerate(pieces):
                ins = pe.transpose(bank[:, out_bank, i * P:(i + 1) * P], piece, ident[:, :])
            ins.then_inc(done, 1)

        def project_out(b, k):
            tok = slice(b * P, (b + 1) * P)
            if b == 0:
                pe.wait_ge(wo_lo_done, 2 * (k + 1))
                if k < ATTN_W // P:
                    pe.wait_ge(mixA_lo_done, k + 1)
                else:
                    pe.wait_ge(mixL_lo_done, 2 * (k - ATTN_W // P + 1))
            hi, lo, i = (mixA_hi, mixA_lo, k) if k < ATTN_W // P else (mixL_hi, mixL_lo, k - ATTN_W // P)
            for h in range(2):
                cols = slice(h * 512, (h + 1) * 512)
                ins = product(bank[:, 2 * (b % 2) + h, :], hi[:, i, tok], lo[:, i, tok], wo_hi[k][:, cols], wo_lo[k][:, cols],
                              k == 0, k == KC - 1)
            return ins

        for kind, n in attn:
            if kind == "transpose":
                b, i = divmod(n, USES)
                pe.wait_ge(qk_lo_done, 2 * (b + 1))
                if prep_free(n) > 0:
                    pe.wait_ge(qkT_out, prep_free(n))
                if i < 2:
                    pieces = [q_pair[pair_set(b)][:, 4 * i + h, :, :].rearrange("p a d -> p (a d)") for h in range(4)]
                else:
                    pieces = [k_pair[pair_set(b)][:, g, v, :, :].rearrange("p a d -> p (a d)") for g in range(KVH) for v in range(2)]
                transposes(prep_bank(n), pieces, qkT_done)
            elif kind == "project_out":
                pe.wait_ge(exp_done, UNITS)
                project_out(0, n)
            elif kind == "slot":
                u, t, v = n, n - T_LAG, n - V_LAG
                if u < UNITS:
                    head, qb = divmod(u, BPS)
                    s, h = divmod(head, HQ)
                    kv = h // (HQ // KVH)
                    pe.wait_ge(qkT_out, USES * BPS * (s + 1))
                    if u >= 2:
                        pe.wait_ge(exp_done, u - 1)
                    q = qT[:, s, h, qb * P:(qb + 1) * P]
                    pe.matmul(bank[:, u % 2, :], q, kT[:, s, kv, 0, :], start=True, stop=False)
                    pe.matmul(bank[:, u % 2, :], q, kT[:, s, kv, 1, :], start=False, stop=True).then_inc(scores_done, 1)
                if 0 <= t < UNITS:
                    head, kc = divmod(t, BPS)
                    pe.wait_ge(prob_done, BPS * (head + 1))
                    if t >= BPS:
                        pe.wait_ge(probT_lo_done, t - BPS + 1)
                    transposes(2 + kc, [prob[:, (BPS * head + qb) % PROB_SLOTS, kc * P:(kc + 1) * P] for qb in range(BPS)], probT_done)
                if 0 <= v < UNITS:
                    head, kc = divmod(v, BPS)
                    pair, s = head // 2, head // HQ
                    if kc == 0 and head % 2 == 0 and pair:
                        pe.wait_ge(mixA_lo_done, pair if pair < PAIRS_ONE_BANK else pair - 1)
                    pe.wait_ge(v_lo_done, 1)
                    pe.wait_ge(v_zeroed, 2)
                    pe.wait_ge(probT_lo_done, v + 1)
                    blk, cols = BPS * s + kc, pair_cols(head)
                    product(bank[:, out_bank(pair), :], v_hi[:, blk, cols], v_lo[:, blk, cols], probT_hi[:, kc, :], probT_lo[:, kc, :],
                            head % 2 == 0 and kc == 0, head % 2 == 1 and kc == BPS - 1).then_inc(pv_done, 1)

        for b in range(NB + 2):
            if b < NB:
                if b >= 2:
                    pe.wait_ge(x2_done, b - 1)
                if b == 1:
                    pe.wait_ge(probT_lo_done, UNITS)
                    pe.wait_ge(mixA_lo_done, HEADS // 2)
                for k in range(0 if b else WO_EARLY, KC):
                    ins = project_out(b, k)
                ins.then_inc(outproj_done, 1)
            c = b - 2
            if 0 <= c < NB:
                pe.wait_ge(h2T_out, 2 * (c + 1))
                if c == 0:
                    pe.wait_ge(consts3_loaded, 2 * 16)
                for k in range(KC):
                    ins = pe.matmul(bank[:, 7, c * E:(c + 1) * E], h2T[:, c % 2, k, :], router[:, k, :], start=(k == 0), stop=(k == KC - 1))
                ins.then_inc(logits_done, 1)
            c = b - 1
            if 0 <= c < NB:
                pe.wait_ge(h2_done, c + 1)
                for h in range(2):
                    if c:
                        pe.wait_ge(h2T_out, 2 * (c - 1) + h + 1)
                    transposes(4 + h, [h2[:, c % 2, (4 * h + i) * P:(4 * h + i + 1) * P] for i in range(4)], h2T_done)
        pe.wait_ge(aff_done, 1)
        for b in range(BPS):
            ins = pe.transpose(bank[0:48, 6, b * P:(b + 1) * P], aff_pad[:, b, :], ident[:, :])
        ins.then_inc(affT_done, 1)
        pe.wait_ge(stacked_done, 1)
        for i in range(2):
            ins = pe.transpose(bank[:, 5, i * E:(i + 1) * E], stacked[:, i, :], ident[0:E, 0:E])
        ins.then_inc(stackedT_done, 1)

        def rows(first, m, first_bank, l_hi, l_lo, between, inc_last=1):
            for j in range(8):
                if j in between:
                    between[j]()
                pe.wait_ge(row_lo, first + (8 * m + j + 1))
                slot = (8 * m + j) % SPLIT
                for h in range(2):
                    cols = slice(h * 512, (h + 1) * 512)
                    ins = product(bank[:, first_bank + h, :], l_hi[:, j, :], l_lo[:, j, :], e_hi[:, slot, cols], e_lo[:, slot, cols],
                                  j == 0, j == 7)
                ins.then_inc(row_used, inc_last if j == 7 else 1)

        def turn_tokens(loaded, parity):
            pe.wait_ge(xs_loaded[parity], loaded)
            for h in range(2):
                transposes(6 + h, [xs[:, parity, (4 * h + i) * P:(4 * h + i + 1) * P] for i in range(4)], xsT_done)

        def turn_hidden(e):
            pe.wait_ge(hid_done, e + 1)
            for h in range(2):
                transposes(6 + h, [hid[:, (4 * h + i) * P:(4 * h + i + 1) * P] for i in range(4)], hidT_done)

        pe.wait_ge(routed, 2)
        turn_tokens(16, 0)
        pe.wait_ge(xsT_lo_done, 2)
        def tokens_1():
            turn_tokens(16, 1)
        rows(0, 0, 0, xsT_hi[:, 0, :, :], xsT_lo[:, 0, :, :], {6: tokens_1}, 9)
        rows(0, 2, 2, xsT_hi[:, 0, :, :], xsT_lo[:, 0, :, :], {})

        def step_pe(e, parity, more):
            n = (e + 1) * 24
            other = 1 - parity
            def hidden():
                pe.wait_ge(xsT_lo_done, e * 2 + 4)
                turn_hidden(e)
            def tokens():
                turn_tokens(tokens_at(e, parity), parity)
            pe.wait_ge(xsT_lo_done, e * 2 + 4)
            pe.wait_ge(silu_done, e + 1)
            rows(n, 0, 0, xsT_hi[:, other, :, :], xsT_lo[:, other, :, :], {6: hidden})
            pe.wait_ge(hidT_lo_done, e * 2 + 2)
            pe.wait_ge(ys_done, e + 1)
            rows(n, 1, 4, hidT_hi, hidT_lo, {4: tokens} if more else {})
            rows(n, 2, 2, xsT_hi[:, other, :, :], xsT_lo[:, other, :, :], {})

        def tokens_at(e, parity):
            return (e - parity) * 8 + 32

        with pe.Fori(0, (E - 2) // 2) as pair:
            e = pair * 2
            step_pe(e, 0, True)
            step_pe(e + 1, 1, True)
        step_pe(E - 2, 0, False)
        turn_hidden(E - 1)
        pe.wait_ge(hidT_lo_done, 2 * E)
        pe.wait_ge(ys_done, E)
        rows(24 * E, 0, 4, hidT_hi, hidT_lo, {})

    @block.vector
    def _(dve):
        own = [0]

        def link(ins):
            own[0] += 1
            ins.then_inc(dve_step, 1)
            dve.wait_ge(dve_step, own[0])

        def newton(rstd, mean_sq, tmp):
            link(dve.tensor_tensor(tmp, rstd, rstd, ALU.mult))
            link(dve.tensor_tensor(tmp, tmp, mean_sq, ALU.mult))
            link(dve.tensor_scalar(tmp, tmp, -0.5, 1.5, ALU.mult, ALU.add))
            return dve.tensor_tensor(rstd, rstd, tmp, ALU.mult)

        def prepare(kind, n=0):
            quarter = HD // 4
            if kind == "sum":
                dve.wait_ge(qk_sq_done, n + 1)
                dve.tensor_reduce(qk_stat[:, 0, n * NH:(n + 1) * NH], qk_sq[:, n % 2, :].rearrange("p (h d) -> p h d", h=NH),
                                  AX_X, ALU.add).then_inc(qk_sum_done, 1)
            elif kind == "rstd":
                dve.wait_ge(qk_sum_done, NB)
                dve.tensor_scalar(qk_stat[:, 1, :], qk_stat[:, 0, :], 1.0 / HD, EPS, ALU.mult, ALU.add)
                dve.wait_ge(qk_root_done, 1)
                link(dve.reciprocal(qk_stat[:, 3, :], qk_stat[:, 2, :]))
                newton(qk_stat[:, 3, :], qk_stat[:, 1, :], qk_stat[:, 2, :]).then_inc(qk_rstd_done, 1)
            elif kind == "turn":
                b = n
                if b == 0:
                    dve.wait_ge(tabs_done, 13)
                    dve.wait_ge(gates_done, 2 * CT)
                for i, (c0, h) in enumerate(((0, HQ), (ATTN_W, KVH))):
                    for a in range(2):
                        src = qkv[:, b, c0:c0 + h * HD].rearrange("p (h a o d) -> p h a o d", h=h, a=2, o=2)[:, :, a, ::-1, :]
                        out = swapped[b % 2][:, c0:c0 + h * HD].rearrange("p (h a o d) -> p h a o d", h=h, a=2, o=2)[:, :, a, :, :]
                        sin = tab[:, 2 * i + 1, b % BPS:b % BPS + 1, a * 2 * quarter:(a + 1) * 2 * quarter].rearrange(
                            "p b (o d) -> p b o d", o=2).to_broadcast([P, h, 2, quarter])
                        ins = dve.tensor_tensor(out, src, sin, ALU.mult)
                ins.then_inc(swapped_done, 1)
            elif kind == "norm":
                b = n
                dve.wait_ge(turned_done, 2 * (b + 1))
                dve.wait_ge(swapped_done, b + 1)
                link(dve.tensor_tensor(turned[b % 2][:, :], turned[b % 2][:, :], swapped[b % 2][:, :], ALU.add))
                dve.wait_ge(qk_rstd_done, 1)
                dve.tensor_tensor(qkv[:, b, 0:QK].rearrange("p (h d) -> p h d", h=NH), turned[b % 2][:, :].rearrange("p (h d) -> p h d", h=NH),
                                  qk_stat[:, 3, b * NH:(b + 1) * NH].unsqueeze(2).to_broadcast([P, NH, HD]),
                                  ALU.mult).then_inc(qk_norm_done, 1)
            elif kind == "lo":
                b, i = n, pair_set(n)
                qn = qkv[:, b, 0:QK].rearrange("p (h d) -> p h d", h=NH)
                dve.wait_ge(qk_norm_done, b + 1)
                dve.wait_ge(qk_hi_done, b + 1)
                dve.tensor_tensor(q_pair[i][:, :, 1, :].bitcast(F32R), qn[:, 0:HQ, :], q_pair[i][:, :, 0, :], ALU.subtract).then_inc(qk_lo_done, 1)
                for copy in range(2):
                    ins = dve.tensor_tensor(k_pair[i][:, :, 1, copy, :].bitcast(F32R), qn[:, HQ:NH, :], k_pair[i][:, :, 0, 0, :], ALU.subtract)
                ins.then_inc(qk_lo_done, 1)

        dve.wait_ge(g1_loaded, 16)
        for step in steps:
            kind, arg = step[0], step[1:]
            if kind == "normalise":
                b, = arg

                def empty_turned(b):
                    for h in range(2):
                        dve.wait_ge(ht_hi_done, 2 * b + h + 1)
                        out = hT_lo[:, 4 * h:4 * h + 4, b * P:(b + 1) * P]
                        dve.tensor_tensor(out, bank[:, 4 + 2 * (b % 2) + h, :].rearrange("p (k t) -> p k t", k=4),
                                          hT_hi[:, 4 * h:4 * h + 4, b * P:(b + 1) * P].bitcast(F32),
                                          ALU.subtract).then_inc(ht_lo_done, 1)

                if b == BPS:
                    empty_turned(b - 1)
                if b < NB:
                    dve.wait_ge(root_ready, b + 1)
                    dve.reciprocal(rstd1[:, b:b + 1], root1[:, b:b + 1]).then_inc(rstd_ready, 1)
                    dve.wait_ge(rstd_ready, b + 1)
                    if b >= 2:
                        dve.wait_ge(xt_done, 2 * (b - 1))
                    dve.scalar_tensor_tensor(out=x_norm[:, b % 2, :], in0=x_nat[:, b, :], scalar=rstd1[:, b:b + 1],
                                             in1=g1b[:, :], op0=ALU.mult, op1=ALU.mult).then_inc(xn_ready, 1)
                if b and b != BPS:
                    empty_turned(b - 1)
            elif kind == "w_lo":
                g, = arg
                dve.wait_ge(whi_done, g + 1)
                dve.tensor_tensor(w_lo[:, g % 2, :, :], w_raw[:, :, :], w_hi[:, g % 2, :, :].bitcast(F32),
                                  ALU.subtract).then_inc(wlo_done, 1)
            elif kind == "vectors":
                dve.wait_ge(vec_t, 1)
                dve.tensor_copy(vecs[:, :], bank[:, 0, 0:44]).then_inc(vec_copied, 1)
                dve.wait_ge(vec_copied, 1)
            elif kind == "softplus":
                lam = vecs[:, V_LAM:V_LAM + 2 * CT]
                link(dve.tensor_scalar(sp_neg, lam, -1.0, None, ALU.mult))
                dve.tensor_tensor(sp_abs, lam, sp_neg, ALU.max).then_inc(sp_abs_done, 1)
                dve.tensor_scalar(sp_pos, sp_neg, 0.0, None, ALU.max)
                dve.wait_ge(sp_exp_done, 1)
                link(dve.tensor_scalar(sp_den, sp_exp, 2.0, None, ALU.add))
                link(dve.reciprocal(sp_z, sp_den))
                link(dve.tensor_tensor(sp_z, sp_z, sp_exp, ALU.mult))
                link(dve.tensor_tensor(sp_z2, sp_z, sp_z, ALU.mult))
                link(dve.tensor_scalar(sp_p, sp_z2, 1.0 / 17, None, ALU.mult))
                for n in range(15, 1, -2):
                    link(dve.scalar_tensor_tensor(out=sp_p, in0=sp_p, scalar=1.0 / n, in1=sp_z2, op0=ALU.add, op1=ALU.mult))
                link(dve.scalar_tensor_tensor(out=sp_p, in0=sp_p, scalar=1.0, in1=sp_z, op0=ALU.add, op1=ALU.mult))
                link(dve.scalar_tensor_tensor(out=sp_p, in0=sp_p, scalar=2.0, in1=sp_pos, op0=ALU.mult, op1=ALU.add))
                dve.tensor_scalar(lru_c, sp_p, LRU_C, None, ALU.mult)
                dve.tensor_scalar(neg_c, sp_p, -LRU_C, None, ALU.mult)
                dve.tensor_scalar(neg_2c, sp_p, -2 * LRU_C, None, ALU.mult).then_inc(lru_c_done, 1)
            elif kind == "empty":
                g, j = arg
                what, c0, _ = GROUPS[g]
                if what == "xr":
                    dve.wait_ge(proj_done, JOBS * g + j + 1)
                    dve.tensor_copy(xr_pad[:, c0 + j % 2, j // 2, CONV_LEFT:CONV_LEFT + S], bank[:, j, :]).then_inc(xr_out, 1)
            elif kind == "conv":
                ct, = arg
                xcs = xc[:, :].rearrange("p (s t) -> p s t", s=SEQS)
                taps = [xr_pad[:, ct, :, i:i + S] for i in range(TAPS)]
                w = [vecs[:, V_CONVW + CT * i + ct:V_CONVW + CT * i + ct + 1] for i in range(TAPS)]
                dve.wait_ge(xr_out, JOBS * (ct // 2) + 3 + ct % 2)
                link(dve.tensor_scalar(xcs, taps[0], w[0], vecs[:, V_CONVB + ct:V_CONVB + ct + 1], ALU.mult, ALU.add))
                for i in range(1, TAPS):
                    ins = dve.scalar_tensor_tensor(out=xcs, in0=taps[i], scalar=w[i], in1=xcs, op0=ALU.mult, op1=ALU.add)
                    if i < TAPS - 1:
                        link(ins)
                ins.then_inc(xc_done, 1)
                dve.wait_ge(bd_hi_done, ct + 1)
                dve.tensor_tensor(bd_lo[:, :, :], bd_raw[:, :, :], bd_hi[:, :, :].bitcast(F32), ALU.subtract).then_inc(bd_lo_done, 1)
                dve.wait_ge(xc_hi_done, ct + 1)
                dve.tensor_tensor(xc_lo[ct][:, :], xc[:, :], xc_hi[:, :].bitcast(F32), ALU.subtract).then_inc(xc_lo_done, 1)
            elif kind == "decay":
                ct, = arg
                for d in range(2):
                    dve.wait_ge(sigm_done, 4 * ct + 2 * d + 2)
                    link(dve.tensor_tensor(ib[d][:, :], ib[d][:, :], xc[:, :], ALU.mult))
            elif kind == "scan":
                ct, = arg
                for d in range(2):
                    dve.wait_ge(tanh_done, 2 * ct + d + 1)
                    dve.scalar_tensor_tensor(out=mult[d][:, :], in0=mult[d][:, :], scalar=1.0, in1=rt[d][:, :],
                                             op0=ALU.add, op1=ALU.mult).then_inc(mult2_done, 1)
                for d in range(2):
                    dve.wait_ge(root_done, 2 * ct + d + 1)
                    link(dve.tensor_tensor(ib[d][:, :], ib[d][:, :], mult[d][:, :], ALU.mult))
                    for s in range(SEQS):
                        a, b = (v[:, s * S:(s + 1) * S] for v in (decay[d], ib[d]))
                        if d:
                            a, b = (v[d][:, (s + 1) * S - 1:s * S - 1 if s else None:-1] for v in (decay, ib))
                        ins = dve.tensor_tensor_scan(b, a, b, 0.0, ALU.mult, ALU.add)
                link(ins)
                dve.tensor_tensor(lru_out[:, ct, :], ib[0][:, :], ib[1][:, :], ALU.add).then_inc(scan_done, 1)
            elif kind in PREPARE:
                prepare(kind, *arg)

        dve.wait_ge(proj_done, NG * JOBS)
        def split_wo_lo(k, half):
            cols = slice(half * D // 2, (half + 1) * D // 2)
            dve.wait_ge(wo_hi_done, 2 * k + half + 1)
            dve.tensor_tensor(wo_lo[k][:, cols], wo_raw[k][:, cols], wo_hi[k][:, cols].bitcast(F32), ALU.subtract).then_inc(wo_lo_done, 1)

        for kind, n in attn:
            if kind == "lo":
                prepare(kind, n)
            elif kind == "v":
                dve.wait_ge(v_hi_done, 1)
                dve.tensor_tensor(v_of(v_lo), v_in(qkv), v_of(v_hi).bitcast(F32), ALU.subtract).then_inc(v_lo_done, 1)
            elif kind == "split_lo":
                if n < 2 * WO_EARLY:
                    split_wo_lo(n // 2, n % 2)
            elif kind == "slot":
                u, t, v = n, n - T_LAG, n - V_LAG - 1
                if u < UNITS:
                    dve.wait_ge(scores_done, u + 1)
                    dve.tensor_reduce(row_stat[:, 0, u:u + 1], bank[:, u % 2, :], AX_X, ALU.max, negate=True).then_inc(max_done, 1)
                if v >= 0 and v % (2 * BPS) == 2 * BPS - 1:
                    pair = v // (2 * BPS)
                    head = 2 * pair
                    dve.wait_ge(mixA_hi_done, pair + 1)
                    where = (slice(None), head % HQ // 2, slice(head // HQ * S, (head // HQ + 1) * S))
                    dve.tensor_tensor(mixA_lo[where], bank[:, out_bank(pair), :], mixA_hi[where].bitcast(F32), ALU.subtract).then_inc(mixA_lo_done, 1)
                if 0 <= u - 1 < UNITS:
                    dve.wait_ge(exp_done, u)
                    dve.reciprocal(row_stat[:, 2, u - 1:u], row_stat[:, 1, u - 1:u]).then_inc(recip_done, 1)
                if 0 <= t < UNITS:
                    dve.wait_ge(probT_hi_done, t + 1)
                    dve.tensor_tensor(probT_lo[:, t % BPS, :], bank[:, 2 + t % BPS, :], probT_hi[:, t % BPS, :].bitcast(F32),
                                      ALU.subtract).then_inc(probT_lo_done, 1)

        for k in range(WO_EARLY, KC):
            for half in range(2):
                split_wo_lo(k, half)
        for b in range(NB):
            dve.wait_ge(outproj_done, b + 1)
            dve.wait_ge(xa_loaded, 16 * (b + 1))
            if b >= 2:
                dve.wait_ge(x2_stored[b % 2], 16 * (b // 2))
            dve.tensor_tensor(x2[:, b % 2, :], bank[:, 2 * (b % 2):2 * (b % 2) + 2, :].rearrange("p a b -> p (a b)"),
                              x_again[:, :], ALU.add).then_inc(x2_done, 1)
            dve.wait_ge(sumsq2_done, b + 1)
            r, v, t = rstd1[:, b:b + 1], small[:, 120:121], small[:, 121:122]
            link(dve.tensor_scalar(v, sumsq1[:, b:b + 1], 1.0 / D, EPS, ALU.mult, ALU.add))
            dve.wait_ge(root2_done, b + 1)
            link(dve.reciprocal(r, root1[:, b:b + 1]))
            link(newton(r, v, t))
            if b == 0:
                dve.wait_ge(consts3_loaded, 2 * 16)
            dve.scalar_tensor_tensor(out=h2[:, b % 2, :], in0=x2[:, b % 2, :], scalar=r, in1=g2b[:, :],
                                     op0=ALU.mult, op1=ALU.mult).then_inc(h2_done, 1)
        logits = bank[:, 7, 0:NB * E].rearrange("p (b e) -> p b e", b=NB)
        spread = lambda v: v.unsqueeze(2).to_broadcast([P, NB, E])
        dve.wait_ge(logits_done, NB)
        link(dve.tensor_reduce(aff_stat[:, 0, :], logits, AX_X, ALU.max))
        dve.tensor_tensor(aff_e[:, :, :], logits, spread(aff_stat[:, 0, :]), ALU.subtract).then_inc(aff_shifted, 1)
        dve.wait_ge(aff_exp_done, 1)
        link(dve.tensor_reduce(aff_stat[:, 1, :], aff_e[:, :, :], AX_X, ALU.add))
        link(dve.reciprocal(aff_stat[:, 2, :], aff_stat[:, 1, :]))
        dve.wait_ge(pad_zeroed, 1)
        for s in range(SEQS):
            blocks = slice(s * BPS, (s + 1) * BPS)
            ins = dve.tensor_tensor(aff_pad[:, :, 32 * s:32 * s + E], aff_e[:, blocks, :],
                                    spread(aff_stat[:, 2, :])[:, blocks, :], ALU.mult)
        ins.then_inc(aff_done, 1)
        dve.wait_ge(affT_done, 1)
        dve.wait_ge(outproj_done, NB)
        link(dve.tensor_copy(aff_work[:, 0, :], bank[0:48, 6, :]))
        for r in range(CAP // 8):
            now, then = aff_work[:, r % 2, :], aff_work[:, (r + 1) % 2, :]
            eight = slice(8 * r, 8 * r + 8)
            link(dve.max(top_val[:, eight], now))
            link(dve.max_index(top_idx[:, eight], top_val[:, eight], now))
            if r < CAP // 8 - 1:
                link(dve.match_replace(then, top_val[:, eight], now, -1.0))
        link(dve.tensor_copy(stacked[:, 0, 0:CAP], top_idx[0:E, :]))
        dve.tensor_scalar(stacked[:, 0, CAP:P], top_idx[32:32 + E, :], float(S), None, ALU.add)
        dve.tensor_copy(stacked[:, 1, 0:CAP], top_val[0:E, :])
        dve.tensor_copy(stacked[:, 1, CAP:P], top_val[32:32 + E, :]).then_inc(stacked_done, 1)
        dve.wait_ge(stackedT_done, 1)
        dve.tensor_copy(idx_all[:, :], bank[:, 5, 0:E]).then_inc(routed, 1)
        dve.tensor_copy(gate_all[:, :], bank[:, 5, E:2 * E]).then_inc(routed, 1)

        def lo_row(first, m, raw, j, inc=1):
            slot = (8 * m + j) % SPLIT
            dve.wait_ge(row_hi, first + (8 * m + j + 1))
            dve.tensor_tensor(e_lo[:, slot, :], raw[:, j // 2, j % 2, :], e_hi[:, slot, :].bitcast(F32), ALU.subtract).then_inc(row_lo, inc)

        def turn_lo(out, hi, hi_done, count, done):
            for h in range(2):
                dve.wait_ge(hi_done, count + (h + 1))
                dve.tensor_tensor(out[:, 4 * h:4 * h + 4, :], bank[:, 6 + h, :].rearrange("p (k t) -> p k t", k=4),
                                  hi[:, 4 * h:4 * h + 4, :].bitcast(F32), ALU.subtract).then_inc(done, 1)

        def hidden(e):
            dve.wait_ge(row_used, e * 24 + 24)
            dve.wait_ge(silu_done, e + 1)
            dve.tensor_tensor(hid[:, :], bank[:, 2:4, :].rearrange("p a b -> p (a b)"), silu[:, :], ALU.mult).then_inc(hid_done, 1)

        turn_lo(xsT_lo[:, 0, :, :], xsT_hi[:, 0, :, :], xsT_hi_done, 0, xsT_lo_done)
        dve.wait_ge(row_lo, SPLIT)
        for j in range(SPLIT, 8):
            lo_row(0, 0, raw_gate, j, 9 if j == 7 else 1)
        turn_lo(xsT_lo[:, 1, :, :], xsT_hi[:, 1, :, :], xsT_hi_done, 2, xsT_lo_done)
        for j in range(8):
            lo_row(0, 2, raw_up, j)

        def step_dve(e, parity, more):
            n = (e + 1) * 24
            for j in range(8):
                lo_row(n, 0, raw_gate, j)
                if j == 3:
                    hidden(e)
            turn_lo(hidT_lo, hidT_hi, hidT_hi_done, e * 2, hidT_lo_done)
            for j in range(8):
                lo_row(n, 1, raw_down, j)
            if more:
                turn_lo(xsT_lo[:, parity, :, :], xsT_hi[:, parity, :, :], xsT_hi_done, (e + 2) * 2, xsT_lo_done)
            for j in range(8):
                lo_row(n, 2, raw_up, j)
        with dve.Fori(0, (E - 2) // 2) as pair:
            e = pair * 2
            step_dve(e, 0, True)
            step_dve(e + 1, 1, True)
        step_dve(E - 2, 0, False)
        for j in range(2):
            lo_row(24 * E, 0, raw_down, j)
        hidden(E - 1)
        turn_lo(hidT_lo, hidT_hi, hidT_hi_done, 2 * (E - 1), hidT_lo_done)
        for j in range(2, 8):
            lo_row(24 * E, 0, raw_down, j)

    ctx.close()


_INS = ["x_prompt", "x_sample", "norm1_g", "w_in", "q_norm_g", "k_norm_g", "conv_w", "conv_b", "lru_w_r", "lru_b_r",
        "lru_w_i", "lru_b_i", "lru_lambda", "w_out", "norm2_g", "router_w", "exp_w_gate", "exp_w_up", "exp_w_down"]


def rope_tables(S, head_dim):
    import numpy as np
    pos = np.arange(S)
    axis_dim = head_dim // 2
    inv_freq = (np.float32(ROPE_THETA) ** (-np.arange(0, axis_dim, 2, dtype=np.float32) / np.float32(axis_dim))).astype(np.float32)
    row = (pos // GRID_W).astype(np.float32)[:, None] * inv_freq
    col = (pos % GRID_W).astype(np.float32)[:, None] * inv_freq
    cos = np.concatenate([np.cos(row), np.cos(row), np.cos(col), np.cos(col)], axis=1).astype(np.float32)
    sin = np.concatenate([-np.sin(row), np.sin(row), -np.sin(col), np.sin(col)], axis=1).astype(np.float32)
    return cos, sin


def kernel(**inputs):
    import numpy as np
    import concourse.bacc as bacc
    from concourse.bass_utils import run_bass_kernel_spmd

    nc = bacc.Bacc("TRN2", target_bir_lowering=False, num_devices=1)
    arrays, args = {}, []
    S, D = inputs["x_prompt"].shape[1:]
    cos, sin = rope_tables(S, inputs["q_norm_g"].shape[1])
    given = {name: np.ascontiguousarray(inputs[name]) for name in _INS} | {"rope_cos": cos, "rope_sin": sin}
    for name, a in given.items():
        arrays[f"in_{name}_dram"] = a
        args.append(nc.dram_tensor(f"in_{name}_dram", a.shape, mybir.dt.from_np(a.dtype), kind="ExternalInput").ap())
    args.append(nc.dram_tensor("y_dram", (SEQS * S, D), F32, kind="ExternalOutput").ap())
    layer_program(nc, *args)
    y = run_bass_kernel_spmd(nc, [arrays], core_ids=[0]).results[0]["y_dram"].reshape(SEQS, 1, S, D)
    return y[0], y[1]
```
